# Optimizing a Trainium2 kernel written in Bass

```python
import math, functools
import jax, jax.numpy as jnp
from jax import lax
import numpy as np

D_MODEL = 1024
BATCH = 1
SEQ = 1024
DEPTH = 1
DEC_BATCH = 8
DEC_SEQ = 1
PAST_LEN = 2048
PAGE_SIZE = 128

HEAD_DIM = 64
N_HEADS = D_MODEL // HEAD_DIM
N_KV_HEADS = 4
GROUP = N_HEADS // N_KV_HEADS
D_ATTN = N_HEADS * HEAD_DIM
D_KV = N_KV_HEADS * HEAD_DIM
D_RNN = D_MODEL
RNN_BLOCKS = 16
RNN_BLOCK = D_RNN // RNN_BLOCKS
RNN_CONV = 4
RG_C = 8.0
D_FF = ((8 * D_MODEL // 3 + 127) // 128) * 128
FFN_CONV = 3
META_TOKENS = 16
BLOCK = 128
EPS = 1e-6
SB_SCALE = 1.0 / math.sqrt(HEAD_DIM)
SB_BIAS_INIT = -8.0
D_IN = D_ATTN + 2 * D_KV + 2 * D_RNN + 2 * D_MODEL
SPLITS = (D_ATTN, D_ATTN + D_KV, D_ATTN + 2 * D_KV, D_ATTN + 2 * D_KV + D_RNN,
          D_ATTN + 2 * D_KV + 2 * D_RNN)

kernel_name = 'hybrid_stickbreak_rglru_convffn_step'

def rms_norm(x, g):
    xf = x.astype(jnp.float32)
    y = xf * lax.rsqrt(jnp.mean(xf * xf, axis=-1, keepdims=True) + EPS)
    return (y * g.astype(jnp.float32)).astype(x.dtype)

def causal_dwconv(u, buf, w, b):
    t = u.shape[1]
    ucat = jnp.concatenate([buf.astype(u.dtype), u], axis=1)
    out = b + sum(ucat[:, j:j + t] * w[j] for j in range(w.shape[0]))
    return out, ucat[:, t:]

def stick_breaking_weights(z, mask):
    log_keep = jnp.where(mask, jax.nn.log_sigmoid(-z), 0.0)
    later = jnp.concatenate([log_keep[..., 1:], jnp.zeros_like(log_keep[..., :1])], axis=-1)
    tail = lax.cumsum(later, axis=z.ndim - 1, reverse=True)
    return jnp.where(mask, jnp.exp(jax.nn.log_sigmoid(z) + tail), 0.0)

def attend_prompt(q, k, v, bias):
    b, t = q.shape[:2]
    pad = (-META_TOKENS) % BLOCK
    qp = jnp.pad(q, ((0, 0), (pad, 0), (0, 0), (0, 0), (0, 0)))
    kp = jnp.pad(k, ((0, 0), (pad, 0), (0, 0), (0, 0))).astype(jnp.float32)
    vp = jnp.pad(v, ((0, 0), (pad, 0), (0, 0), (0, 0))).astype(jnp.float32)
    tp = t + pad
    k_pos = jnp.arange(tp)
    k_valid = k_pos >= pad
    bias_f = bias.astype(jnp.float32)[None, :, :, None, None]

    def one_block(start):
        qb = lax.dynamic_slice_in_dim(qp, start, BLOCK, axis=1).astype(jnp.float32)
        q_pos = start + jnp.arange(BLOCK)
        mask = (k_pos[None, :] < q_pos[:, None]) & k_valid[None, :]
        z = jnp.einsum('bqhgd,bshd->bhgqs', qb, kp) * SB_SCALE + bias_f
        w = stick_breaking_weights(z, mask)
        return jnp.einsum('bhgqs,bshd->bqhgd', w, vp)

    out = lax.map(one_block, jnp.arange(tp // BLOCK) * BLOCK)
    out = jnp.moveaxis(out, 0, 1).reshape(b, tp, D_ATTN)
    return out[:, pad:].astype(q.dtype)

def attend_sample(q, k, v, bias, past_k, past_v):
    b, s = q.shape[:2]
    p = past_k.shape[1]
    qf = q.astype(jnp.float32) * SB_SCALE
    z = jnp.concatenate([
        jnp.einsum('bqhgd,bshd->bhgqs', qf, past_k.astype(jnp.float32)),
        jnp.einsum('bqhgd,bshd->bhgqs', qf, k.astype(jnp.float32))], axis=-1)
    z = z + bias.astype(jnp.float32)[None, :, :, None, None]
    q_pos = p + jnp.arange(s)
    k_pos = jnp.arange(p + s)
    mask = k_pos[None, :] < q_pos[:, None]
    w = stick_breaking_weights(z, mask)
    out = (jnp.einsum('bhgqs,bshd->bqhgd', w[..., :p], past_v.astype(jnp.float32))
           + jnp.einsum('bhgqs,bshd->bqhgd', w[..., p:], v.astype(jnp.float32)))
    return out.reshape(b, s, D_ATTN).astype(q.dtype)

def rg_lru(xc, h0, w_rgate, b_rgate, w_igate, b_igate, lam):
    b, t, _ = xc.shape
    xb = xc.reshape(b, t, RNN_BLOCKS, RNN_BLOCK)
    r = jax.nn.sigmoid(jnp.einsum('btnc,ncd->btnd', xb, w_rgate).reshape(b, t, D_RNN) + b_rgate).astype(jnp.float32)
    i = jax.nn.sigmoid(jnp.einsum('btnc,ncd->btnd', xb, w_igate).reshape(b, t, D_RNN) + b_igate).astype(jnp.float32)
    log_a = -RG_C * r * jax.nn.softplus(-lam.astype(jnp.float32))
    a = jnp.exp(log_a)
    u = jnp.sqrt(-jnp.expm1(2.0 * log_a)) * i * xc.astype(jnp.float32)

    def combine(lhs, rhs):
        al, bl = lhs
        ar, br = rhs
        return al * ar, ar * bl + br

    a_cum, b_cum = lax.associative_scan(combine, (a, u), axis=1)
    h = a_cum * h0.astype(jnp.float32)[:, None] + b_cum
    return h.astype(xc.dtype), h[:, -1].astype(xc.dtype)

def hybrid_layer(x, attend, rnn_h0, rnn_buf, ffn_buf, lw):
    (g_mix, w_in, sb_bias, w_rnn_conv, b_rnn_conv, w_rgate, b_rgate, w_igate, b_igate,
     rglru_lambda, w_out, g_ffn, w_up, w_ffn_conv, b_ffn_conv, w_down) = lw
    b, t, _ = x.shape
    n = rms_norm(x, g_mix)
    q, k, v, xr, gr, gates = jnp.split(n @ w_in, SPLITS, axis=-1)
    q = q.reshape(b, t, N_KV_HEADS, GROUP, HEAD_DIM)
    k = k.reshape(b, t, N_KV_HEADS, HEAD_DIM)
    v = v.reshape(b, t, N_KV_HEADS, HEAD_DIM)
    attn = attend(q, k, v, sb_bias.reshape(N_KV_HEADS, GROUP))
    xc, rnn_buf_new = causal_dwconv(xr, rnn_buf, w_rnn_conv, b_rnn_conv)
    hseq, h_last = rg_lru(xc, rnn_h0, w_rgate, b_rgate, w_igate, b_igate, rglru_lambda)
    rnn = hseq * jax.nn.gelu(gr)
    gate_a, gate_b = jnp.split(jax.nn.sigmoid(gates), 2, axis=-1)
    x = x + (gate_a * attn + gate_b * rnn) @ w_out
    up, ffn_buf_new = causal_dwconv(rms_norm(x, g_ffn) @ w_up, ffn_buf, w_ffn_conv, b_ffn_conv)
    ua, ub = jnp.split(up, 2, axis=-1)
    x = x + (jax.nn.gelu(ua) * ub) @ w_down
    return x, k, v, h_last, rnn_buf_new, ffn_buf_new

def setup_inputs(seed: int = 0) -> dict:
    key = jax.random.key(seed)
    ks = jax.random.split(key, 28)

    def nrm(k, shape, scale):
        return jax.random.normal(k, shape, jnp.float32) * scale

    n_pages = PAST_LEN // PAGE_SIZE
    n_phys = (DEC_BATCH * n_pages * 5) // 4
    page_table = jax.random.permutation(ks[4], n_phys)[:DEC_BATCH * n_pages].reshape(DEC_BATCH, n_pages).astype(jnp.int32)
    u = jax.random.uniform(ks[17], (DEPTH, D_RNN), jnp.float32, minval=0.9, maxval=0.999)
    a_base = u ** (1.0 / RG_C)
    lam = jnp.log(a_base) - jnp.log1p(-a_base)
    return {
        'x_prompt': nrm(ks[0], (BATCH, SEQ, D_MODEL), 1.0),
        'x_sample': nrm(ks[1], (DEC_BATCH, DEC_SEQ, D_MODEL), 1.0),
        'cache_k': nrm(ks[2], (DEPTH, n_phys, PAGE_SIZE, N_KV_HEADS, HEAD_DIM), 1.0),
        'cache_v': nrm(ks[3], (DEPTH, n_phys, PAGE_SIZE, N_KV_HEADS, HEAD_DIM), 1.0),
        'page_table': page_table,
        'state_rnn_h': nrm(ks[5], (DEPTH, DEC_BATCH, D_RNN), 0.5),
        'state_rnn_conv': nrm(ks[6], (DEPTH, DEC_BATCH, RNN_CONV - 1, D_RNN), 1.0),
        'state_ffn_conv': nrm(ks[7], (DEPTH, DEC_BATCH, FFN_CONV - 1, 2 * D_FF), 1.0),
        'meta_tokens': nrm(ks[8], (META_TOKENS, D_MODEL), 1.0),
        'g_mix': 1.0 + nrm(ks[9], (DEPTH, D_MODEL), 0.02),
        'w_in': nrm(ks[10], (DEPTH, D_MODEL, D_IN), D_MODEL ** -0.5),
        'sb_bias': SB_BIAS_INIT + nrm(ks[25], (DEPTH, N_HEADS), 0.1),
        'w_rnn_conv': nrm(ks[11], (DEPTH, RNN_CONV, D_RNN), RNN_CONV ** -0.5),
        'b_rnn_conv': nrm(ks[12], (DEPTH, D_RNN), 0.01),
        'w_rgate': nrm(ks[13], (DEPTH, RNN_BLOCKS, RNN_BLOCK, RNN_BLOCK), RNN_BLOCK ** -0.5),
        'b_rgate': nrm(ks[14], (DEPTH, D_RNN), 0.01),
        'w_igate': nrm(ks[15], (DEPTH, RNN_BLOCKS, RNN_BLOCK, RNN_BLOCK), RNN_BLOCK ** -0.5),
        'b_igate': nrm(ks[16], (DEPTH, D_RNN), 0.01),
        'rglru_lambda': lam,
        'w_out': nrm(ks[18], (DEPTH, D_MODEL, D_MODEL), D_MODEL ** -0.5),
        'g_ffn': 1.0 + nrm(ks[19], (DEPTH, D_MODEL), 0.02),
        'w_up': nrm(ks[20], (DEPTH, D_MODEL, 2 * D_FF), D_MODEL ** -0.5),
        'w_ffn_conv': nrm(ks[21], (DEPTH, FFN_CONV, 2 * D_FF), FFN_CONV ** -0.5),
        'b_ffn_conv': nrm(ks[22], (DEPTH, 2 * D_FF), 0.01),
        'w_down': nrm(ks[23], (DEPTH, D_FF, D_MODEL), D_FF ** -0.5),
        'g_final': 1.0 + nrm(ks[24], (D_MODEL,), 0.02),
    }

def reference(x_prompt, x_sample, cache_k, cache_v, page_table, state_rnn_h, state_rnn_conv,
              state_ffn_conv, meta_tokens, g_mix, w_in, sb_bias, w_rnn_conv, b_rnn_conv, w_rgate,
              b_rgate, w_igate, b_igate, rglru_lambda, w_out, g_ffn, w_up, w_ffn_conv, b_ffn_conv,
              w_down, g_final):
    dt = x_prompt.dtype
    b = x_prompt.shape[0]
    db = x_sample.shape[0]
    per_layer = (g_mix, w_in, sb_bias, w_rnn_conv, b_rnn_conv, w_rgate, b_rgate, w_igate, b_igate,
                 rglru_lambda, w_out, g_ffn, w_up, w_ffn_conv, b_ffn_conv, w_down)

    xp = jnp.concatenate([jnp.broadcast_to(meta_tokens[None].astype(dt), (b, META_TOKENS, D_MODEL)), x_prompt], axis=1)
    pk, pv, ph, prc, pfc = [], [], [], [], []
    for layer in range(DEPTH):
        lw = tuple(p[layer] for p in per_layer)
        xp, k, v, h, rb, fb = hybrid_layer(
            xp, attend_prompt, jnp.zeros((b, D_RNN), dt),
            jnp.zeros((b, RNN_CONV - 1, D_RNN), dt), jnp.zeros((b, FFN_CONV - 1, 2 * D_FF), dt), lw)
        pk.append(k); pv.append(v); ph.append(h); prc.append(rb); pfc.append(fb)
    y_prompt = rms_norm(xp, g_final)[:, META_TOKENS:]

    xs = x_sample
    sk, sv, sh, src, sfc = [], [], [], [], []
    for layer in range(DEPTH):
        lw = tuple(p[layer] for p in per_layer)
        past_k = cache_k[layer][page_table].reshape(db, -1, N_KV_HEADS, HEAD_DIM)
        past_v = cache_v[layer][page_table].reshape(db, -1, N_KV_HEADS, HEAD_DIM)
        attend = functools.partial(attend_sample, past_k=past_k, past_v=past_v)
        xs, k, v, h, rb, fb = hybrid_layer(
            xs, attend, state_rnn_h[layer], state_rnn_conv[layer], state_ffn_conv[layer], lw)
        sk.append(k); sv.append(v); sh.append(h); src.append(rb); sfc.append(fb)
    y_sample = rms_norm(xs, g_final)

    return (y_prompt, y_sample,
            jnp.stack(pk), jnp.stack(pv), jnp.stack(ph), jnp.stack(prc), jnp.stack(pfc),
            jnp.stack(sk), jnp.stack(sv), jnp.stack(sh), jnp.stack(src), jnp.stack(sfc))


_drawn_inputs = setup_inputs


def setup_inputs(seed=0):
    import zlib

    import numpy as np

    out = dict(_drawn_inputs(seed))
    spreads = {}
    factors = {'cache_k': 4.882,
     'cache_v': 4.01,
     'g_mix': 2.782,
     'sb_bias': 8.0,
     'b_rgate': 26.51,
     'b_igate': 22.631,
     'g_ffn': 2.855,
     'b_ffn_conv': 7.45,
     'g_final': 8.003}
    for name, (base, spread) in spreads.items():
        noise = np.random.default_rng([zlib.crc32(name.encode()), seed]).standard_normal(out[name].shape)
        drawn = base * np.exp(spread * noise) if base else spread * noise
        out[name] = __import__('jax').numpy.asarray(drawn.astype(out[name].dtype))
    for name, factor in factors.items():
        out[name] = (out[name] * factor).astype(out[name].dtype)
    return out
```

```python
import concourse.bass as bass
from concourse import mybir
from contextlib import ExitStack

F32, F32R, BF16, I32 = mybir.dt.float32, mybir.dt.float32r, mybir.dt.bfloat16, mybir.dt.int32
ALU, ACT = mybir.AluOpType, mybir.ActivationFunctionType

P = 128
D = 1024
KT = D // P
SEQ, META, DEC = 1024, 16, 8
HD, HEADS, KVH = 64, 16, 4
PROMPT = META + SEQ
FIRST = DEC
LAST = DEC + PROMPT
COLS = 1050
CHUNKS = 3
CW = COLS // CHUNKS
TILES = 9
HEAD_ROWS = DEC + META
K_COL, V_COL, XR_COL, GR_COL, GA_COL, GB_COL = 1024, 1280, 1536, 2560, 3584, 4608
DFF = 2816
FT = DFF // P
EPS = 1e-6
PAGES, PAGE, N_PHYS = 16, 128, 160

R_CONVSTATE, R_H0, R_CONVW, R_CONVB, R_BR, R_BI, R_LAM, R_GMIX, R_GFFN, N_ROWS = 0, 24, 32, 36, 37, 38, 39, 40, 41, 42
F_STATE, F_W, F_B, F_ROWS = 0, 16, 19, 20


def token_tile(t):
    return (0, HEAD_ROWS) if t == 0 else (HEAD_ROWS + P * (t - 1), P)


def tiles_for_chunk(c):
    return next(t + 1 for t in range(TILES) if t == TILES - 1 or sum(token_tile(t)) >= CW * (c + 1))


def nth(turn, per_turn, index, credit=0):
    return turn * per_turn + (index + 1 + credit)


class Chain:

    def __init__(self, eng, sem):
        self.eng, self.sem, self.base, self.n = eng, sem, 0, 0

    def turn(self, base, i, per_turn):
        self.base, self.n = base + i * per_turn, 0

    def step(self, ins):
        ins.then_inc(self.sem, 1)
        self.n += 1
        self.eng.wait_ge(self.sem, self.base + self.n)


def project(pe, out, w_hi, w_lo, x_hi, x_lo, col):
    return project_part(pe, out, w_hi, w_lo, x_hi, x_lo, col, 0, KT)


def project_part(pe, out, w_hi, w_lo, x_hi, x_lo, col, k0, k1):
    last = None
    for k in range(k0, k1):
        for w, x in ((w_hi, x_hi), (w_hi, x_lo), (w_lo, x_hi)):
            last = pe.matmul(out, w[:, k, :], x[:, k, col:col + CW],
                             start=(k == 0 and w is w_hi and x is x_hi), stop=(k == KT - 1 and w is w_lo))
    return last


def phase_qkv(nc, g, sem):
    ctx = ExitStack()
    with ctx:
        sb = lambda name, shape, dt=F32: ctx.enter_context(nc.sbuf_tensor(name, shape, dt))
        pb = lambda name, shape: ctx.enter_context(nc.psum_tensor(name, shape, F32))
        w_raw = sb("a_w_raw", [P, 2, KT, P])
        w_hi = sb("a_w_hi", [P, 2, KT, P], F32R)
        w_lo = sb("a_w_lo", [P, 2, KT, P], F32R)
        x_tok = g.mix[:, :, :].rearrange("p a b -> p (a b)")[:, 0:TILES * D].rearrange("p (t d) -> p t d", d=D)
        rows = sb("a_rows", [N_ROWS, D])
        bias_col = sb("a_bias_col", [HEADS, 1])
        bias_rows = sb("a_bias_rows", [HEADS, PROMPT])
        junk = sb("a_junk", [P, 2, D])
        tmp = sb("a_tmp", [P, 2, KT, P])
        stat = sb("a_stat", [P, 3, TILES])
        q_stage = sb("a_q_stage", [P, 2, COLS])
        kv_ch = sb("a_kv_ch", [P, 4, COLS])
        kv_tok = sb("a_kv_tok", [P, 2, 4 * P])
        lam = sb("a_lam", [P, 6, KT])
        proj = pb("a_proj", [P, 2, 512])
        xt = pb("a_xt", [P, 2, KT, P])
        pt = pb("a_pt", [P, 512])
        kvt = xt[:, :, :, :].rearrange("p a b c -> p a (b c)")

        rows_in = sem("a_rows_in")
        bias_in = sem("a_bias_in")
        x_in = [sem(f"a_x_in{t}") for t in range(TILES)]
        w_in = [sem(f"a_w_in{s}") for s in range(2)]
        consts = sem("a_consts")
        rows_t = sem("a_rows_t")
        params = sem("a_params")
        squared = sem("a_squared")
        meaned = sem("a_meaned")
        rooted = sem("a_rooted")
        normed = sem("a_normed")
        x_turned = sem("a_x_turned")
        scaled = sem("a_scaled")
        hi_ready = sem("a_hi_ready")
        lo_ready = sem("a_lo_ready")
        w_hi_ready = sem("a_w_hi_ready")
        w_lo_ready = sem("a_w_lo_ready")
        proj_done = sem("a_proj_done")
        proj_out = sem("a_proj_out")
        q_cols = sem("a_q_cols")
        q_stored = [sem(f"a_q_stored{s}") for s in range(2)]
        k_stored = sem("a_k_stored")
        bias_made = sem("a_bias_made")
        kv_turned = sem("a_kv_turned")
        kv_out = sem("a_kv_out")
        kv_stored = [sem(f"a_kv_stored{s}") for s in range(2)]
        dve_step = sem("a_dve_step")
        act_step = sem("a_act_step")
        lam_exp = sem("a_lam_exp")
        q_block0 = sem("a_q_block0")
        old_rows = sem("a_old_rows")

        w_view = g.w_in.rearrange("o (k p) c -> p (o k) c", p=P)

        with nc.Block() as block:

            @block.sync
            def _(sp):
                def load_w(slot, index, col):
                    sp.wait_ge(w_lo_ready, index)
                    sp.dma_start(w_raw[:, slot, :, :], w_view[:, :, bass.ds(col, P)]).then_inc(w_in[slot], 16)

                sp.sem_inc(q_stored[0], 32)
                sp.sem_inc(q_stored[1], 32)
                for r, n, src in ((R_CONVSTATE, 24, g.state_rnn_conv.rearrange("o s j d -> (o s j) d")),
                                  (R_H0, 8, g.state_rnn_h[0]), (R_CONVW, 4, g.w_rnn_conv[0]),
                                  (R_CONVB, 1, g.b_rnn_conv), (R_BR, 1, g.b_rgate), (R_BI, 1, g.b_igate),
                                  (R_LAM, 1, g.rglru_lambda), (R_GMIX, 1, g.g_mix), (R_GFFN, 1, g.g_ffn)):
                    sp.dma_start(rows[r:r + n, :], src).then_inc(rows_in, 16)
                sp.dma_start(x_tok[0:DEC, 0, :], g.x_sample.rearrange("s o d -> (s o) d")).then_inc(x_in[0], 16)
                sp.dma_start(x_tok[DEC:HEAD_ROWS, 0, :], g.meta_tokens).then_inc(x_in[0], 16)
                for t in range(1, TILES):
                    sp.dma_start(x_tok[:, t, :], g.x_prompt[0, P * (t - 1):P * t, :]).then_inc(x_in[t], 16)
                    if t == 4:
                        load_w(0, 1, 0)
                load_w(1, 2, P)
                sp.dma_start(bias_col[:, :], g.sb_bias.rearrange("o h -> h o")).then_inc(bias_in, 16)
                sp.dma_start(g.bias_all[:, :], g.sb_bias[0, :].partition_broadcast(P)).then_inc(bias_in, 16)
                sp.dma_start(g.table[0:1, PAGES:PAGES + DEC * PAGES],
                             g.page_table.rearrange("(o a) b -> o (a b)", o=1)).then_inc(bias_in, 16)
                sp.dma_start(g.sample_rnn_conv[0, :, 0:2, :], g.state_rnn_conv[0, :, 1:3, :]).then_inc(old_rows, 16)
                sp.dma_start(g.sample_ffn_conv[0, :, 0:1, :], g.state_ffn_conv[0, :, 1:2, :]).then_inc(old_rows, 16)
                sp.wait_ge(bias_made, 1)
                sp.dma_start(g.q_scr[:, HD, :], bias_rows[:, :]).then_inc(k_stored, 16)
                with sp.Fori(0, KT // 2, 1) as i:
                    for s in range(2):
                        load_w(s, nth(i, 2, s) + 2, i * (2 * P) + (2 + s) * P)
                        sp.wait_ge(q_cols, nth(i, 2, s))
                        for h in range(2):
                            sp.dma_start(g.q_scr[bass.ds(i * 4 + 2 * s + h, 1), 0:HD, :].rearrange("a p c -> p (a c)"),
                                         q_stage[HD * h:HD * (h + 1), s, FIRST:LAST]).then_inc(q_stored[s], 16)
                for n in (10, 11):
                    load_w(n % 2, n + 1, P * n)
                for j in range(2):
                    sp.wait_ge(proj_out, 2 + CHUNKS * (KT + j + 1))
                    for h in range(2):
                        sp.dma_start(g.k_scr[2 * j + h, :, :],
                                     kv_ch[HD * h:HD * (h + 1), j, FIRST:LAST]).then_inc(k_stored, 16)
                for t in range(TILES):
                    sp.wait_ge(kv_out, t + 1)
                    done = kv_stored[t % 2]
                    for kv, seq, dec in ((0, g.prompt_k, g.sample_k), (1, g.prompt_v, g.sample_v)):
                        src = kv_tok[:, t % 2, 256 * kv:256 * kv + 256]
                        to = seq[0, 0].rearrange("t h d -> t (h d)")
                        if t == 0:
                            sp.dma_start(to[0:META, :], src[DEC:HEAD_ROWS, :]).then_inc(done, 16)
                            sp.dma_start(dec[0, :, 0].rearrange("s h d -> s (h d)"), src[0:DEC, :]).then_inc(done, 16)
                        else:
                            r = META + P * (t - 1)
                            sp.dma_start(to[r:r + P, :], src).then_inc(done, 16)
                    if t == 0:
                        sp.dma_start(g.v_scr[0:META, :], kv_tok[DEC:HEAD_ROWS, 0, 256:512]).then_inc(done, 16)
                    else:
                        sp.dma_start(g.v_scr[r:r + P, :], kv_tok[:, t % 2, 256:512]).then_inc(done, 16)
                sp.wait_ge(kv_stored[0], 16 * (5 + 3 * 4))
                sp.wait_ge(kv_stored[1], 16 * (3 * 4))
                sp.wait_ge(k_stored, 16 * 5)
                sp.wait_ge(q_stored[0], 32 * 5)
                sp.wait_ge(q_stored[1], 32 * 5)
                sp.wait_ge(old_rows, 32)
                sp.wait_ge(bias_in, 48)

            @block.gpsimd
            def _(pool):
                pool.sem_inc(w_lo_ready, 2)
                pool.memset(g.ident[:, :], 0.0).then_inc(consts, 1)
                pool.memset(g.tri[:, :], 1.0).then_inc(consts, 1)
                pool.wait_ge(consts, 2)
                pool.affine_select(out=g.ident[:, :], in_=g.ident[:, :], compare_op=ALU.not_equal, fill=1.0,
                                   base=0, pattern=[[-1, P]], channel_multiplier=1).then_inc(consts, 1)
                pool.affine_select(out=g.tri[:, :], in_=g.tri[:, :], compare_op=ALU.is_ge, fill=0.0,
                                   base=0, pattern=[[-1, P]], channel_multiplier=1).then_inc(consts, 1)
                pool.memset(g.ones[:, :], 1.0).then_inc(consts, 1)
                pool.memset(g.q_block[:, :, :, :], 0.0).then_inc(q_block0, 1)
                pool.memset(g.table[:, 0:PAGES], 0).then_inc(q_block0, 1)
                pool.memset(g.page_mask[:, :, :], 1.0).then_inc(consts, 1)
                pool.wait_ge(consts, 6)
                pool.memset(g.page_mask[:, :, PAGES - 1:PAGES + 1], 0.0).then_inc(consts, 1)
                pool.memset(g.n_hi[:, :, LAST:COLS].bitcast(F32), 0.0).then_inc(consts, 1)
                pool.memset(g.n_lo[:, :, LAST:COLS].bitcast(F32), 0.0).then_inc(consts, 1)

                def low_part(slot, index):
                    pool.wait_ge(w_hi_ready, index)
                    pool.tensor_tensor(w_lo[:, slot, :, :], w_raw[:, slot, :, :],
                                       w_hi[:, slot, :, :].bitcast(F32), ALU.subtract).then_inc(w_lo_ready, 1)

                with pool.Fori(0, 6, 1) as i:
                    for s in range(2):
                        low_part(s, nth(i, 2, s))

            @block.scalar
            def _(act):
                own = Chain(act, act_step)
                act.sem_inc(proj_out, 2)

                def square(t):
                    _, nr = token_tile(t)
                    act.wait_ge(x_in[t], 32 if t == 0 else 16)
                    if t >= 2:
                        act.wait_ge(squared, t - 1)
                    act.activation(junk[0:nr, t % 2, :], x_tok[0:nr, t, :], ACT.Square,
                                   accum_out=stat[0:nr, 0, t:t + 1]).then_inc(squared, 1)

                def high_part(slot, chunks, turn):
                    act.wait_ge(w_in[slot], turn)
                    act.wait_ge(proj_done, chunks)
                    act.activation(w_hi[:, slot, :, :], w_raw[:, slot, :, :], ACT.Copy).then_inc(w_hi_ready, 1)

                square(0)
                square(1)
                for t in range(TILES):
                    c0, nr = token_tile(t)
                    act.wait_ge(meaned, t + 1)
                    act.activation(stat[0:nr, 2, t:t + 1], stat[0:nr, 1, t:t + 1], ACT.Sqrt).then_inc(rooted, 1)
                    if t + 2 < TILES:
                        square(t + 2)
                    act.wait_ge(scaled, t + 1)
                    act.activation(g.n_hi[:, :, c0:c0 + nr], tmp[:, t % 2, :, 0:nr], ACT.Copy).then_inc(hi_ready, 1)
                    if t in (4, 6):
                        high_part((t - 4) // 2, 3 * (t - 2) // 2, 16)
                act.activation(lam[:, 0, :], g.par[:, :, R_LAM], ACT.Abs).then_inc(act_step, 1)
                act.wait_ge(act_step, 1)
                act.activation(lam[:, 1, :], lam[:, 0, :], ACT.Exp, scale=-1.0).then_inc(lam_exp, 1)

                def evacuate(bank, index, out, scale):
                    act.wait_ge(proj_done, index + 6)
                    act.activation(out, proj[:, bank, 0:CW], ACT.Copy, scale=scale).then_inc(proj_out, 1)

                with act.Fori(0, KT // 2, 1) as i:
                    for s in range(2):
                        act.wait_ge(q_stored[s], nth(i, 32, 31))
                        for c in range(CHUNKS):
                            n = CHUNKS * s + c
                            evacuate(n % 2, nth(i, 6, n), q_stage[:, s, CW * c:CW * (c + 1)], HD ** -0.5)
                            if c == 1 and s == 1:
                                high_part(0, nth(i, 6, 8), nth(i, 16, 31))
                    high_part(1, nth(i, 6, 11), nth(i, 16, 31))
                for j in range(4):
                    for c in range(CHUNKS):
                        n = 24 + CHUNKS * j + c
                        evacuate(n % 2, n + 1, kv_ch[:, j, CW * c:CW * (c + 1)], 1.0)
                    if j < 2:
                        high_part(j, 3 * (11 + j), 16 * 6)

            @block.vector
            def _(dve):
                own = Chain(dve, dve_step)
                dve.wait_ge(rows_t, 1)
                dve.tensor_copy(g.par[:, :, :].rearrange("p k r -> p (k r)"),
                                pt[:, 0:KT * N_ROWS]).then_inc(params, 1)
                dve.wait_ge(params, 1)
                for t in range(TILES):
                    c0, nr = token_tile(t)
                    dve.wait_ge(squared, t + 1)
                    dve.tensor_scalar(stat[0:nr, 1, t:t + 1], stat[0:nr, 0, t:t + 1], 1.0 / D, EPS,
                                      ALU.mult, ALU.add).then_inc(meaned, 1)
                    dve.wait_ge(rooted, t + 1)
                    own.step(dve.reciprocal(stat[0:nr, 2, t:t + 1], stat[0:nr, 2, t:t + 1]))
                    dve.tensor_scalar(x_tok[0:nr, t, :], x_tok[0:nr, t, :], stat[0:nr, 2, t:t + 1], None,
                                      ALU.mult).then_inc(normed, 1)
                    dve.wait_ge(x_turned, t + 1)
                    if t >= 2:
                        dve.wait_ge(hi_ready, t - 1)
                    dve.tensor_tensor(tmp[:, t % 2, :, 0:nr], xt[:, t % 2, :, 0:nr],
                                      g.par[:, :, R_GMIX:R_GMIX + 1].to_broadcast([P, KT, nr]),
                                      ALU.mult).then_inc(scaled, 1)
                    dve.wait_ge(hi_ready, t + 1)
                    dve.tensor_tensor(g.n_lo[:, :, c0:c0 + nr], tmp[:, t % 2, :, 0:nr],
                                      g.n_hi[:, :, c0:c0 + nr].bitcast(F32), ALU.subtract).then_inc(lo_ready, 1)
                own.step(dve.memset(bias_rows[:, :], 1.0))
                dve.wait_ge(bias_in, 48)
                dve.tensor_scalar(bias_rows[:, :], bias_rows[:, :], bias_col[:, 0:1], None,
                                  ALU.mult).then_inc(bias_made, 1)
                dve.wait_ge(lam_exp, 1)
                own.step(dve.tensor_scalar(lam[:, 2, :], lam[:, 1, :], 2.0, None, ALU.add))
                own.step(dve.reciprocal(lam[:, 2, :], lam[:, 2, :]))
                own.step(dve.tensor_tensor(lam[:, 2, :], lam[:, 1, :], lam[:, 2, :], ALU.mult))
                own.step(dve.tensor_tensor(lam[:, 3, :], lam[:, 2, :], lam[:, 2, :], ALU.mult))
                own.step(dve.tensor_scalar(lam[:, 4, :], lam[:, 3, :], 1.0 / 15, None, ALU.mult))
                for odd in (13, 11, 9, 7, 5, 3):
                    own.step(dve.scalar_tensor_tensor(lam[:, 4, :], lam[:, 4, :], 1.0 / odd, lam[:, 3, :],
                                                      ALU.add, ALU.mult))
                own.step(dve.scalar_tensor_tensor(lam[:, 4, :], lam[:, 4, :], 1.0, lam[:, 2, :], ALU.add, ALU.mult))
                own.step(dve.tensor_scalar(lam[:, 5, :], g.par[:, :, R_LAM], -1.0, 0.0, ALU.mult, ALU.max))
                own.step(dve.scalar_tensor_tensor(lam[:, 4, :], lam[:, 4, :], 2.0, lam[:, 5, :], ALU.mult, ALU.add))
                own.step(dve.tensor_scalar(g.rates[:, 0, :], lam[:, 4, :], -4.0, None, ALU.mult))
                own.step(dve.tensor_scalar(g.rates[:, 1, :], lam[:, 4, :], 4.0, None, ALU.mult))
                own.step(dve.tensor_scalar(g.rates[:, 2, :], g.par[:, :, R_BR], 0.5, None, ALU.mult))
                own.step(dve.tensor_scalar(g.rates[:, 3, :], g.par[:, :, R_BI], 0.5, None, ALU.mult))
                with dve.Fori(0, KT // 2, 1) as i:
                    for s in range(2):
                        dve.wait_ge(proj_out, nth(i, 6, 3 * s + 2, 2))
                        dve.tensor_copy(g.q_dec[:, bass.ds(i * 2 + s, 1), :].rearrange("p a c -> p (a c)"),
                                        q_stage[:, s, 0:DEC]).then_inc(q_cols, 1)
                dve.wait_ge(q_cols, KT)
                dve.wait_ge(q_block0, 1)
                for h in range(HEADS):
                    half, src = (h % 8) // 4, HD * (h % 2)
                    dve.tensor_copy(g.q_block[HD * half:HD * (half + 1), h // 8, :, h % 8],
                                    g.q_dec[src:src + HD, h // 2, :])
                for t in range(TILES):
                    _, nr = token_tile(t)
                    dve.wait_ge(kv_turned, t + 1)
                    if t >= 2:
                        dve.wait_ge(kv_stored[t % 2], 16 * (5 * (t % 2 == 0) + 3 * (t // 2 - (t % 2 == 0))))
                    dve.tensor_copy(kv_tok[0:nr, t % 2, :], kvt[0:nr, t % 2, 0:512]).then_inc(kv_out, 1)

            @block.tensor
            def _(pe):
                pe.sem_inc(proj_done, 6)
                pe.wait_ge(consts, 3)
                pe.wait_ge(rows_in, 16 * 9)
                for k in range(KT):
                    last = pe.transpose(pt[:, N_ROWS * k:N_ROWS * (k + 1)], rows[:, P * k:P * (k + 1)],
                                        g.ident[0:N_ROWS, 0:N_ROWS])
                last.then_inc(rows_t, 1)
                for t in range(TILES):
                    _, nr = token_tile(t)
                    pe.wait_ge(normed, t + 1)
                    if t >= 2:
                        pe.wait_ge(scaled, t - 1)
                    for k in range(KT):
                        last = pe.transpose(xt[:, t % 2, k, 0:nr], x_tok[0:nr, t, P * k:P * (k + 1)],
                                            g.ident[0:nr, 0:nr])
                    last.then_inc(x_turned, 1)
                pe.wait_ge(lo_ready, TILES)
                pe.wait_ge(consts, 9)

                def tile(slot, index, first_chunk, base):
                    pe.wait_ge(w_lo_ready, index + 2)
                    for c in range(CHUNKS):
                        n = first_chunk + c
                        pe.wait_ge(proj_out, base + n + 1)
                        last = project(pe, proj[:, n % 2, 0:CW], w_hi[:, slot], w_lo[:, slot],
                                       g.n_hi, g.n_lo, CW * c)
                        last.then_inc(proj_done, 1)

                with pe.Fori(0, 6, 1) as i:
                    for s in range(2):
                        tile(s, nth(i, 2, s), CHUNKS * s, i * 6)
                pe.wait_ge(proj_out, 2 + 36)
                for t in range(TILES):
                    c0, nr = token_tile(t)
                    if t >= 2:
                        pe.wait_ge(kv_out, t - 1)
                    for j in range(4):
                        last = pe.transpose(kvt[0:nr, t % 2, P * j:P * (j + 1)], kv_ch[:, j, c0:c0 + nr],
                                            g.ident[:, :])
                    last.then_inc(kv_turned, 1)


BLOCK_ORDER = (8, 0, 7, 1, 6, 2, 5, 3, 4)
UNITS = tuple((a, b) for a in range(2) for b in BLOCK_ORDER)
SLOTS = len(UNITS)
Z_AT = (0, 1040, 1056, 0, 144, 928, 1200, 0, 400, 928, 0, 16, 928, 1072, 0, 272, 1040, 1440)
Z_RING = 1968
Z_BANK_AT = {0: 1040, 1: 1024, 2: 1024, 3: 1024}
LAG = 2
SUMS_RING = 2096


def unit(s):
    a, b = UNITS[s]
    return (a, b, 0, META, META) if b == 0 else (a, b, META + P * (b - 1), P, META + P * b)


def key_groups(b):
    blocks = [(m, META + P * (m - 1), P) for m in range(1, b + 1)] + [(0, 0, META)]
    return [blocks[n:n + 4] for n in range(0, len(blocks), 4)]


GROUPS_TO = [0]
for _, _b in UNITS:
    GROUPS_TO.append(GROUPS_TO[-1] + len(key_groups(_b)))
GROUPS = GROUPS_TO[-1]


def keys_of(s):
    return unit(s)[4] if 0 <= s < SLOTS else 0


def soft_at(s):
    return 0 if s % 2 == 0 else SUMS_RING - keys_of(s)


def pos_at(s):
    at = keys_of(s) if s % 2 == 0 else keys_of(s + 1)
    assert at + keys_of(s) <= (SUMS_RING - keys_of(s + 1) if s % 2 == 0 else soft_at(s))
    return at


def score_banks(s):
    at = Z_BANK_AT.get(unit(s)[1], 0)
    return set(range(at // 512, (at + keys_of(s) - 1) // 512 + 1))


def phase_mix(nc, g, sem):
    ctx = ExitStack()
    with ctx:
        sb = lambda name, shape, dt=F32: ctx.enter_context(nc.sbuf_tensor(name, shape, dt))
        pb = lambda name, shape: ctx.enter_context(nc.psum_tensor(name, shape, F32))
        w_raw = sb("b_w_raw", [P, 2, KT, P])
        w_hi = sb("b_w_hi", [P, 2, KT, P], F32R)
        w_lo = sb("b_w_lo", [P, 2, KT, P], F32R)
        q_in = sb("b_q_in", [HD + 1, 2, PROMPT])
        k_in = sb("b_k_in", [HD + 1, PROMPT])
        v_in = sb("b_v_in", [P, TILES, HD])
        z = sb("b_z", [P, Z_RING])
        sums = sb("b_sums", [P, SUMS_RING])
        never = sb("b_never", [P, P], BF16)
        ident_b = sb("b_ident_b", [P, P], BF16)
        w_t = sb("b_w_t", [P, 2, 4, P])
        xr = sb("b_xr", [P, COLS])
        xc = sb("b_xc", [P, COLS])
        gr = sb("b_gr", [P, COLS])
        gb = sb("b_gb", [P, COLS])
        rg = sb("b_rg", [P, COLS])
        ig = sb("b_ig", [P, COLS])
        gate_w = sb("b_gate_w", [P, 2, P])
        pc = sb("b_pc", [P, N_ROWS])
        rc = sb("b_rc", [P, 4])
        k_page = sb("b_k_page", [P, 2, 2, KVH * HD])
        v_page = sb("b_v_page", [P, 2, KVH * HD])
        k_t = sb("b_k_t", [P, 4, P])
        zd = sb("b_zd", [P, HEADS, PAGES])
        softd = sb("b_softd", [P, HEADS, PAGES])
        posd = sb("b_posd", [P, HEADS, PAGES])
        spd = sb("b_spd", [P, HEADS, PAGES + 1])
        laterd = sb("b_laterd", [P, HEADS, PAGES + 1])
        vacc = sb("b_vacc", [P, 2, 8])
        p_proj = pb("b_p_proj", [P, 2, 512])
        p_z = pb("b_p_z", [P, 3 * 512])
        p_wt = pb("b_p_wt", [P, 4, P])
        p_av = pb("b_p_av", [P, 512])
        p_kt = pb("b_p_kt", [P, 512])
        p_zd = p_av[:, 256:512].rearrange("p (h n) -> p h n", n=PAGES)
        p_td = p_kt[:, 0:256].rearrange("p (h n) -> p h n", n=PAGES)
        p_vd = p_kt[:, 0:16].rearrange("p (a h) -> p a h", a=2)

        w_in = [sem(f"b_w_in{s}") for s in range(2)]
        q_arr = [sem(f"b_q_arr{s}") for s in range(2)]
        k_arr, v_arr, gw_arr = sem("b_k_arr"), sem("b_v_arr"), sem("b_gw_arr")
        kp_arr = [sem(f"b_kp_arr{s}") for s in range(2)]
        vp_arr = sem("b_vp_arr")
        inits = sem("b_inits")
        w_hi_ready = sem("b_w_hi_ready")
        w_lo_ready = sem("b_w_lo_ready")
        proj_done = sem("b_proj_done")
        proj_out = sem("b_proj_out")
        qk_done = sem("b_qk_done")
        z_copied = sem("b_z_copied")
        pos_done = sem("b_pos_done")
        soft_done = sem("b_soft_done")
        summed = sem("b_summed")
        arg_ready = sem("b_arg_ready")
        w_ready = sem("b_w_ready")
        wt_turned = sem("b_wt_turned")
        wt_out = sem("b_wt_out")
        av_group = sem("b_av_group")
        av_out = sem("b_av_out")
        kt_turned = sem("b_kt_turned")
        kt_out = sem("b_kt_out")
        zd_done = sem("b_zd_done")
        zd_read = sem("b_zd_read")
        posd_done = sem("b_posd_done")
        softd_done = sem("b_softd_done")
        laterd_done = sem("b_laterd_done")
        td_done = sem("b_td_done")
        argd_ready = sem("b_argd_ready")
        wd_ready = sem("b_wd_ready")
        vd_done = sem("b_vd_done")
        vd_added = sem("b_vd_added")
        att_out = sem("b_att_out")
        xc_ready = sem("b_xc_ready")
        tail_done = sem("b_tail_done")
        tail_act = sem("b_tail_act")
        act_step = sem("b_act_step")
        dve_step = sem("b_dve_step")
        gated = sem("b_gated")
        root_used = sem("b_root_used")
        masks = sem("b_masks")
        passed = sem("b_passed")

        w_view = g.w_in.rearrange("o (k p) c -> p (o k) c", p=P)
        T_GR, T_GB, T_R, T_I, T_GA, T_Y, T_SQRT, T_LN, T_A, T_RS, TAIL = range(11)

        with nc.Block() as block:

            @block.sync
            def _(sp):
                def load_w(slot, index, col):
                    sp.wait_ge(w_lo_ready, index)
                    sp.dma_start(w_raw[:, slot, :, :], w_view[:, :, bass.ds(col, P)]).then_inc(w_in[slot], 16)

                def load_pages(i, j, first, cache, to, arrived):
                    for n in range(2):
                        page = sp.value_load(g.table[0:1, bass.ds(first + (2 * j + n), 1)],
                                             min_val=0, max_val=N_PHYS - 1)
                        src = cache[0].rearrange("n t h d -> n t (h d)")[bass.ds(page, 1), :, :]
                        sp.dma_start(to[:, n, :], src.rearrange("a t c -> (a t) c")).then_inc(arrived, 16)

                def load_k_pages(i, j):
                    sp.wait_ge(kt_turned, nth(i, 8, j))
                    load_pages(i, j, i * PAGES + PAGES, g.cache_k, k_page[:, j % 2], kp_arr[j % 2])

                def load_v_pages(i, j):
                    sp.wait_ge(vd_done, nth(i, 8, j))
                    load_pages(i, j, i * PAGES, g.cache_v, v_page, vp_arr)

                load_w(0, 1, XR_COL)
                with sp.Fori(0, KT, 1) as i:
                    load_w(1, nth(i, 4, 1), i * P + GA_COL)
                    load_k_pages(i, 0)

                    def load_q(a):
                        sp.wait_ge(qk_done, nth(i, SLOTS, 9 * a + 8))
                        sp.dma_start(q_in[:, a, :], g.q_scr[bass.ds(i * 2 + a, 1), :, :]
                                     .rearrange("a p c -> p (a c)")).then_inc(q_arr[a], 16)
                    load_q(0)
                    load_w(0, nth(i, 4, 2), i * P + GR_COL)
                    load_k_pages(i, 1)
                    load_v_pages(i, 0)
                    load_q(1)
                    group = i // 2
                    sp.dma_start(k_in[0:HD, :], g.k_scr[bass.ds(group, 1), :, :]
                                 .rearrange("a p c -> p (a c)")).then_inc(k_arr, 16)
                    sp.wait_ge(proj_done, nth(i, SLOTS, SLOTS - 1))
                    for n, w in ((0, g.w_rgate), (1, g.w_igate)):
                        for h in range(2):
                            sp.dma_start(gate_w[HD * h:HD * (h + 1), n, HD * h:HD * (h + 1)],
                                         w[0, bass.ds(i * 2 + h, 1), :, :].rearrange("a p c -> p (a c)"))\
                              .then_inc(gw_arr, 16)
                    sp.wait_ge(av_group, nth(i, GROUPS, GROUPS - 1))
                    sp.dma_start(v_in[0:META, 0, :], g.v_scr[0:META, bass.ds(group * HD, HD)]).then_inc(v_arr, 16)
                    sp.dma_start(v_in[:, 1:TILES, :], g.v_scr[META:PROMPT, bass.ds(group * HD, HD)]
                                 .rearrange("(t p) d -> p t d", p=P)).then_inc(v_arr, 16)
                    load_w(1, nth(i, 4, 3), i * P + GB_COL)
                    load_k_pages(i, 2)
                    load_v_pages(i, 1)
                    load_k_pages(i, 3)
                    load_w(0, nth(i, 4, 4), i * P + (XR_COL + P))
                    for j in range(2, 8):
                        load_v_pages(i, j)
                        if j + 2 < 8:
                            load_k_pages(i, j + 2)
                for j in range(8):
                    load_v_pages(KT, j)

            @block.gpsimd
            def _(pool):
                pool.sem_inc(w_lo_ready, 2)
                for n, (part, value) in enumerate(((z[:, 0:P], 0.0), (gate_w[:, :, :], 0.0), (k_in[HD:HD + 1, :], 1.0),
                                                   (xc[:, LAST:COLS], 0.0), (zd[:, :, :], 0.0),
                                                   (spd[:, :, PAGES:PAGES + 1], 0.0))):
                    if n:
                        pool.wait_ge(inits, n)
                    pool.memset(part, value).then_inc(inits, 1)
                pool.affine_select(out=z[:, 0:P], in_=z[:, 0:P], compare_op=ALU.is_gt, fill=-1e30, base=0,
                                   pattern=[[-1, P]], channel_multiplier=1).then_inc(inits, 1)

                def low_part(slot, index):
                    pool.wait_ge(w_hi_ready, index)
                    pool.tensor_tensor(w_lo[:, slot, :, :], w_raw[:, slot, :, :],
                                       w_hi[:, slot, :, :].bitcast(F32), ALU.subtract).then_inc(w_lo_ready, 1)

                low_part(0, 1)
                with pool.Fori(0, KT, 1) as i:
                    for t in range(4):
                        low_part((t + 1) % 2, nth(i, 4, t + 1))

            @block.scalar
            def _(act):
                own = Chain(act, act_step)
                act.sem_inc(proj_out, 2)
                act.sem_inc(wd_ready, 1)

                def high_part(slot, chunks, turns):
                    act.wait_ge(w_in[slot], turns)
                    act.wait_ge(proj_done, chunks)
                    act.activation(w_hi[:, slot, :, :], w_raw[:, slot, :, :], ACT.Copy).then_inc(w_hi_ready, 1)

                def tail_step(i, out, in_, func, after=None, **kw):
                    if after is not None:
                        act.wait_ge(tail_act, nth(i, TAIL, after))
                    act.activation(out, in_, func, **kw).then_inc(tail_act, 1)

                def tail(i):
                    ga = g.mix[:, bass.ds(i + 1, 1), :].rearrange("p a c -> p (a c)")
                    act.wait_ge(proj_out, nth(i, SLOTS, SLOTS - 1, 2))
                    tail_step(i, gr[:, :], gr[:, :], ACT.Gelu_apprx_tanh)
                    tail_step(i, gb[:, :], gb[:, :], ACT.Tanh, scale=0.5)
                    tail_step(i, rg[:, :], rg[:, :], ACT.Tanh, bias=rc[:, 2:3], scale=0.5)
                    tail_step(i, ig[:, :], ig[:, :], ACT.Tanh, bias=rc[:, 3:4], scale=0.5)
                    tail_step(i, ga, ga, ACT.Tanh, scale=0.5)
                    act.wait_ge(gated, nth(i, 1, 0))
                    tail_step(i, gr[:, :], rg[:, :], ACT.Tanh, T_R, bias=rc[:, 1:2], scale=rc[:, 1:2])
                    tail_step(i, xr[:, :], gr[:, :], ACT.Sqrt, T_Y, scale=2.0)
                    act.preload_act_table_set("natural_log_exp_and_others")
                    tail_step(i, gr[:, :], gr[:, :], ACT.Ln, T_SQRT, bias=1.0)

                def late_tail(i, s):
                    if s == 0:
                        tail_step(i, rg[:, :], rg[:, :], ACT.Exp, bias=rc[:, 0:1], scale=rc[:, 0:1])
                    if s == 1:
                        tail_step(i, gr[:, :], gr[:, :], ACT.Exp, T_LN, scale=-0.5)

                act.wait_ge(inits, 7)
                act.activation(never[:, :], z[:, 0:P], ACT.Copy).then_inc(masks, 1)
                act.activation(ident_b[:, :], g.ident[:, :], ACT.Copy).then_inc(masks, 1)
                high_part(0, SLOTS, 16)
                act.preload_act_table_set("natural_log_exp_and_others")

                def slots(i, first):
                    own.turn(0, i, 2 * SLOTS + 2)
                    for s in range(SLOTS + LAG):
                        if s % 3 == 0 and s < 12:
                            t = s // 3
                            high_part((t + 1) % 2, nth(i, SLOTS, 11) if t == 0 else nth(i, SLOTS, 3 * t - 1, SLOTS),
                                      16 * (nth(i, 2, (0, 1, 1, 2)[t])))
                        if s < SLOTS:
                            a, b, q0, nq, nk = unit(s)
                            zs, so = z[0:nq, Z_AT[s]:Z_AT[s] + nk], sums[0:nq, soft_at(s):soft_at(s) + nk]
                            act.wait_ge(z_copied, nth(i, SLOTS, s, 2))
                            act.wait_ge(summed, nth(i, SLOTS, s))
                            own.step(act.activation(so, zs, ACT.Abs))
                            own.step(act.activation(so, so, ACT.Exp, scale=-1.0))
                            act.activation(so, so, ACT.Ln, bias=1.0).then_inc(soft_done, 1)
                        if 1 <= s <= SLOTS:
                            a, b, q0, nq, nk = unit(s - 1)
                            zs = z[0:nq, Z_AT[s - 1]:Z_AT[s - 1] + nk]
                            act.wait_ge(arg_ready, nth(i, SLOTS, s - 1, 1))
                            act.activation(zs, zs, ACT.Exp).then_inc(w_ready, 1)
                        if s < SLOTS:
                            n, c = s // CHUNKS, s % CHUNKS
                            if n < 4:
                                cols = slice(CW * c, CW * (c + 1))
                                out = (xr[:, cols],
                                       g.mix[:, bass.ds(i + 1, 1), cols].rearrange("p a c -> p (a c)"),
                                       gr[:, cols], gb[:, cols])[n]
                            else:
                                c = (s - 12) // 2
                                out = (rg, ig)[s % 2][:, CW * c:CW * (c + 1)]
                            if s == 0 and not first:
                                act.wait_ge(root_used, nth(i, 1, 0) - 1)
                            if s == 6 and not first:
                                act.wait_ge(tail_done, nth(i, 1, 0) - 1)
                            act.wait_ge(proj_done, nth(i, SLOTS, s, SLOTS))
                            act.activation(out, p_proj[:, s % 2, 0:CW], ACT.Copy).then_inc(proj_out, 1)
                        if not first:
                            late_tail(i - 1, s)
                        if s == SLOTS:
                            act.wait_ge(zd_read, nth(i, 1, 0, 1))
                            own.step(act.activation(softd[:, :, :], zd[:, :, :], ACT.Abs))
                            own.step(act.activation(softd[:, :, :], softd[:, :, :], ACT.Exp, scale=-1.0))
                            act.activation(softd[:, :, :], softd[:, :, :], ACT.Ln, bias=1.0).then_inc(softd_done, 1)
                    assert own.n == 2 * SLOTS + 2
                    tail(i)
                    act.wait_ge(argd_ready, nth(i, 1, 0, 1))
                    act.activation(zd[:, :, :], zd[:, :, :], ACT.Exp).then_inc(wd_ready, 1)

                slots(0, True)
                with act.Fori(1, KT, 1) as i:
                    slots(i, False)
                for s in range(2):
                    late_tail(KT - 1, s)

            @block.vector
            def _(dve):
                own = Chain(dve, dve_step)
                for s, n in ((z_copied, 2), (summed, 2), (arg_ready, 1), (wt_out, 1), (av_out, 1), (zd_read, 1),
                             (argd_ready, 1), (vd_added, 1)):
                    dve.sem_inc(s, n)
                dve.wait_ge(inits, 7)
                dve.wait_ge(masks, 2)

                def turn_out(i, s, n):
                    a, b, q0, nq, nk = unit(s)
                    q = GROUPS_TO[s] + n
                    blocks = key_groups(b)[n]
                    full = [m for m, _, size in blocks if size == P]
                    dve.wait_ge(wt_turned, nth(i, GROUPS, q, GROUPS))
                    dve.wait_ge(av_group, nth(i, GROUPS, q - 2, GROUPS))
                    if full and len(blocks) > len(full):
                        dve.tensor_copy(w_t[:, q % 2, 0:len(full), 0:nq], p_wt[:, 0:len(full), 0:nq])
                    if len(blocks) > len(full):
                        r = len(full)
                        dve.tensor_copy(w_t[0:META, q % 2, r, 0:nq], p_wt[0:META, r, 0:nq]).then_inc(wt_out, 1)
                    else:
                        dve.tensor_copy(w_t[:, q % 2, 0:len(full), 0:nq], p_wt[:, 0:len(full), 0:nq])\
                           .then_inc(wt_out, 1)

                def values_out(i, s):
                    a, b, q0, nq, nk = unit(s)
                    dve.wait_ge(av_group, nth(i, GROUPS, GROUPS_TO[s + 1] - 1, GROUPS))
                    rows = slice(HD * a, HD * (a + 1))
                    dve.tensor_copy(g.mix[rows, bass.ds(i, 1), FIRST + q0:FIRST + q0 + nq]
                                    .rearrange("p a c -> p (a c)"),
                                    p_av[rows, P * (s % 2):P * (s % 2) + nq]).then_inc(av_out, 1)

                def conv(i, s):
                    cw = lambda j: pc[:, R_CONVW + j:R_CONVW + j + 1]
                    cb = pc[:, R_CONVB:R_CONVB + 1]
                    if s == 3:
                        own.step(dve.tensor_copy(pc[:, :], g.par[:, bass.ds(i, 1), :].rearrange("p a r -> p (a r)")))
                        own.step(dve.tensor_copy(rc[:, :], g.rates[:, :, bass.ds(i, 1)].rearrange("p r a -> p (r a)")))
                        dve.wait_ge(proj_out, nth(i, SLOTS, 2, 2))
                        own.step(dve.tensor_copy(g.x_out[:, bass.ds(i, 1), 0:DEC].rearrange("p a c -> p (a c)"),
                                                 xr[:, 0:DEC]))
                        own.step(dve.tensor_copy(g.x_out[:, bass.ds(i, 1), DEC:DEC + 3].rearrange("p a c -> p (a c)"),
                                                 xr[:, LAST - 3:LAST]))
                        own.step(dve.tensor_scalar(xc[:, 0:DEC], xr[:, 0:DEC], cw(3), cb, ALU.mult, ALU.add))
                        for j in range(3):
                            own.step(dve.scalar_tensor_tensor(xc[:, 0:DEC], pc[:, R_CONVSTATE + j:R_CONVSTATE + 24:3],
                                                              cw(j), xc[:, 0:DEC], ALU.mult, ALU.add))
                    if s == 5:
                        own.step(dve.memset(xr[:, FIRST - 3:FIRST], 0.0))
                        own.step(dve.tensor_scalar(xc[:, FIRST:LAST], xr[:, FIRST:LAST], cw(3), cb,
                                                   ALU.mult, ALU.add))
                    if s in (7, 8, 10):
                        j = {7: 2, 8: 1, 10: 0}[s]
                        ins = dve.scalar_tensor_tensor(xc[:, FIRST:LAST], xr[:, FIRST - 3 + j:LAST - 3 + j], cw(j),
                                                       xc[:, FIRST:LAST], ALU.mult, ALU.add)
                        if j:
                            own.step(ins)
                        else:
                            ins.then_inc(xc_ready, 1)

                CONV_STEPS = 8 + 2 + 2

                def decode_values(i, j):
                    dve.wait_ge(vd_done, nth(i, 8, j, 1))
                    if j == 0:
                        dve.tensor_copy(vacc[:, :, :], p_vd).then_inc(vd_added, 1)
                    else:
                        dve.tensor_tensor(vacc[:, :, :], vacc[:, :, :], p_vd, ALU.add).then_inc(vd_added, 1)
                    dve.wait_ge(vd_added, nth(i, 8, j, 1))

                def decode_values_out(i):
                    for pair in range(2):
                        for half in range(2):
                            for odd in range(2):
                                t0 = 4 * pair + 2 * half
                                last = dve.tensor_copy(g.att_dec[HD * odd:HD * (odd + 1), t0:t0 + 2, bass.ds(i, 1)],
                                                vacc[HD * half:HD * (half + 1), pair,
                                                     4 * half + odd:4 * half + odd + 3:2].unsqueeze(2))
                    last.then_inc(att_out, 1)

                def tail(i):
                    here = g.mix[:, bass.ds(i, 1), :].rearrange("p a c -> p (a c)")
                    ga = g.mix[:, bass.ds(i + 1, 1), :].rearrange("p a c -> p (a c)")
                    done = lambda n: dve.wait_ge(tail_act, nth(i, TAIL, n))
                    done(T_GB)
                    dve.scalar_tensor_tensor(gb[:, :], gb[:, :], 1.0, gr[:, :], ALU.add, ALU.mult).then_inc(gated, 1)
                    done(T_I)
                    own.step(dve.scalar_tensor_tensor(ig[:, :], ig[:, :], 1.0, xc[:, :], ALU.add, ALU.mult))
                    done(T_GA)
                    own.step(dve.tensor_scalar(g.gate_dec[:, bass.ds(i, 1), :].rearrange("p a c -> p (a c)"),
                                               ga[:, 0:DEC], 1.0, None, ALU.add))
                    dve.wait_ge(av_out, nth(i, SLOTS, SLOTS - 1, 1))
                    own.step(dve.scalar_tensor_tensor(here[:, FIRST:LAST], ga[:, FIRST:LAST], 1.0,
                                                      here[:, FIRST:LAST], ALU.add, ALU.mult))
                    done(T_SQRT)
                    dve.scalar_tensor_tensor(ig[:, :], ig[:, :], 0.5, xr[:, :], ALU.mult, ALU.mult)\
                       .then_inc(root_used, 1)

                def late_tail(i, s):
                    here = g.mix[:, bass.ds(i, 1), :].rearrange("p a c -> p (a c)")
                    if s == 1:
                        dve.wait_ge(root_used, nth(i, 1, 0))
                        dve.wait_ge(tail_act, nth(i, TAIL, T_RS))
                        own.step(dve.tensor_tensor(ig[:, :], ig[:, :], gr[:, :], ALU.mult))
                    if s == 3:
                        own.step(dve.tensor_tensor_scan(ig[:, FIRST:LAST], rg[:, FIRST:LAST], ig[:, FIRST:LAST], 0.0,
                                                        ALU.mult, ALU.add))
                        own.step(dve.tensor_tensor(rg[:, 0:DEC], rg[:, 0:DEC], pc[:, R_H0:R_H0 + DEC], ALU.mult))
                        own.step(dve.tensor_tensor(ig[:, 0:DEC], ig[:, 0:DEC], rg[:, 0:DEC], ALU.add))
                        own.step(dve.tensor_copy(g.h_out[:, bass.ds(i, 1), 0:DEC].rearrange("p a c -> p (a c)"),
                                                 ig[:, 0:DEC]))
                        own.step(dve.tensor_copy(g.h_out[:, bass.ds(i, 1), DEC:DEC + 1].rearrange("p a c -> p (a c)"),
                                                 ig[:, LAST - 1:LAST]))
                    if s == 4:
                        own.step(dve.tensor_tensor(gb[:, 0:LAST], gb[:, 0:LAST], ig[:, 0:LAST], ALU.mult))
                        own.step(dve.tensor_copy(here[:, 0:DEC], gb[:, 0:DEC]))
                    if s == 5:
                        dve.tensor_tensor(here[:, FIRST:LAST], gb[:, FIRST:LAST], here[:, FIRST:LAST],
                                          ALU.add).then_inc(tail_done, 1)

                TAIL_STEPS, LATE_STEPS = 3, 8

                def slots(i, first):
                    if first:
                        own.turn(0, 0, 0)
                    else:
                        own.turn(-LATE_STEPS, i, CONV_STEPS + TAIL_STEPS + LATE_STEPS)
                    for s in range(SLOTS + LAG):
                        v = s - LAG
                        if s < SLOTS:
                            a, b, q0, nq, nk = unit(s)
                            zs = z[0:nq, Z_AT[s]:Z_AT[s] + nk]
                            zp = Z_BANK_AT.get(b, 0)
                            dve.wait_ge(qk_done, nth(i, SLOTS, s, SLOTS))
                            before = GROUPS_TO[s - 2] + GROUPS if s >= 3 else GROUPS_TO[s + 16]
                            dve.wait_ge(wt_turned, nth(i, GROUPS, before - 1))
                            dve.tensor_copy(zs, p_z[0:nq, zp:zp + nk]).then_inc(z_copied, 1)
                        if v >= 0:
                            turn_out(i, v, 0)
                        if 1 <= s <= SLOTS:
                            u = s - 1
                            a, b, q0, nq, nk = unit(u)
                            zs = z[0:nq, Z_AT[u]:Z_AT[u] + nk]
                            so = sums[0:nq, soft_at(u):soft_at(u) + nk]
                            pos = sums[0:nq, pos_at(u):pos_at(u) + nk]
                            dve.wait_ge(z_copied, nth(i, SLOTS, u, 2))
                            dve.wait_ge(arg_ready, nth(i, SLOTS, u))
                            dve.tensor_scalar(pos, zs, 0.0, None, ALU.max).then_inc(pos_done, 1)
                            dve.wait_ge(pos_done, nth(i, SLOTS, u))
                            dve.wait_ge(soft_done, nth(i, SLOTS, u))
                            dve.tensor_tensor_scan(pos[:, ::-1], so[:, ::-1], pos[:, ::-1], 0.0, ALU.add, ALU.add)\
                               .then_inc(summed, 1)
                            dve.wait_ge(summed, nth(i, SLOTS, u, 2))
                            dve.tensor_tensor(zs, zs, pos, ALU.subtract).then_inc(arg_ready, 1)
                        if v >= 0:
                            for n in range(1, len(key_groups(UNITS[v][1]))):
                                turn_out(i, v, n)
                            values_out(i, v)
                        if s < 16:
                            j = s // 2
                            if s % 2 == 0:
                                dve.wait_ge(kt_turned, nth(i, 8, j, 2))
                                if j:
                                    dve.wait_ge(zd_done, nth(i, 8, j - 1))
                                dve.tensor_copy(k_t[:, :, :].rearrange("p a c -> p (a c)"), p_kt[:, :])\
                                   .then_inc(kt_out, 1)
                            else:
                                decode_values(i, j)
                        if not first:
                            late_tail(i - 1, s)
                        conv(i, s)
                        if s == 16:
                            decode_values_out(i)
                            dve.wait_ge(zd_done, nth(i, 8, 7))
                            dve.tensor_tensor(zd[:, :, :], p_zd,
                                              g.bias_all[:, :].unsqueeze(2).to_broadcast([P, HEADS, PAGES]),
                                              ALU.add).then_inc(zd_read, 1)
                            dve.wait_ge(zd_read, nth(i, 1, 0, 1))
                            dve.tensor_scalar(posd[:, :, :], zd[:, :, :], 0.0, None, ALU.max).then_inc(posd_done, 1)
                            dve.wait_ge(posd_done, nth(i, 2, 0))
                        if s == SLOTS + 1:
                            dve.wait_ge(softd_done, nth(i, 1, 0))
                            dve.tensor_tensor(spd[:, :, 0:PAGES], softd[:, :, :], posd[:, :, :],
                                              ALU.add).then_inc(posd_done, 1)
                            dve.wait_ge(posd_done, nth(i, 2, 1))
                            flat = lambda x: x[:, :, :].rearrange("p h n -> p (h n)")
                            n = HEADS * (PAGES + 1)
                            dve.tensor_tensor_scan(flat(laterd)[:, 0:n - 1][:, ::-1],
                                                   flat(g.page_mask)[:, 0:n - 1][:, ::-1],
                                                   flat(spd)[:, 1:n][:, ::-1], 0.0,
                                                   ALU.mult, ALU.add).then_inc(laterd_done, 1)
                    tail(i)
                    assert own.n == CONV_STEPS + TAIL_STEPS + (0 if first else LATE_STEPS), own.n
                    dve.wait_ge(td_done, nth(i, 1, 0))
                    dve.tensor_tensor(zd[:, :, :], zd[:, :, :], p_td, ALU.subtract).then_inc(argd_ready, 1)

                slots(0, True)
                with dve.Fori(1, KT, 1) as i:
                    slots(i, False)
                own.turn(KT * (CONV_STEPS + TAIL_STEPS + LATE_STEPS) - LATE_STEPS, 0, 0)
                for s in (1, 3, 4, 5):
                    late_tail(KT - 1, s)
                dve.wait_ge(tail_done, KT)
                for j in range(8):
                    decode_values(KT, j)
                decode_values_out(KT)
                dve.wait_ge(att_out, KT + 1)
                own.step(dve.tensor_tensor(g.gate_dec[:, :, :], g.gate_dec[:, :, :], g.att_dec[:, :, 1:DEC + 1],
                                           ALU.mult))
                own.step(dve.tensor_tensor(g.mix[:, 0:KT, 0:DEC], g.mix[:, 0:KT, 0:DEC], g.gate_dec[:, :, :],
                                           ALU.add))

            @block.tensor
            def _(pe):
                for s, n in ((proj_done, SLOTS), (qk_done, SLOTS), (wt_turned, GROUPS), (av_group, GROUPS),
                             (kt_turned, 2), (vd_done, 1)):
                    pe.sem_inc(s, n)
                pe.wait_ge(masks, 2)

                def scores(i, s):
                    a, b, q0, nq, nk = unit(s)
                    zp = Z_BANK_AT.get(b, 0)
                    if s == 0:
                        pe.wait_ge(k_arr, 16 * nth(i, 1, 0))
                    if s % 9 == 0:
                        pe.wait_ge(q_arr[a], 16 * nth(i, 1, 0))
                    alone = s == 0 or score_banks(s) & score_banks(s - 1)
                    pe.wait_ge(z_copied, nth(i, SLOTS, s + 1 if alone else s))
                    diagonal = zp + nk - nq
                    c = zp
                    while c < zp + nk:
                        e = min(zp + nk, (c // 512 + 1) * 512)
                        m = max(c, diagonal)
                        last = pe.matmul(p_z[0:nq, c:e], q_in[:, a, q0:q0 + nq], k_in[:, c - zp:e - zp],
                                         start=True, stop=m >= e)
                        if m < e:
                            last = pe.matmul(p_z[0:nq, m:e], ident_b[0:nq, 0:nq],
                                             never[0:nq, m - diagonal:e - diagonal], start=False, stop=True)
                        c = e
                    last.then_inc(qk_done, 1)

                def turn(i, s, n):
                    a, b, q0, nq, nk = unit(s)
                    q = GROUPS_TO[s] + n
                    if n == 0:
                        pe.wait_ge(w_ready, nth(i, SLOTS, s))
                    pe.wait_ge(wt_out, nth(i, GROUPS, q))
                    if b == 0:
                        pe.sem_inc(passed, 1)
                    for r, (m, k0, size) in enumerate(key_groups(b)[n]):
                        last = pe.transpose(p_wt[0:size, r, 0:nq], z[0:nq, Z_AT[s] + k0:Z_AT[s] + k0 + size],
                                            g.ident[0:nq, 0:nq])
                    last.then_inc(wt_turned, 1)

                def values(i, s, n):
                    a, b, q0, nq, nk = unit(s)
                    q = GROUPS_TO[s] + n
                    groups = key_groups(b)
                    if s == 0 and n == 0:
                        pe.wait_ge(v_arr, 32 * nth(i, 1, 0))
                    if n == 0:
                        pe.wait_ge(av_out, nth(i, SLOTS, s))
                    if n == 0 and s == 17 - LAG:
                        pe.wait_ge(zd_read, nth(i, 1, 0, 1))
                    pe.wait_ge(wt_out, nth(i, GROUPS, q, 1))
                    for r, (m, k0, size) in enumerate(groups[n]):
                        last = pe.matmul(p_av[HD * a:HD * (a + 1), P * (s % 2):P * (s % 2) + nq],
                                         v_in[0:size, m, :], w_t[0:size, q % 2, r, 0:nq],
                                         start=(n == 0 and r == 0), stop=(m == 0))
                    last.then_inc(av_group, 1)

                def decode(i, s):
                    j = s // 2
                    if s % 2 == 0:
                        pe.wait_ge(kp_arr[j % 2], 32 * nth(i, 4, j // 2))
                        if j:
                            pe.wait_ge(kt_out, nth(i, 8, j - 1))
                            pe.wait_ge(vd_added, nth(i, 8, j))
                        else:
                            pe.wait_ge(argd_ready, nth(i, 1, 0))
                        for n in range(2):
                            for pair in range(2):
                                r = 2 * n + pair
                                last = pe.transpose(p_kt[:, P * r:P * (r + 1)],
                                                    k_page[:, j % 2, n, P * pair:P * (pair + 1)], g.ident[:, :])
                        last.then_inc(kt_turned, 1)
                    else:
                        pe.wait_ge(kt_out, nth(i, 8, j))
                        if j == 0:
                            pe.wait_ge(zd_read, nth(i, 1, 0))
                        if s > LAG:
                            pe.wait_ge(av_out, nth(i, SLOTS, s - LAG))
                        for n in range(2):
                            for pair in range(2):
                                last = pe.matmul(p_zd[:, 8 * pair:8 * (pair + 1), 2 * j + n], k_t[:, 2 * n + pair, :],
                                                 g.q_block[:, pair, bass.ds(i, 1), :].rearrange("p a h -> p (a h)"),
                                                 start=True, stop=True)
                        last.then_inc(zd_done, 1)
                        decode_v(i, j)

                def decode_v(i, j):
                    if j == 0:
                        pe.wait_ge(wd_ready, nth(i, 1, 0))
                    pe.wait_ge(vp_arr, 32 * nth(i, 8, j))
                    pe.wait_ge(vd_added, nth(i, 8, j))
                    for pair in range(2):
                        for n in range(2):
                            last = pe.matmul(p_vd[:, pair, :], v_page[:, n, P * pair:P * (pair + 1)],
                                             zd[:, 8 * pair:8 * (pair + 1), 2 * j + n], start=(n == 0), stop=(n == 1))
                    last.then_inc(vd_done, 1)

                with pe.Fori(0, KT, 1) as i:
                    for s in range(SLOTS + LAG):
                        v = s - LAG
                        if s == 0:
                            scores(i, 0)
                        groups = len(key_groups(UNITS[v][1])) if v >= 0 else 0
                        if groups:
                            turn(i, v, 0)
                        if s < 12:
                            if s % 3 == 0:
                                pe.wait_ge(w_lo_ready, nth(i, 4, s // 3, 2))
                            pe.wait_ge(proj_out, nth(i, SLOTS, s))
                        for n, (k0, k1) in enumerate(((0, 3), (3, 6), (6, 8))):
                            if s < 12:
                                last = project_part(pe, p_proj[:, s % 2, 0:CW], w_hi[:, s // 3 % 2],
                                                    w_lo[:, s // 3 % 2], g.n_hi, g.n_lo, CW * (s % 3), k0, k1)
                                if n == 2:
                                    last.then_inc(proj_done, 1)
                            elif s < SLOTS and n == 0:
                                if s == 12:
                                    pe.wait_ge(xc_ready, nth(i, 1, 0))
                                    pe.wait_ge(gw_arr, 64 * nth(i, 1, 0))
                                pe.wait_ge(proj_out, nth(i, SLOTS, s))
                                c = (s - 12) // 2
                                pe.matmul(p_proj[:, s % 2, 0:CW], gate_w[:, s % 2, :], xc[:, CW * c:CW * (c + 1)],
                                          start=True, stop=True).then_inc(proj_done, 1)
                            if n == 0 and s < 16:
                                decode(i, s)
                            if n < groups:
                                values(i, v, n)
                            if n + 1 < groups:
                                turn(i, v, n + 1)
                        if s + 1 < SLOTS:
                            scores(i, s + 1)
                    pe.wait_ge(laterd_done, nth(i, 1, 0))
                    pe.wait_ge(vd_added, nth(i, 8, 7, 1))
                    pe.matmul(p_td, g.tri[:, :], spd[:, :, 0:PAGES], start=True, stop=False)
                    pe.matmul(p_td, g.ones[:, :], laterd[:, :, 0:PAGES], start=False, stop=True)\
                      .then_inc(td_done, 1)
                for j in range(8):
                    decode_v(KT, j)


def phase_out(nc, g, sem):
    ctx = ExitStack()
    with ctx:
        sb = lambda name, shape, dt=F32: ctx.enter_context(nc.sbuf_tensor(name, shape, dt))
        pb = lambda name, shape: ctx.enter_context(nc.psum_tensor(name, shape, F32))
        wo_raw = sb("c_wo_raw", [P, 2, D])
        wo_hi = sb("c_wo_hi", [P, KT, D], F32R)
        wo_lo = sb("c_wo_lo", [P, KT, D], F32R)
        x1 = sb("c_x1", [P, 2, D])
        xn = sb("c_xn", [P, D])
        tmp = sb("c_tmp", [P, KT, P])
        stat = sb("c_stat", [P, 3, TILES])
        p_x1 = pb("c_p_x1", [P, 2, D])
        p_xt = pb("c_p_xt", [P, KT, P])
        p_junk = pb("c_p_junk", [P, D])

        w_arr = [sem(f"c_w_arr{s}") for s in range(2)]
        x_arr = [sem(f"c_x_arr{s}") for s in range(2)]
        wo_hi_ready, wo_lo_ready = sem("c_wo_hi_ready"), sem("c_wo_lo_ready")
        mix_hi, mix_lo = sem("c_mix_hi"), sem("c_mix_lo")
        multiplied = sem("c_multiplied")
        added = sem("c_added")
        stored = [sem(f"c_stored{s}") for s in range(2)]
        squared, meaned, rooted, inverted = sem("c_squared"), sem("c_meaned"), sem("c_rooted"), sem("c_inverted")
        normed, turned, scaled = sem("c_normed"), sem("c_turned"), sem("c_scaled")
        hi_ready, lo_ready = sem("c_hi_ready"), sem("c_lo_ready")

        def rows_of(t):
            return g.x1_scr[0:HEAD_ROWS, :] if t == 0 else g.x1_scr[HEAD_ROWS + P * (t - 1):HEAD_ROWS + P * t, :]

        with nc.Block() as block:

            @block.sync
            def _(sp):
                def load_x(t):
                    if t >= 2:
                        sp.wait_ge(stored[t % 2], 16 * (t // 2))
                        sp.wait_ge(normed, t - 1)
                    if t == 0:
                        sp.dma_start(x1[0:DEC, 0, :], g.x_sample.rearrange("s o d -> (s o) d")).then_inc(x_arr[0], 16)
                        sp.dma_start(x1[DEC:HEAD_ROWS, 0, :], g.meta_tokens).then_inc(x_arr[0], 16)
                    else:
                        sp.dma_start(x1[:, t % 2, :], g.x_prompt[0, P * (t - 1):P * t, :]).then_inc(x_arr[t % 2], 16)

                for k in range(KT):
                    if k >= 2:
                        sp.wait_ge(wo_lo_ready, k - 1)
                    sp.dma_start(wo_raw[:, k % 2, :], g.w_out[0, P * k:P * (k + 1), :]).then_inc(w_arr[k % 2], 16)
                    if k == 1:
                        load_x(0)
                        load_x(1)
                for t in range(TILES):
                    _, nr = token_tile(t)
                    sp.wait_ge(added, t + 1)
                    sp.dma_start(rows_of(t), x1[0:nr, t % 2, :]).then_inc(stored[t % 2], 16)
                    if t + 2 < TILES:
                        load_x(t + 2)
                for n in range(2):
                    sp.wait_ge(stored[n], 16 * (5 - n))

            @block.gpsimd
            def _(pool):
                for k in range(KT):
                    pool.wait_ge(wo_hi_ready, k + 1)
                    pool.tensor_tensor(wo_lo[:, k, :], wo_raw[:, k % 2, :], wo_hi[:, k, :].bitcast(F32),
                                       ALU.subtract).then_inc(wo_lo_ready, 1)

            @block.scalar
            def _(act):
                for k in range(KT):
                    act.wait_ge(w_arr[k % 2], 16 * (k // 2 + 1))
                    act.activation(wo_hi[:, k, :], wo_raw[:, k % 2, :], ACT.Copy).then_inc(wo_hi_ready, 1)
                    act.activation(g.n_hi[:, k, 0:LAST], g.mix[:, k, 0:LAST], ACT.Copy, scale=0.5).then_inc(mix_hi, 1)
                for t in range(TILES):
                    c0, nr = token_tile(t)
                    act.wait_ge(added, t + 1)
                    if t:
                        act.wait_ge(squared, t)
                    act.activation(p_junk[0:nr, :], x1[0:nr, t % 2, :], ACT.Square,
                                   accum_out=stat[0:nr, 0, t:t + 1]).then_inc(squared, 1)
                    act.wait_ge(meaned, t + 1)
                    act.activation(stat[0:nr, 2, t:t + 1], stat[0:nr, 1, t:t + 1], ACT.Sqrt).then_inc(rooted, 1)
                    act.wait_ge(scaled, t + 1)
                    act.activation(g.n_hi[:, :, c0:c0 + nr], tmp[:, :, 0:nr], ACT.Copy).then_inc(hi_ready, 1)

            @block.vector
            def _(dve):
                for k in range(KT):
                    dve.wait_ge(mix_hi, k + 1)
                    dve.scalar_tensor_tensor(g.n_lo[:, k, 0:LAST], g.mix[:, k, 0:LAST], 0.5,
                                             g.n_hi[:, k, 0:LAST].bitcast(F32), ALU.mult,
                                             ALU.subtract).then_inc(mix_lo, 1)
                for t in range(TILES):
                    c0, nr = token_tile(t)
                    dve.wait_ge(multiplied, 2 * t + 2)
                    dve.wait_ge(x_arr[t % 2], 16 * (t // 2 + 1 + (t % 2 == 0)))
                    dve.tensor_tensor(x1[0:nr, t % 2, :], p_x1[0:nr, t % 2, :], x1[0:nr, t % 2, :],
                                      ALU.add).then_inc(added, 1)
                    dve.wait_ge(squared, t + 1)
                    dve.tensor_scalar(stat[0:nr, 1, t:t + 1], stat[0:nr, 0, t:t + 1], 1.0 / D, EPS,
                                      ALU.mult, ALU.add).then_inc(meaned, 1)
                    dve.wait_ge(rooted, t + 1)
                    dve.reciprocal(stat[0:nr, 2, t:t + 1], stat[0:nr, 2, t:t + 1]).then_inc(inverted, 1)
                    dve.wait_ge(inverted, t + 1)
                    if t:
                        dve.wait_ge(turned, t)
                    dve.tensor_scalar(xn[0:nr, :], x1[0:nr, t % 2, :], stat[0:nr, 2, t:t + 1], None,
                                      ALU.mult).then_inc(normed, 1)
                    dve.wait_ge(turned, t + 1)
                    if t:
                        dve.wait_ge(lo_ready, t)
                    dve.tensor_tensor(tmp[:, :, 0:nr], p_xt[:, :, 0:nr],
                                      g.par[:, :, R_GFFN:R_GFFN + 1].to_broadcast([P, KT, nr]),
                                      ALU.mult).then_inc(scaled, 1)
                    dve.wait_ge(hi_ready, t + 1)
                    dve.tensor_tensor(g.n_lo[:, :, c0:c0 + nr], tmp[:, :, 0:nr],
                                      g.n_hi[:, :, c0:c0 + nr].bitcast(F32), ALU.subtract).then_inc(lo_ready, 1)

            @block.tensor
            def _(pe):
                pe.wait_ge(mix_lo, KT)
                for t in range(TILES + 1):
                    if t < TILES:
                        c0, nr = token_tile(t)
                        if t >= 2:
                            pe.wait_ge(added, t - 1)
                        for half in range(2):
                            cols = slice(512 * half, 512 * (half + 1))
                            for k in range(KT):
                                if t == 0 and half == 0:
                                    pe.wait_ge(wo_lo_ready, k + 1)
                                for x, w in ((g.n_hi, wo_hi), (g.n_hi, wo_lo), (g.n_lo, wo_hi)):
                                    last = pe.matmul(p_x1[0:nr, t % 2, cols], x[:, k, c0:c0 + nr], w[:, k, cols],
                                                     start=(k == 0 and x is g.n_hi and w is wo_hi),
                                                     stop=(k == KT - 1 and x is g.n_lo))
                            last.then_inc(multiplied, 1)
                    if t:
                        _, nr = token_tile(t - 1)
                        pe.wait_ge(normed, t)
                        if t >= 2:
                            pe.wait_ge(scaled, t - 1)
                        for k in range(KT):
                            last = pe.transpose(p_xt[:, k, 0:nr], xn[0:nr, P * k:P * (k + 1)], g.ident[0:nr, 0:nr])
                        last.then_inc(turned, 1)


FPAIR = 2
TURNS = FT // FPAIR
UPC = 2 * FPAIR * CHUNKS
DOWNC = KT * CHUNKS


def phase_ffn(nc, g, sem):
    ctx = ExitStack()
    with ctx:
        sb = lambda name, shape, dt=F32: ctx.enter_context(nc.sbuf_tensor(name, shape, dt))
        pb = lambda name, shape: ctx.enter_context(nc.psum_tensor(name, shape, F32))
        y = g.mix
        w_raw = sb("d_w_raw", [P, 2, KT, P])
        w_hi = sb("d_w_hi", [P, 2, KT, P], F32R)
        w_lo = sb("d_w_lo", [P, 2, KT, P], F32R)
        wd_hi = sb("d_wd_hi", [P, FPAIR, D], F32R)
        wd_lo = sb("d_wd_lo", [P, FPAIR, D], F32R)
        up = sb("d_up", [P, 2, COLS])
        cv = sb("d_cv", [P, 2, COLS])
        prod = sb("d_prod", [P, FPAIR, COLS])
        a_hi = sb("d_a_hi", [P, FPAIR, COLS], F32R)
        a_lo = sb("d_a_lo", [P, FPAIR, COLS], F32R)
        fp = sb("d_fp", [P, F_ROWS])
        fpar = sb("d_fpar", [P, 2 * FT, F_ROWS])
        p_up = pb("d_p_up", [P, 2, 512])
        p_down = pb("d_p_down", [P, 4, 512])
        p_par = pb("d_p_par", [P, 2, 512])

        w_arr = [sem(f"d_w_arr{s}") for s in range(2)]
        par_arr = sem("d_par_arr")
        par_turned, par_out = sem("d_par_turned"), sem("d_par_out")
        inits = sem("d_inits")
        hi_up, hi_down = sem("d_hi_up"), sem("d_hi_down")
        lo_ready = sem("d_lo_ready")
        up_done = sem("d_up_done")
        up_out = sem("d_up_out")
        conv_done = sem("d_conv_done")
        gelu_done = sem("d_gelu_done")
        prod_done = sem("d_prod_done")
        a_hi_ready, a_lo_ready = sem("d_a_hi_ready"), sem("d_a_lo_ready")
        down_done = sem("d_down_done")
        down_out = sem("d_down_out")
        dve_step = sem("d_dve_step")

        up_view = g.w_up.rearrange("o (k p) c -> p (o k) c", p=P)
        pieces = [up[0:F_ROWS, 0, :], up[0:F_ROWS, 1, :], cv[0:F_ROWS, 0, :], cv[0:F_ROWS, 1, :],
                  prod[0:F_ROWS, 0, :], prod[0:F_ROWS, 1, :]]

        def up_col(i, u):
            return i * (FPAIR * P) + (P * (u // 2) + (DFF if u % 2 else 0))

        with nc.Block() as block:

            @block.sync
            def _(sp):
                def load_up(slot, index, i, u):
                    sp.wait_ge(lo_ready, index)
                    sp.dma_start(w_raw[:, slot, :, :], up_view[:, :, bass.ds(up_col(i, u), P)]).then_inc(w_arr[slot], 16)

                def load_down(slot, index, i, n):
                    sp.wait_ge(lo_ready, index)
                    sp.dma_start(w_raw[:, slot, :, :].rearrange("p k c -> p (k c)"),
                                 g.w_down[0, bass.ds(i * (FPAIR * P) + P * n, P), :]).then_inc(w_arr[slot], 16)

                load_up(0, 1, 0, 0)
                for n, piece in enumerate(pieces):
                    c0, c1 = D * n, min(D * (n + 1), 2 * DFF)
                    for r, rows in ((F_STATE, g.state_ffn_conv.rearrange("o s j c -> (o s j) c")),
                                    (F_W, g.w_ffn_conv[0]), (F_B, g.b_ffn_conv)):
                        nrow = rows.shape[0]
                        sp.dma_start(piece[r:r + nrow, 0:c1 - c0], rows[:, c0:c1]).then_inc(par_arr, 16)
                for n in (1, 2, 3):
                    load_up(n % 2, n + 1, 0, n)
                load_up(0, 5, 1, 0)
                with sp.Fori(0, TURNS - 1, 1) as m:
                    for n in (1, 2, 3):
                        load_up(n % 2, nth(m, 6, n + 4), m + 1, n)
                    load_down(0, nth(m, 6, 8), m, 0)
                    load_down(1, nth(m, 6, 9), m, 1)
                    load_up(0, nth(m, 6, 10), m + 2, 0)
                load_down(1, 6 * (TURNS - 1) + 6, TURNS - 1, 0)
                load_down(0, 6 * (TURNS - 1) + 7, TURNS - 1, 1)

            @block.gpsimd
            def _(pool):
                pool.sem_inc(lo_ready, 2)
                pool.memset(y[:, 0:KT, :], 0.0).then_inc(inits, 1)

                def low_up(slot, index, raw):
                    pool.wait_ge(hi_up, index)
                    pool.tensor_tensor(w_lo[:, slot, :, :], w_raw[:, raw, :, :],
                                       w_hi[:, slot, :, :].bitcast(F32), ALU.subtract).then_inc(lo_ready, 1)

                def low_down(n, index, raw):
                    pool.wait_ge(hi_down, index)
                    pool.tensor_tensor(wd_lo[:, n, :], w_raw[:, raw, :, :].rearrange("p k c -> p (k c)"),
                                       wd_hi[:, n, :].bitcast(F32), ALU.subtract).then_inc(lo_ready, 1)

                for n in range(5):
                    low_up(n % 2, n + 1, n % 2)
                with pool.Fori(0, TURNS - 1, 1) as m:
                    for n in (1, 2, 3):
                        low_up(n % 2, nth(m, 4, n + 4), n % 2)
                    low_down(0, nth(m, 2, 0), 0)
                    low_down(1, nth(m, 2, 1), 1)
                    low_up(0, nth(m, 4, 8), 0)
                low_down(0, 2 * TURNS - 1, 1)
                low_down(1, 2 * TURNS, 0)

            @block.scalar
            def _(act):
                act.sem_inc(up_out, 2)

                def high_up(slot, chunks, raw, turns):
                    act.wait_ge(w_arr[raw], turns)
                    act.wait_ge(up_done, chunks)
                    act.activation(w_hi[:, slot, :, :], w_raw[:, raw, :, :], ACT.Copy).then_inc(hi_up, 1)

                def high_down(n, chunks, raw, turns):
                    act.wait_ge(w_arr[raw], turns)
                    act.wait_ge(down_done, chunks)
                    act.activation(wd_hi[:, n, :], w_raw[:, raw, :, :].rearrange("p k c -> p (k c)"),
                                   ACT.Copy).then_inc(hi_down, 1)

                def up_tile(i, u):
                    act.wait_ge(conv_done, nth(i, 4, u))
                    for c in range(CHUNKS):
                        n = CHUNKS * u + c
                        act.wait_ge(up_done, nth(i, UPC, n, 6))
                        act.activation(up[:, u % 2, CW * c:CW * (c + 1)], p_up[:, n % 2, 0:CW],
                                       ACT.Copy).then_inc(up_out, 1)

                def gelu(i, n):
                    act.wait_ge(conv_done, nth(i, 4, 2 * n, 2))
                    act.activation(cv[:, 0, 0:LAST], cv[:, 0, 0:LAST], ACT.Gelu_apprx_tanh).then_inc(gelu_done, 1)

                def high_a(i):
                    for n in range(FPAIR):
                        act.wait_ge(prod_done, nth(i, FPAIR, n))
                        act.activation(a_hi[:, n, 0:LAST], prod[:, n, 0:LAST], ACT.Copy).then_inc(a_hi_ready, 1)

                high_up(0, 3, 0, 16)
                act.wait_ge(par_out, 2)
                high_up(1, 6, 1, 16)
                for u in range(4):
                    up_tile(0, u)
                    slot = u % 2
                    high_up(slot, 3 * (u + 1) + 6, slot, 16 * (u // 2 + 2)) if u < 3 else None
                    if u % 2 == 0:
                        gelu(0, u // 2)
                with act.Fori(0, TURNS - 1, 1) as m:
                    i = m + 1
                    act.wait_ge(down_done, nth(m, DOWNC, DOWNC - 1))
                    act.wait_ge(prod_done, nth(m, FPAIR, 1, 2))
                    high_up(1, nth(i, UPC, -1, 6), 1, 16 * nth(m, 3, 2))
                    for n in range(FPAIR):
                        act.activation(a_hi[:, n, 0:LAST], prod[:, n, 0:LAST], ACT.Copy).then_inc(a_hi_ready, 1)
                    up_tile(i, 0)
                    high_up(0, nth(i, UPC, 2, 6), 0, 16 * nth(m, 3, 3))
                    gelu(i, 0)
                    up_tile(i, 1)
                    high_up(1, nth(i, UPC, 5, 6), 1, 16 * nth(m, 3, 3))
                    up_tile(i, 2)
                    high_down(0, nth(m, DOWNC, DOWNC - 1), 0, 16 * nth(m, 3, 4))
                    gelu(i, 1)
                    high_down(1, nth(m, DOWNC, DOWNC - 1), 1, 16 * nth(m, 3, 4))
                    up_tile(i, 3)
                    high_up(0, nth(i, UPC, 8, 6), 0, 16 * nth(m, 3, 5))
                act.wait_ge(prod_done, 2 * TURNS + 2)
                act.wait_ge(down_done, DOWNC * TURNS)
                for n in range(FPAIR):
                    act.activation(a_hi[:, n, 0:LAST], prod[:, n, 0:LAST], ACT.Copy).then_inc(a_hi_ready, 1)
                high_down(0, DOWNC * TURNS, 1, 16 * (3 * TURNS))
                high_down(1, DOWNC * TURNS, 0, 16 * (3 * TURNS + 1))

            @block.vector
            def _(dve):
                own = Chain(dve, dve_step)
                for s, n in ((conv_done, 2), (down_out, 4), (prod_done, 2)):
                    dve.sem_inc(s, n)
                CONV = 7

                def conv(i, u):
                    x, c = up[:, u % 2, :], cv[:, u % 2, :]
                    tile = i * FPAIR + (u // 2 + (FT if u % 2 else 0))
                    dve.wait_ge(up_out, nth(i, UPC, CHUNKS * u + 2, 2))
                    par = fpar[:, bass.ds(tile, 1), :].rearrange("p a r -> p (a r)")
                    own.step(dve.tensor_copy(fp[:, :], par))
                    cw = lambda j: fp[:, F_W + j:F_W + j + 1]
                    cb = fp[:, F_B:F_B + 1]
                    here = g.u_out[:, bass.ds(tile, 1), :].rearrange("p a r -> p (a r)")
                    dve.tensor_copy(here[:, 0:DEC], x[:, 0:DEC])
                    dve.tensor_copy(here[:, DEC:DEC + 2], x[:, LAST - 2:LAST])
                    own.step(dve.tensor_scalar(c[:, 0:DEC], x[:, 0:DEC], cw(2), cb, ALU.mult, ALU.add))
                    for j in range(2):
                        own.step(dve.scalar_tensor_tensor(c[:, 0:DEC], fp[:, F_STATE + j:F_STATE + 16:2], cw(j),
                                                          c[:, 0:DEC], ALU.mult, ALU.add))
                    own.step(dve.memset(x[:, FIRST - 2:FIRST], 0.0))
                    own.step(dve.tensor_scalar(c[:, FIRST:LAST], x[:, FIRST:LAST], cw(2), cb, ALU.mult, ALU.add))
                    own.step(dve.scalar_tensor_tensor(c[:, FIRST:LAST], x[:, FIRST - 1:LAST - 1], cw(1),
                                                      c[:, FIRST:LAST], ALU.mult, ALU.add))
                    dve.scalar_tensor_tensor(c[:, FIRST:LAST], x[:, FIRST - 2:LAST - 2], cw(0),
                                             c[:, FIRST:LAST], ALU.mult, ALU.add).then_inc(conv_done, 1)

                def gated(i, n):
                    dve.wait_ge(gelu_done, nth(i, FPAIR, n))
                    dve.wait_ge(conv_done, nth(i, 4, 2 * n + 1, 2))
                    dve.tensor_tensor(prod[:, n, 0:LAST], cv[:, 0, 0:LAST], cv[:, 1, 0:LAST],
                                      ALU.mult).then_inc(prod_done, 1)
                    dve.wait_ge(prod_done, nth(i, FPAIR, n, 2))

                def low_a(m):
                    for n in range(FPAIR):
                        dve.wait_ge(a_hi_ready, nth(m, FPAIR, n))
                        dve.tensor_tensor(a_lo[:, n, 0:LAST], prod[:, n, 0:LAST], a_hi[:, n, 0:LAST].bitcast(F32),
                                          ALU.subtract).then_inc(a_lo_ready, 1)
                    dve.wait_ge(a_lo_ready, nth(m, FPAIR, 1, 1))

                def add_down(m):
                    for n in range(DOWNC):
                        tile, c = n // CHUNKS, n % CHUNKS
                        to = y[:, tile, CW * c:CW * (c + 1)]
                        dve.wait_ge(down_done, nth(m, DOWNC, n, DOWNC))
                        dve.tensor_tensor(to, to, p_down[:, n % 4, 0:CW], ALU.add).then_inc(down_out, 1)

                for half in range(2):
                    dve.wait_ge(par_turned, half + 1)
                    dve.tensor_copy(fpar[:, FT * half:FT * (half + 1), :].rearrange("p t r -> p (t r)"),
                                    p_par[:, half, 0:FT * F_ROWS]).then_inc(par_out, 1)
                dve.wait_ge(par_out, 2)
                dve.memset(a_hi[:, :, LAST:COLS].bitcast(F32), 0.0).then_inc(a_lo_ready, 1)
                dve.memset(a_lo[:, :, LAST:COLS].bitcast(F32), 0.0)
                dve.wait_ge(inits, 1)
                for u in range(4):
                    conv(0, u)
                    if u % 2:
                        gated(0, u // 2)
                with dve.Fori(0, TURNS - 1, 1) as m:
                    own.turn(4 * CONV, m, 4 * CONV)
                    low_a(m)
                    for u in range(4):
                        conv(m + 1, u)
                        if u % 2:
                            gated(m + 1, u // 2)
                    assert own.n == 4 * CONV, own.n
                    add_down(m)
                low_a(TURNS - 1)
                add_down(TURNS - 1)

            @block.tensor
            def _(pe):
                for s, n in ((up_done, 6), (down_done, DOWNC)):
                    pe.sem_inc(s, n)
                pe.wait_ge(par_arr, 16 * 18)
                for half in range(2):
                    for n in range(FT):
                        t = FT * half + n
                        last = pe.transpose(p_par[:, half, F_ROWS * n:F_ROWS * (n + 1)],
                                            pieces[t // KT][:, P * (t % KT):P * (t % KT + 1)],
                                            g.ident[0:F_ROWS, 0:F_ROWS])
                    last.then_inc(par_turned, 1)

                def up_tiles(i, split):
                    for u in range(4):
                        pe.wait_ge(lo_ready, split(u))
                        for c in range(CHUNKS):
                            n = CHUNKS * u + c
                            pe.wait_ge(up_out, nth(i, UPC, n))
                            project(pe, p_up[:, n % 2, 0:CW], w_hi[:, u % 2], w_lo[:, u % 2],
                                    g.n_hi, g.n_lo, CW * c).then_inc(up_done, 1)

                def down(m, split):
                    pe.wait_ge(lo_ready, split)
                    pe.wait_ge(a_lo_ready, nth(m, FPAIR, 1, 1))
                    for n in range(DOWNC):
                        tile, c = n // CHUNKS, n % CHUNKS
                        pe.wait_ge(down_out, nth(m, DOWNC, n))
                        for k in range(FPAIR):
                            for w, a in ((wd_hi, a_hi), (wd_hi, a_lo), (wd_lo, a_hi)):
                                last = pe.matmul(p_down[:, n % 4, 0:CW], w[:, k, P * tile:P * (tile + 1)],
                                                 a[:, k, CW * c:CW * (c + 1)],
                                                 start=(k == 0 and w is wd_hi and a is a_hi),
                                                 stop=(k == FPAIR - 1 and w is wd_lo))
                        last.then_inc(down_done, 1)

                up_tiles(0, lambda u: 2 + u + 1)
                with pe.Fori(0, TURNS - 1, 1) as m:
                    up_tiles(m + 1, lambda u: nth(m, 6, 4 + u, 2))
                    down(m, nth(m, 6, 9, 2))
                down(TURNS - 1, 2 + 5 + 6 * (TURNS - 1) + 2)


def phase_last(nc, g, sem):
    ctx = ExitStack()
    with ctx:
        sb = lambda name, shape, dt=F32: ctx.enter_context(nc.sbuf_tensor(name, shape, dt))
        pb = lambda name, shape: ctx.enter_context(nc.psum_tensor(name, shape, F32))
        x1 = sb("e_x1", [P, TILES, D])
        g_last = sb("e_g_last", [P, D])
        out = sb("e_out", [P, 2, D])
        stat = sb("e_stat", [P, 3, TILES])
        junk = sb("e_junk", [P, 2, D])
        u_rows = sb("e_u_rows", [DEC + 2, 2 * DFF])
        x_rows = sb("e_x_rows", [DEC + 3, D])
        h_rows = sb("e_h_rows", [DEC + 1, D])
        p_y = pb("e_p_y", [P, 2, D])
        p_rows = pb("e_p_rows", [P, 4, 512])

        x_arr = [sem(f"e_x_arr{t}") for t in range(TILES)]
        g_arr = sem("e_g_arr")
        turned, added, squared, meaned = sem("e_turned"), sem("e_added"), sem("e_squared"), sem("e_meaned")
        rooted, inverted, made = sem("e_rooted"), sem("e_inverted"), sem("e_made")
        stored = [sem(f"e_stored{s}") for s in range(2)]
        rows_turned, rows_out, rows_stored = sem("e_rows_turned"), sem("e_rows_out"), sem("e_rows_stored")

        kept = [(g.u_out, t, u_rows) for t in range(0, 2 * FT, 4)] + \
               [(g.x_out, t, x_rows) for t in (0, 4)] + [(g.h_out, t, h_rows) for t in (0, 4)]

        with nc.Block() as block:

            @block.sync
            def _(sp):
                for t in range(TILES):
                    c0, nr = token_tile(t)
                    sp.dma_start(x1[0:nr, t, :], g.x1_scr[c0:c0 + nr, :]).then_inc(x_arr[t], 16)
                    if t == 0:
                        sp.dma_start(g_last[:, :], g.g_final.partition_broadcast(P)).then_inc(g_arr, 16)
                for t in range(TILES):
                    sp.wait_ge(made, t + 1)
                    if t == 0:
                        sp.dma_start(g.y_sample.rearrange("s o d -> (s o) d"), out[0:DEC, 0, :]).then_inc(stored[0], 16)
                    else:
                        sp.dma_start(g.y_prompt[0, P * (t - 1):P * t, :], out[:, t % 2, :]).then_inc(stored[t % 2], 16)
                sp.wait_ge(rows_out, len(kept))
                for to, rows in ((g.prompt_ffn_conv[0, 0], u_rows[DEC:DEC + 2, :]),
                                 (g.sample_ffn_conv[0, :, 1, :], u_rows[0:DEC, :]),
                                 (g.prompt_rnn_conv[0, 0], x_rows[DEC:DEC + 3, :]),
                                 (g.sample_rnn_conv[0, :, 2, :], x_rows[0:DEC, :]),
                                 (g.prompt_rnn_h[0], h_rows[DEC:DEC + 1, :]),
                                 (g.sample_rnn_h[0], h_rows[0:DEC, :])):
                    sp.dma_start(to, rows).then_inc(rows_stored, 16)
                sp.wait_ge(rows_stored, 16 * 6)
                for n in range(2):
                    sp.wait_ge(stored[n], 16 * (5 - n))

            @block.scalar
            def _(act):
                def rows(n):
                    src, t, to = kept[n]
                    act.wait_ge(rows_turned, n + 1)
                    act.activation(to[:, P * t:P * (t + 4)], p_rows[0:to.shape[0], n % 4, :],
                                   ACT.Copy).then_inc(rows_out, 1)

                for t in range(TILES):
                    _, nr = token_tile(t)
                    act.wait_ge(added, t + 1)
                    if t >= 2:
                        act.wait_ge(squared, t - 1)
                    act.activation(junk[0:nr, t % 2, :], x1[0:nr, t, :], ACT.Square,
                                   accum_out=stat[0:nr, 0, t:t + 1]).then_inc(squared, 1)
                    act.wait_ge(meaned, t + 1)
                    act.activation(stat[0:nr, 2, t:t + 1], stat[0:nr, 1, t:t + 1], ACT.Sqrt).then_inc(rooted, 1)
                for n in range(len(kept)):
                    rows(n)

            @block.vector
            def _(dve):
                for t in range(TILES + 1):
                    if t < TILES:
                        _, nr = token_tile(t)
                        dve.wait_ge(turned, t + 1)
                        dve.wait_ge(x_arr[t], 16)
                        dve.tensor_tensor(x1[0:nr, t, :], p_y[0:nr, t % 2, :], x1[0:nr, t, :],
                                          ALU.add).then_inc(added, 1)
                    if t:
                        u = t - 1
                        _, nr = token_tile(u)
                        dve.wait_ge(squared, u + 1)
                        dve.tensor_scalar(stat[0:nr, 1, u:u + 1], stat[0:nr, 0, u:u + 1], 1.0 / D, EPS,
                                          ALU.mult, ALU.add).then_inc(meaned, 1)
                        dve.wait_ge(rooted, u + 1)
                        dve.reciprocal(stat[0:nr, 2, u:u + 1], stat[0:nr, 2, u:u + 1]).then_inc(inverted, 1)
                        dve.wait_ge(inverted, u + 1)
                        if u == 0:
                            dve.wait_ge(g_arr, 16)
                        if u >= 2:
                            dve.wait_ge(stored[u % 2], 16 * (u // 2))
                        dve.scalar_tensor_tensor(out[0:nr, u % 2, :], x1[0:nr, u, :], stat[0:nr, 2, u:u + 1],
                                                 g_last[0:nr, :], ALU.mult, ALU.mult).then_inc(made, 1)

            @block.tensor
            def _(pe):
                for t in range(TILES):
                    c0, nr = token_tile(t)
                    if t >= 2:
                        pe.wait_ge(added, t - 1)
                    for k in range(KT):
                        last = pe.transpose(p_y[0:nr, t % 2, P * k:P * (k + 1)], g.mix[:, k, c0:c0 + nr],
                                            g.ident[:, :])
                    last.then_inc(turned, 1)
                for n, (src, t, to) in enumerate(kept):
                    if n >= 4:
                        pe.wait_ge(rows_out, n - 3)
                    for r in range(4):
                        last = pe.transpose(p_rows[0:to.shape[0], n % 4, P * r:P * (r + 1)], src[:, t + r, :],
                                            g.ident[:, :])
                    last.then_inc(rows_turned, 1)


class Shared:

    def __init__(self, ins, outs):
        (self.x_prompt, self.x_sample, self.cache_k, self.cache_v, self.page_table, self.state_rnn_h,
         self.state_rnn_conv, self.state_ffn_conv, self.meta_tokens, self.g_mix, self.w_in, self.sb_bias,
         self.w_rnn_conv, self.b_rnn_conv, self.w_rgate, self.b_rgate, self.w_igate, self.b_igate,
         self.rglru_lambda, self.w_out, self.g_ffn, self.w_up, self.w_ffn_conv, self.b_ffn_conv,
         self.w_down, self.g_final) = (ins[name] for name in _INS)
        (self.y_prompt, self.y_sample, self.prompt_k, self.prompt_v, self.prompt_rnn_h, self.prompt_rnn_conv,
         self.prompt_ffn_conv, self.sample_k, self.sample_v, self.sample_rnn_h, self.sample_rnn_conv,
         self.sample_ffn_conv) = (outs[name] for name, _ in _OUTS)


def hybrid_step(nc, a, o):
    ctx = ExitStack()
    with ctx:
        sb = lambda name, shape, dt=F32: ctx.enter_context(nc.sbuf_tensor(name, shape, dt))
        sem = lambda name: ctx.enter_context(nc.semaphore(name))
        g = Shared(a, o)
        g.n_hi = sb("n_hi", [P, KT, COLS], F32R)
        g.n_lo = sb("n_lo", [P, KT, COLS], F32R)
        g.mix = sb("mix", [P, KT + 1, COLS])
        g.ident = sb("ident", [P, P])
        g.tri = sb("tri", [P, P])
        g.ones = sb("ones", [P, P])
        g.par = sb("par", [P, KT, N_ROWS])
        g.rates = sb("rates", [P, 4, KT])
        g.bias_all = sb("bias_all", [P, HEADS])
        g.q_dec = sb("q_dec", [P, KT, DEC])
        g.q_block = sb("q_block", [P, 2, DEC, 8])
        g.table = sb("table", [1, PAGES + DEC * PAGES], I32)
        g.page_mask = sb("page_mask", [P, HEADS, PAGES + 1])
        g.x_out = sb("x_out", [P, KT, DEC + 3])
        g.h_out = sb("h_out", [P, KT, DEC + 1])
        g.att_dec = sb("att_dec", [P, KT, DEC + 1])
        g.gate_dec = sb("gate_dec", [P, KT, DEC])
        g.q_scr = nc.dram_tensor("q_scr", (HEADS, HD + 1, PROMPT), F32).ap()
        g.k_scr = nc.dram_tensor("k_scr", (KVH, HD, PROMPT), F32).ap()
        g.x1_scr = nc.dram_tensor("x1_scr", (HEAD_ROWS + SEQ, D), F32).ap()
        g.v_scr = nc.dram_tensor("v_scr", (PROMPT, KVH * HD), F32).ap()
        phase_qkv(nc, g, sem)
        phase_mix(nc, g, sem)
        phase_out(nc, g, sem)
        g.u_out = sb("u_out", [P, 2 * FT, DEC + 2])
        phase_ffn(nc, g, sem)
        phase_last(nc, g, sem)


_INS = ['x_prompt', 'x_sample', 'cache_k', 'cache_v', 'page_table', 'state_rnn_h', 'state_rnn_conv',
        'state_ffn_conv', 'meta_tokens', 'g_mix', 'w_in', 'sb_bias', 'w_rnn_conv', 'b_rnn_conv', 'w_rgate',
        'b_rgate', 'w_igate', 'b_igate', 'rglru_lambda', 'w_out', 'g_ffn', 'w_up', 'w_ffn_conv', 'b_ffn_conv',
        'w_down', 'g_final']
_OUTS = [('y_prompt', (1, SEQ, D)), ('y_sample', (DEC, 1, D)),
         ('prompt_k', (1, 1, PROMPT, KVH, HD)), ('prompt_v', (1, 1, PROMPT, KVH, HD)),
         ('prompt_rnn_h', (1, 1, D)), ('prompt_rnn_conv', (1, 1, 3, D)), ('prompt_ffn_conv', (1, 1, 2, 2 * DFF)),
         ('sample_k', (1, DEC, 1, KVH, HD)), ('sample_v', (1, DEC, 1, KVH, HD)),
         ('sample_rnn_h', (1, DEC, D)), ('sample_rnn_conv', (1, DEC, 3, D)),
         ('sample_ffn_conv', (1, DEC, 2, 2 * DFF))]


def kernel(**inputs):
    import numpy as np
    import concourse.bacc as bacc
    from concourse.bass_utils import run_bass_kernel_spmd

    nc = bacc.Bacc("TRN2", target_bir_lowering=False, num_devices=1)
    arrays, ins, outs = {}, {}, {}
    for name in _INS:
        x = np.ascontiguousarray(inputs[name])
        arrays[f"in_{name}"] = x
        ins[name] = nc.dram_tensor(f"in_{name}", x.shape, mybir.dt.from_np(x.dtype), kind="ExternalInput").ap()
    for name, shape in _OUTS:
        outs[name] = nc.dram_tensor(f"out_{name}", shape, F32, kind="ExternalOutput").ap()
    hybrid_step(nc, ins, outs)
    r = run_bass_kernel_spmd(nc, [arrays], core_ids=[0])
    return tuple(r.results[0][f"out_{name}"] for name, _ in _OUTS)
```

```python
import concourse.bass as bass
from concourse import mybir
from contextlib import ExitStack

F32, F32R, BF16, I32 = mybir.dt.float32, mybir.dt.float32r, mybir.dt.bfloat16, mybir.dt.int32
ALU, ACT = mybir.AluOpType, mybir.ActivationFunctionType

P = 128
D = 1024
KT = D // P
SEQ, META, DEC = 1024, 16, 8
HD, HEADS, KVH = 64, 16, 4
PROMPT = META + SEQ
FIRST = DEC
LAST = DEC + PROMPT
COLS = 1050
CHUNKS = 3
CW = COLS // CHUNKS
TILES = 9
HEAD_ROWS = DEC + META
K_COL, V_COL, XR_COL, GR_COL, GA_COL, GB_COL = 1024, 1280, 1536, 2560, 3584, 4608
DFF = 2816
FT = DFF // P
EPS = 1e-6
PAGES, PAGE, N_PHYS = 16, 128, 160

R_CONVSTATE, R_H0, R_CONVW, R_CONVB, R_BR, R_BI, R_LAM, R_GMIX, R_GFFN, N_ROWS = 0, 24, 32, 36, 37, 38, 39, 40, 41, 42
F_STATE, F_W, F_B, F_ROWS = 0, 16, 19, 20


def token_tile(t):
    return (0, HEAD_ROWS) if t == 0 else (HEAD_ROWS + P * (t - 1), P)


def tiles_for_chunk(c):
    return next(t + 1 for t in range(TILES) if t == TILES - 1 or sum(token_tile(t)) >= CW * (c + 1))


def nth(turn, per_turn, index, credit=0):
    return turn * per_turn + (index + 1 + credit)


class Chain:

    def __init__(self, eng, sem):
        self.eng, self.sem, self.base, self.n = eng, sem, 0, 0

    def turn(self, base, i, per_turn):
        self.base, self.n = base + i * per_turn, 0

    def mark(self, ins):
        ins.then_inc(self.sem, 1)
        self.n += 1

    def step(self, ins):
        self.mark(ins)
        self.eng.wait_ge(self.sem, self.base + self.n)


def project(pe, out, w_hi, w_lo, x_hi, x_lo, col):
    return project_part(pe, out, w_hi, w_lo, x_hi, x_lo, col, 0, KT)


def project_part(pe, out, w_hi, w_lo, x_hi, x_lo, col, k0, k1):
    last = None
    for k in range(k0, k1):
        for w, x in ((w_hi, x_hi), (w_hi, x_lo), (w_lo, x_hi)):
            last = pe.matmul(out, w[:, k, :], x[:, k, col:col + CW],
                             start=(k == 0 and w is w_hi and x is x_hi), stop=(k == KT - 1 and w is w_lo))
    return last


def phase_qkv(nc, g, sem):
    ctx = ExitStack()
    with ctx:
        sb = lambda name, shape, dt=F32: ctx.enter_context(nc.sbuf_tensor(name, shape, dt))
        pb = lambda name, shape: ctx.enter_context(nc.psum_tensor(name, shape, F32))
        w_raw = g.w_raw
        w_hi = sb("a_w_hi", [P, 2, KT, P], F32R)
        w_lo = sb("a_w_lo", [P, 2, KT, P], F32R)
        x_tok = g.mix[:, :, :].rearrange("p a b -> p (a b)")[:, 0:TILES * D].rearrange("p (t d) -> p t d", d=D)
        rows = sb("a_rows", [N_ROWS, D])
        bias_col = sb("a_bias_col", [HEADS, 1])
        bias_rows = sb("a_bias_rows", [HEADS, PROMPT])
        junk = sb("a_junk", [P, 2, D])
        tmp = sb("a_tmp", [P, 2, KT, P])
        stat = sb("a_stat", [P, 3, TILES])
        q_stage = sb("a_q_stage", [P, 2, COLS])
        kv_ch = sb("a_kv_ch", [P, 4, COLS])
        kv_tok = sb("a_kv_tok", [P, 2, 4 * P])
        lam = sb("a_lam", [P, 6, KT])
        proj = pb("a_proj", [P, 2, 512])
        xt = pb("a_xt", [P, 2, KT, P])
        pt = pb("a_pt", [P, 512])
        kvt = xt[:, :, :, :].rearrange("p a b c -> p a (b c)")

        rows_in = sem("a_rows_in")
        bias_in = sem("a_bias_in")
        x_in = [sem(f"a_x_in{t}") for t in range(TILES)]
        w_in = [sem(f"a_w_in{s}") for s in range(2)]
        consts = sem("a_consts")
        rows_t = sem("a_rows_t")
        params = sem("a_params")
        squared = sem("a_squared")
        meaned = sem("a_meaned")
        rooted = sem("a_rooted")
        normed = sem("a_normed")
        x_turned = sem("a_x_turned")
        scaled = sem("a_scaled")
        hi_ready = sem("a_hi_ready")
        lo_ready = sem("a_lo_ready")
        w_hi_ready = sem("a_w_hi_ready")
        w_lo_ready = sem("a_w_lo_ready")
        proj_done = sem("a_proj_done")
        proj_out = sem("a_proj_out")
        q_cols = sem("a_q_cols")
        q_stored = [sem(f"a_q_stored{s}") for s in range(2)]
        k_stored = sem("a_k_stored")
        bias_made = sem("a_bias_made")
        kv_turned = sem("a_kv_turned")
        kv_out = sem("a_kv_out")
        kv_stored = [sem(f"a_kv_stored{s}") for s in range(2)]
        dve_step = sem("a_dve_step")
        act_step = sem("a_act_step")
        lam_exp = sem("a_lam_exp")
        q_block0 = sem("a_q_block0")
        old_rows = sem("a_old_rows")

        w_view = g.w_in.rearrange("o (k p) c -> p (o k) c", p=P)

        with nc.Block() as block:

            @block.sync
            def _(sp):
                def load_w(slot, index, col):
                    sp.wait_ge(w_lo_ready, index)
                    sp.dma_start(w_raw[:, slot, :, :], w_view[:, :, bass.ds(col, P)]).then_inc(w_in[slot], 16)

                sp.sem_inc(q_stored[0], 32)
                sp.sem_inc(q_stored[1], 32)
                for r, n, src in ((R_CONVSTATE, 24, g.state_rnn_conv.rearrange("o s j d -> (o s j) d")),
                                  (R_H0, 8, g.state_rnn_h[0]), (R_CONVW, 4, g.w_rnn_conv[0]),
                                  (R_CONVB, 1, g.b_rnn_conv), (R_BR, 1, g.b_rgate), (R_BI, 1, g.b_igate),
                                  (R_LAM, 1, g.rglru_lambda), (R_GMIX, 1, g.g_mix), (R_GFFN, 1, g.g_ffn)):
                    sp.dma_start(rows[r:r + n, :], src).then_inc(rows_in, 16)
                sp.dma_start(x_tok[0:DEC, 0, :], g.x_sample.rearrange("s o d -> (s o) d")).then_inc(x_in[0], 16)
                sp.dma_start(x_tok[DEC:HEAD_ROWS, 0, :], g.meta_tokens).then_inc(x_in[0], 16)
                for t in range(1, TILES):
                    sp.dma_start(x_tok[:, t, :], g.x_prompt[0, P * (t - 1):P * t, :]).then_inc(x_in[t], 16)
                    if t == 4:
                        load_w(0, 1, 0)
                load_w(1, 2, P)
                sp.dma_start(bias_col[:, :], g.sb_bias.rearrange("o h -> h o")).then_inc(bias_in, 16)
                sp.dma_start(g.bias_all[:, :], g.sb_bias[0, :].partition_broadcast(P)).then_inc(bias_in, 16)
                sp.dma_start(g.table[:, :],
                             g.page_table.rearrange("(o a) b -> o (a b)", o=1)).then_inc(bias_in, 16)
                sp.dma_start(g.sample_rnn_conv[0, :, 0:2, :], g.state_rnn_conv[0, :, 1:3, :]).then_inc(old_rows, 16)
                sp.dma_start(g.sample_ffn_conv[0, :, 0:1, :], g.state_ffn_conv[0, :, 1:2, :]).then_inc(old_rows, 16)
                sp.wait_ge(bias_made, 1)
                sp.dma_start(g.q_scr[:, HD, :], bias_rows[:, :]).then_inc(k_stored, 16)
                with sp.Fori(0, KT // 2, 1) as i:
                    for s in range(2):
                        load_w(s, nth(i, 2, s) + 2, i * (2 * P) + (2 + s) * P)
                        sp.wait_ge(q_cols, nth(i, 2, s))
                        for h in range(2):
                            sp.dma_start(g.q_scr[bass.ds(i * 4 + 2 * s + h, 1), 0:HD, :].rearrange("a p c -> p (a c)"),
                                         q_stage[HD * h:HD * (h + 1), s, FIRST:LAST]).then_inc(q_stored[s], 16)
                for n in (10, 11):
                    load_w(n % 2, n + 1, P * n)
                for j in range(2):
                    sp.wait_ge(proj_out, 2 + CHUNKS * (KT + j + 1))
                    for h in range(2):
                        sp.dma_start(g.k_scr[2 * j + h, :, :],
                                     kv_ch[HD * h:HD * (h + 1), j, FIRST:LAST]).then_inc(k_stored, 16)
                for t in range(TILES):
                    sp.wait_ge(kv_out, t + 1)
                    done = kv_stored[t % 2]
                    for kv, seq, dec in ((0, g.prompt_k, g.sample_k), (1, g.prompt_v, g.sample_v)):
                        src = kv_tok[:, t % 2, 256 * kv:256 * kv + 256]
                        to = seq[0, 0].rearrange("t h d -> t (h d)")
                        if t == 0:
                            sp.dma_start(to[0:META, :], src[DEC:HEAD_ROWS, :]).then_inc(done, 16)
                            sp.dma_start(dec[0, :, 0].rearrange("s h d -> s (h d)"), src[0:DEC, :]).then_inc(done, 16)
                        else:
                            r = META + P * (t - 1)
                            sp.dma_start(to[r:r + P, :], src).then_inc(done, 16)
                    if t == 0:
                        sp.dma_start(g.v_scr[0:META, :], kv_tok[DEC:HEAD_ROWS, 0, 256:512]).then_inc(done, 16)
                    else:
                        sp.dma_start(g.v_scr[r:r + P, :], kv_tok[:, t % 2, 256:512]).then_inc(done, 16)
                sp.wait_ge(kv_stored[0], 16 * (5 + 3 * 4))
                sp.wait_ge(kv_stored[1], 16 * (3 * 4))
                sp.wait_ge(k_stored, 16 * 5)
                sp.wait_ge(q_stored[0], 32 * 5)
                sp.wait_ge(q_stored[1], 32 * 5)
                sp.wait_ge(old_rows, 32)
                sp.wait_ge(bias_in, 48)

            @block.gpsimd
            def _(pool):
                pool.sem_inc(w_lo_ready, 2)
                pool.memset(g.ident[:, :], 0.0).then_inc(consts, 1)
                pool.memset(g.tri[:, :], 1.0).then_inc(consts, 1)
                pool.wait_ge(consts, 2)
                pool.affine_select(out=g.ident[:, :], in_=g.ident[:, :], compare_op=ALU.not_equal, fill=1.0,
                                   base=0, pattern=[[-1, P]], channel_multiplier=1).then_inc(consts, 1)
                pool.affine_select(out=g.tri[:, :], in_=g.tri[:, :], compare_op=ALU.is_ge, fill=0.0,
                                   base=0, pattern=[[-1, P]], channel_multiplier=1).then_inc(consts, 1)
                pool.memset(g.ones[:, :], 1.0).then_inc(consts, 1)
                pool.memset(g.q_block[:, :, :, :], 0.0).then_inc(q_block0, 1)
                pool.memset(g.page_mask[:, :, :], 1.0).then_inc(consts, 1)
                pool.wait_ge(consts, 6)
                pool.memset(g.page_mask[:, :, PAGES - 1:PAGES + 1], 0.0).then_inc(consts, 1)
                pool.memset(g.n_hi[:, :, LAST:COLS].bitcast(F32), 0.0).then_inc(consts, 1)
                pool.memset(g.n_lo[:, :, LAST:COLS].bitcast(F32), 0.0).then_inc(consts, 1)

                def low_part(slot, index):
                    pool.wait_ge(w_hi_ready, index)
                    pool.tensor_tensor(w_lo[:, slot, :, :], w_raw[:, slot, :, :],
                                       w_hi[:, slot, :, :].bitcast(F32), ALU.subtract).then_inc(w_lo_ready, 1)

                with pool.Fori(0, 6, 1) as i:
                    for s in range(2):
                        low_part(s, nth(i, 2, s))

            @block.scalar
            def _(act):
                own = Chain(act, act_step)
                act.sem_inc(proj_out, 2)

                def square(t):
                    _, nr = token_tile(t)
                    act.wait_ge(x_in[t], 32 if t == 0 else 16)
                    if t >= 2:
                        act.wait_ge(squared, t - 1)
                    act.activation(junk[0:nr, t % 2, :], x_tok[0:nr, t, :], ACT.Square,
                                   accum_out=stat[0:nr, 0, t:t + 1]).then_inc(squared, 1)

                def high_part(slot, chunks, turn):
                    act.wait_ge(w_in[slot], turn)
                    act.wait_ge(proj_done, chunks)
                    act.activation(w_hi[:, slot, :, :], w_raw[:, slot, :, :], ACT.Copy).then_inc(w_hi_ready, 1)

                square(0)
                square(1)
                for t in range(TILES):
                    c0, nr = token_tile(t)
                    act.wait_ge(meaned, t + 1)
                    act.activation(stat[0:nr, 2, t:t + 1], stat[0:nr, 1, t:t + 1], ACT.Sqrt).then_inc(rooted, 1)
                    if t + 2 < TILES:
                        square(t + 2)
                    act.wait_ge(scaled, t + 1)
                    act.activation(g.n_hi[:, :, c0:c0 + nr], tmp[:, t % 2, :, 0:nr], ACT.Copy).then_inc(hi_ready, 1)
                    if t in (4, 6):
                        high_part((t - 4) // 2, 3 * (t - 2) // 2, 16)
                act.activation(lam[:, 0, :], g.par[:, :, R_LAM], ACT.Abs).then_inc(act_step, 1)
                act.wait_ge(act_step, 1)
                act.activation(lam[:, 1, :], lam[:, 0, :], ACT.Exp, scale=-1.0).then_inc(lam_exp, 1)

                def evacuate(bank, index, out, scale):
                    act.wait_ge(proj_done, index + 6)
                    act.activation(out, proj[:, bank, 0:CW], ACT.Copy, scale=scale).then_inc(proj_out, 1)

                with act.Fori(0, KT // 2, 1) as i:
                    for s in range(2):
                        act.wait_ge(q_stored[s], nth(i, 32, 31))
                        for c in range(CHUNKS):
                            n = CHUNKS * s + c
                            evacuate(n % 2, nth(i, 6, n), q_stage[:, s, CW * c:CW * (c + 1)], HD ** -0.5)
                            if c == 1 and s == 1:
                                high_part(0, nth(i, 6, 8), nth(i, 16, 31))
                    high_part(1, nth(i, 6, 11), nth(i, 16, 31))
                for j in range(4):
                    for c in range(CHUNKS):
                        n = 24 + CHUNKS * j + c
                        evacuate(n % 2, n + 1, kv_ch[:, j, CW * c:CW * (c + 1)], 1.0)
                    if j < 2:
                        high_part(j, 3 * (11 + j), 16 * 6)

            @block.vector
            def _(dve):
                own = Chain(dve, dve_step)
                dve.wait_ge(rows_t, 1)
                dve.tensor_copy(g.par[:, :, :].rearrange("p k r -> p (k r)"),
                                pt[:, 0:KT * N_ROWS]).then_inc(params, 1)
                dve.wait_ge(params, 1)
                for t in range(TILES):
                    c0, nr = token_tile(t)
                    dve.wait_ge(squared, t + 1)
                    dve.tensor_scalar(stat[0:nr, 1, t:t + 1], stat[0:nr, 0, t:t + 1], 1.0 / D, EPS,
                                      ALU.mult, ALU.add).then_inc(meaned, 1)
                    dve.wait_ge(rooted, t + 1)
                    own.step(dve.reciprocal(stat[0:nr, 2, t:t + 1], stat[0:nr, 2, t:t + 1]))
                    dve.tensor_scalar(x_tok[0:nr, t, :], x_tok[0:nr, t, :], stat[0:nr, 2, t:t + 1], None,
                                      ALU.mult).then_inc(normed, 1)
                    dve.wait_ge(x_turned, t + 1)
                    if t >= 2:
                        dve.wait_ge(hi_ready, t - 1)
                    dve.tensor_tensor(tmp[:, t % 2, :, 0:nr], xt[:, t % 2, :, 0:nr],
                                      g.par[:, :, R_GMIX:R_GMIX + 1].to_broadcast([P, KT, nr]),
                                      ALU.mult).then_inc(scaled, 1)
                    dve.wait_ge(hi_ready, t + 1)
                    dve.tensor_tensor(g.n_lo[:, :, c0:c0 + nr], tmp[:, t % 2, :, 0:nr],
                                      g.n_hi[:, :, c0:c0 + nr].bitcast(F32), ALU.subtract).then_inc(lo_ready, 1)
                own.step(dve.memset(bias_rows[:, :], 1.0))
                dve.wait_ge(bias_in, 48)
                dve.tensor_scalar(bias_rows[:, :], bias_rows[:, :], bias_col[:, 0:1], None,
                                  ALU.mult).then_inc(bias_made, 1)
                dve.wait_ge(lam_exp, 1)
                own.step(dve.tensor_scalar(lam[:, 2, :], lam[:, 1, :], 2.0, None, ALU.add))
                own.step(dve.reciprocal(lam[:, 2, :], lam[:, 2, :]))
                own.step(dve.tensor_tensor(lam[:, 2, :], lam[:, 1, :], lam[:, 2, :], ALU.mult))
                own.step(dve.tensor_tensor(lam[:, 3, :], lam[:, 2, :], lam[:, 2, :], ALU.mult))
                own.step(dve.tensor_scalar(lam[:, 4, :], lam[:, 3, :], 1.0 / 15, None, ALU.mult))
                for odd in (13, 11, 9, 7, 5, 3):
                    own.step(dve.scalar_tensor_tensor(lam[:, 4, :], lam[:, 4, :], 1.0 / odd, lam[:, 3, :],
                                                      ALU.add, ALU.mult))
                own.step(dve.scalar_tensor_tensor(lam[:, 4, :], lam[:, 4, :], 1.0, lam[:, 2, :], ALU.add, ALU.mult))
                own.step(dve.tensor_scalar(lam[:, 5, :], g.par[:, :, R_LAM], -1.0, 0.0, ALU.mult, ALU.max))
                own.step(dve.scalar_tensor_tensor(lam[:, 4, :], lam[:, 4, :], 2.0, lam[:, 5, :], ALU.mult, ALU.add))
                own.step(dve.tensor_scalar(g.rates[:, 0, :], lam[:, 4, :], -4.0, None, ALU.mult))
                own.step(dve.tensor_scalar(g.rates[:, 1, :], lam[:, 4, :], 4.0, None, ALU.mult))
                own.step(dve.tensor_scalar(g.rates[:, 2, :], g.par[:, :, R_BR], 0.5, None, ALU.mult))
                own.step(dve.tensor_scalar(g.rates[:, 3, :], g.par[:, :, R_BI], 0.5, None, ALU.mult))
                with dve.Fori(0, KT // 2, 1) as i:
                    for s in range(2):
                        dve.wait_ge(proj_out, nth(i, 6, 3 * s + 2, 2))
                        dve.tensor_copy(g.q_dec[:, bass.ds(i * 2 + s, 1), :].rearrange("p a c -> p (a c)"),
                                        q_stage[:, s, 0:DEC]).then_inc(q_cols, 1)
                dve.wait_ge(q_cols, KT)
                dve.wait_ge(q_block0, 1)
                for h in range(HEADS):
                    half, src = (h % 8) // 4, HD * (h % 2)
                    dve.tensor_copy(g.q_block[HD * half:HD * (half + 1), h // 8, :, h % 8],
                                    g.q_dec[src:src + HD, h // 2, :])
                for t in range(TILES):
                    _, nr = token_tile(t)
                    dve.wait_ge(kv_turned, t + 1)
                    if t >= 2:
                        dve.wait_ge(kv_stored[t % 2], 16 * (5 * (t % 2 == 0) + 3 * (t // 2 - (t % 2 == 0))))
                    dve.tensor_copy(kv_tok[0:nr, t % 2, :], kvt[0:nr, t % 2, 0:512]).then_inc(kv_out, 1)

            @block.tensor
            def _(pe):
                pe.sem_inc(proj_done, 6)
                pe.wait_ge(consts, 3)
                pe.wait_ge(rows_in, 16 * 9)
                for k in range(KT):
                    last = pe.transpose(pt[:, N_ROWS * k:N_ROWS * (k + 1)], rows[:, P * k:P * (k + 1)],
                                        g.ident[0:N_ROWS, 0:N_ROWS])
                last.then_inc(rows_t, 1)
                for t in range(TILES):
                    _, nr = token_tile(t)
                    pe.wait_ge(normed, t + 1)
                    if t >= 2:
                        pe.wait_ge(scaled, t - 1)
                    for k in range(KT):
                        last = pe.transpose(xt[:, t % 2, k, 0:nr], x_tok[0:nr, t, P * k:P * (k + 1)],
                                            g.ident[0:nr, 0:nr])
                    last.then_inc(x_turned, 1)
                pe.wait_ge(lo_ready, TILES)
                pe.wait_ge(consts, 9)

                def tile(slot, index, first_chunk, base):
                    pe.wait_ge(w_lo_ready, index + 2)
                    for c in range(CHUNKS):
                        n = first_chunk + c
                        pe.wait_ge(proj_out, base + n + 1)
                        last = project(pe, proj[:, n % 2, 0:CW], w_hi[:, slot], w_lo[:, slot],
                                       g.n_hi, g.n_lo, CW * c)
                        last.then_inc(proj_done, 1)

                with pe.Fori(0, 6, 1) as i:
                    for s in range(2):
                        tile(s, nth(i, 2, s), CHUNKS * s, i * 6)
                pe.wait_ge(proj_out, 2 + 36)
                for t in range(TILES):
                    c0, nr = token_tile(t)
                    if t >= 2:
                        pe.wait_ge(kv_out, t - 1)
                    for j in range(4):
                        last = pe.transpose(kvt[0:nr, t % 2, P * j:P * (j + 1)], kv_ch[:, j, c0:c0 + nr],
                                            g.ident[:, :])
                    last.then_inc(kv_turned, 1)


BLOCK_ORDER = (8, 0, 7, 1, 6, 2, 5, 3, 4)
UNITS = tuple((a, b) for a in range(2) for b in BLOCK_ORDER)
SLOTS = len(UNITS)
Z_AT = (0, 1040, 1056, 0, 144, 928, 1200, 0, 400, 928, 0, 16, 928, 1072, 0, 272, 1040, 1440)
Z_RING = 1968
Z_BANK_AT = {0: 1040, 1: 1024, 2: 1024, 3: 1024}
LAG = 2
SUMS_RING = 2096


def unit(s):
    a, b = UNITS[s]
    return (a, b, 0, META, META) if b == 0 else (a, b, META + P * (b - 1), P, META + P * b)


def key_groups(b):
    blocks = [(m, META + P * (m - 1), P) for m in range(1, b + 1)] + [(0, 0, META)]
    return [blocks[n:n + 4] for n in range(0, len(blocks), 4)]


GROUPS_TO = [0]
for _, _b in UNITS:
    GROUPS_TO.append(GROUPS_TO[-1] + len(key_groups(_b)))
GROUPS = GROUPS_TO[-1]


CHUNK_ORDER = [(w, c) for w in ("xr", "ga", "gr") for c in range(CHUNKS)] + \
    [("rg", 0), ("gb", 0), ("ig", 0), ("rg", 1), ("gb", 1), ("ig", 1), ("rg", 2), ("gb", 2), ("ig", 2)]
STEPS_EARLY = (8, 8, 6, 6, 6, 6, 6, 6, 6, 6, 4, 4)
PLACES = []
_steps = [(n, k) for n in range(9) for k in range(KT)]
for _count in STEPS_EARLY:
    _slot, _steps = _steps[:_count], _steps[_count:]
    _cut = [(_count + 2) // 3, (_count + 2) // 3 + (_count + 1) // 3]
    PLACES.append([[(n, k, k + 1) for n, k in _slot[a:b]] for a, b in ((0, _cut[0]), (_cut[0], _cut[1]), (_cut[1], _count))])
assert not _steps
PLACES += [[[(9, 0, KT)], [(10, 0, 2)], [(10, 2, 3)]], [[(10, 3, 5)], [(10, 5, 7)], [(10, 7, 8)]],
           [[(11, 0, KT)], [], [(12, 0, KT)]], [[(13, 0, 2)], [(13, 2, 4)], [(13, 4, 5)]],
           [[(13, 5, 7)], [(13, 7, 8)], [(14, 0, KT)]], [[(15, 0, KT)], [(16, 0, 2)], [(16, 2, 3)]],
           [[(16, 3, 5)], [(16, 5, 7)], [(16, 7, 8)]], [[(17, 0, KT)], [], []]]


def chunks_of(s):
    return [n for place in PLACES[s] for n, _, k1 in place if k1 == KT]


def keys_of(s):
    return unit(s)[4] if 0 <= s < SLOTS else 0


def soft_at(s):
    return 0 if s % 2 == 0 else SUMS_RING - keys_of(s)


def pos_at(s):
    at = keys_of(s) if s % 2 == 0 else keys_of(s + 1)
    assert at + keys_of(s) <= (SUMS_RING - keys_of(s + 1) if s % 2 == 0 else soft_at(s))
    return at


def score_banks(s):
    at = Z_BANK_AT.get(unit(s)[1], 0)
    return set(range(at // 512, (at + keys_of(s) - 1) // 512 + 1))


T_GR, T_GA, T_GB, T_R, T_I, T_Y, T_SQRT, T_LN, T_A, T_RS, TAIL = range(11)
TAIL_STEPS, LATE_STEPS = 1, 10


class Branch:

    def __init__(self, nc, ctx, g, sem):
        sb = lambda name, shape: ctx.enter_context(nc.sbuf_tensor(name, shape, F32))
        self.g = g
        self.xr, self.xc, self.gr, self.gb, self.rg, self.ig = (
            sb(f"r_{name}", [P, COLS]) for name in ("xr", "xc", "gr", "gb", "rg", "ig"))
        self.pc = sb("r_pc", [P, N_ROWS])
        self.rc = sb("r_rc", [P, 4])
        self.gated, self.root_used, self.tail_done = sem("r_gated"), sem("r_root_used"), sem("r_tail_done")
        self.tail_act = sem("r_tail_act")

    def views(self, i):
        return (self.g.mix[:, bass.ds(i, 1), :].rearrange("p a c -> p (a c)"),
                self.g.mix[:, bass.ds(i + 1, 1), :].rearrange("p a c -> p (a c)"))

    def act_step(self, act, i, out, in_, func, after=None, **kw):
        if after is not None:
            act.wait_ge(self.tail_act, nth(i, TAIL, after))
        act.activation(out, in_, func, **kw).then_inc(self.tail_act, 1)

    def act_gates(self, act, i):
        _, ga = self.views(i)
        gr, gb, rg = self.gr, self.gb, self.rg
        self.act_step(act, i, gr[:, :], gr[:, :], ACT.Gelu_apprx_tanh)
        self.act_step(act, i, ga, ga, ACT.Tanh, scale=0.5)
        self.act_step(act, i, gb[:, :], gb[:, :], ACT.Tanh, scale=0.5)
        self.act_step(act, i, rg[:, :], rg[:, :], ACT.Tanh, bias=self.rc[:, 2:3], scale=0.5)

    def act_rate(self, act, i):
        gr, rg, ig, rc = self.gr, self.rg, self.ig, self.rc
        self.act_step(act, i, ig[:, :], ig[:, :], ACT.Tanh, bias=rc[:, 3:4], scale=0.5)
        act.wait_ge(self.gated, nth(i, 1, 0))
        self.act_step(act, i, gr[:, :], rg[:, :], ACT.Tanh, T_R, bias=rc[:, 1:2], scale=rc[:, 1:2])

    def act_roots(self, act, i):
        gr = self.gr
        self.act_step(act, i, self.xr[:, :], gr[:, :], ACT.Sqrt, T_Y, scale=2.0)
        act.preload_act_table_set("natural_log_exp_and_others")
        self.act_step(act, i, gr[:, :], gr[:, :], ACT.Ln, T_SQRT, bias=1.0)

    def act_late(self, act, i, s):
        if s == 0:
            self.act_step(act, i, self.rg[:, :], self.rg[:, :], ACT.Exp, bias=self.rc[:, 0:1], scale=self.rc[:, 0:1])
        if s == 1:
            self.act_step(act, i, self.gr[:, :], self.gr[:, :], ACT.Exp, T_LN, scale=-0.5)

    def gate(self, dve, own, i):
        _, ga = self.views(i)
        dve.wait_ge(self.tail_act, nth(i, TAIL, T_GB))
        dve.scalar_tensor_tensor(self.gb[:, :], self.gb[:, :], 1.0, self.gr[:, :], ALU.add,
                                 ALU.mult).then_inc(self.gated, 1)
        own.step(dve.tensor_scalar(self.g.gate_dec[:, bass.ds(i, 1), :].rearrange("p a c -> p (a c)"),
                                   ga[:, 0:DEC], 1.0, None, ALU.add))

    def late(self, dve, own, i, s):
        here, ga = self.views(i)
        g, xr, xc, gr, gb, rg, ig = self.g, self.xr, self.xc, self.gr, self.gb, self.rg, self.ig
        if s == 0:
            dve.wait_ge(self.tail_act, nth(i, TAIL, T_I))
            own.step(dve.scalar_tensor_tensor(ig[:, :], ig[:, :], 1.0, xc[:, :], ALU.add, ALU.mult))
            dve.wait_ge(self.tail_act, nth(i, TAIL, T_SQRT))
            dve.scalar_tensor_tensor(ig[:, :], ig[:, :], 0.5, xr[:, :], ALU.mult, ALU.mult)\
               .then_inc(self.root_used, 1)
        if s == 1:
            own.mark(dve.scalar_tensor_tensor(here[:, FIRST:LAST], ga[:, FIRST:LAST], 1.0,
                                              here[:, FIRST:LAST], ALU.add, ALU.mult))
            dve.wait_ge(self.root_used, nth(i, 1, 0))
            dve.wait_ge(self.tail_act, nth(i, TAIL, T_RS))
            own.step(dve.tensor_tensor(ig[:, :], ig[:, :], gr[:, :], ALU.mult))
        if s == 3:
            own.mark(dve.tensor_tensor_scan(ig[:, FIRST:LAST], rg[:, FIRST:LAST], ig[:, FIRST:LAST], 0.0,
                                            ALU.mult, ALU.add))
            own.step(dve.tensor_tensor(rg[:, 0:DEC], rg[:, 0:DEC], self.pc[:, R_H0:R_H0 + DEC], ALU.mult))
            own.step(dve.tensor_tensor(ig[:, 0:DEC], ig[:, 0:DEC], rg[:, 0:DEC], ALU.add))
            own.mark(dve.tensor_copy(g.h_out[:, bass.ds(i, 1), 0:DEC].rearrange("p a c -> p (a c)"),
                                     ig[:, 0:DEC]))
            own.step(dve.tensor_copy(g.h_out[:, bass.ds(i, 1), DEC:DEC + 1].rearrange("p a c -> p (a c)"),
                                     ig[:, LAST - 1:LAST]))
        if s == 4:
            own.step(dve.tensor_tensor(gb[:, 0:LAST], gb[:, 0:LAST], ig[:, 0:LAST], ALU.mult))
            own.step(dve.tensor_copy(here[:, 0:DEC], gb[:, 0:DEC]))
        if s == 5:
            dve.tensor_tensor(here[:, FIRST:LAST], gb[:, FIRST:LAST], here[:, FIRST:LAST],
                              ALU.add).then_inc(self.tail_done, 1)


def phase_mix(nc, g, branch, sem):
    ctx = ExitStack()
    with ctx:
        sb = lambda name, shape, dt=F32: ctx.enter_context(nc.sbuf_tensor(name, shape, dt))
        pb = lambda name, shape: ctx.enter_context(nc.psum_tensor(name, shape, F32))
        w_raw = g.w_raw
        w_hi = sb("b_w_hi", [P, 2, KT, P], F32R)
        w_lo = sb("b_w_lo", [P, 2, KT, P], F32R)
        q_in = sb("b_q_in", [HD + 1, 2, PROMPT])
        k_in = sb("b_k_in", [HD + 1, PROMPT])
        v_in = sb("b_v_in", [P, TILES, HD])
        z = sb("b_z", [P, Z_RING])
        sums = sb("b_sums", [P, SUMS_RING])
        never = sb("b_never", [P, P], BF16)
        ident_b = sb("b_ident_b", [P, P], BF16)
        w_t = sb("b_w_t", [P, 2, 4, P])
        xr, xc, gr, gb, rg, ig, pc, rc = (branch.xr, branch.xc, branch.gr, branch.gb, branch.rg, branch.ig,
                                          branch.pc, branch.rc)
        gate_w = sb("b_gate_w", [P, 2, P])
        page = sb("b_page", [P, 2, 2, KVH * HD])
        k_t = sb("b_k_t", [P, 4, P])
        zd = sb("b_zd", [P, HEADS, PAGES])
        softd = sb("b_softd", [P, HEADS, PAGES])
        posd = sb("b_posd", [P, HEADS, PAGES])
        spd = sb("b_spd", [P, HEADS, PAGES + 1])
        laterd = sb("b_laterd", [P, HEADS, PAGES + 1])
        vacc = sb("b_vacc", [P, 2, 8])
        p_proj = pb("b_p_proj", [P, 2, 512])
        p_z = pb("b_p_z", [P, 3 * 512])
        p_wt = pb("b_p_wt", [P, 4, P])
        p_av = pb("b_p_av", [P, 512])
        p_kt = pb("b_p_kt", [P, 512])
        p_zd = p_av[:, 256:512].rearrange("p (h n) -> p h n", n=PAGES)
        p_td = p_kt[:, 0:256].rearrange("p (h n) -> p h n", n=PAGES)
        p_vd = p_kt[:, 0:16].rearrange("p (a h) -> p a h", a=2)

        w_in = [sem(f"b_w_in{s}") for s in range(2)]
        q_arr = [sem(f"b_q_arr{s}") for s in range(2)]
        k_arr, v_arr, gw_arr = sem("b_k_arr"), sem("b_v_arr"), sem("b_gw_arr")
        page_arr = [sem(f"b_page_arr{s}") for s in range(2)]
        page_used = sem("b_page_used")
        inits = sem("b_inits")
        w_hi_ready = sem("b_w_hi_ready")
        w_lo_ready = sem("b_w_lo_ready")
        proj_done = sem("b_proj_done")
        proj_out = sem("b_proj_out")
        qk_done = sem("b_qk_done")
        z_copied = sem("b_z_copied")
        pos_done = sem("b_pos_done")
        soft_done = sem("b_soft_done")
        summed = sem("b_summed")
        arg_ready = sem("b_arg_ready")
        w_ready = sem("b_w_ready")
        wt_turned = sem("b_wt_turned")
        wt_out = sem("b_wt_out")
        av_group = sem("b_av_group")
        av_out = sem("b_av_out")
        kt_out = sem("b_kt_out")
        zd_done = sem("b_zd_done")
        zd_read = sem("b_zd_read")
        posd_done = sem("b_posd_done")
        softd_done = sem("b_softd_done")
        laterd_done = sem("b_laterd_done")
        td_done = sem("b_td_done")
        argd_ready = sem("b_argd_ready")
        wd_ready = sem("b_wd_ready")
        vd_added = sem("b_vd_added")
        att_out = sem("b_att_out")
        xc_ready = sem("b_xc_ready")
        act_step = sem("b_act_step")
        dve_step = sem("b_dve_step")
        masks = sem("b_masks")
        passed = [sem(f"b_passed{s}") for s in range(2)]

        w_view = g.w_in.rearrange("o (k p) c -> p (o k) c", p=P)

        with nc.Block() as block:

            @block.sync
            def _(sp):
                def load_w(slot, index, col):
                    sp.wait_ge(w_lo_ready, index)
                    sp.dma_start(w_raw[:, slot, :, :], w_view[:, :, bass.ds(col, P)]).then_inc(w_in[slot], 16)

                def load_pages(i, j):
                    cache = g.cache_k if j < 8 else g.cache_v
                    numbers = [sp.value_load(g.table[0:1, bass.ds(i * PAGES + (2 * (j % 8) + n), 1)],
                                             min_val=0, max_val=N_PHYS - 1) for n in range(2)]
                    sp.wait_ge(page_used, nth(i, 16, j))
                    for n in range(2):
                        src = cache[0].rearrange("n t h d -> n t (h d)")[bass.ds(numbers[n], 1), :, :]
                        sp.dma_start(page[:, j % 2, n, :], src.rearrange("a t c -> (a t) c"))\
                          .then_inc(page_arr[j % 2], 16)

                def load_q(i, a):
                    sp.wait_ge(qk_done, nth(i, SLOTS, 9 * a + 8))
                    sp.dma_start(q_in[:, a, :], g.q_scr[bass.ds(i * 2 + a, 1), :, :]
                                 .rearrange("a p c -> p (a c)")).then_inc(q_arr[a], 16)

                load_w(0, 1, XR_COL)
                sp.wait_ge(inits, 7)
                with sp.Fori(0, KT, 1) as i:
                    group = i // 2
                    load_q(i, 0)
                    load_pages(i, 0)
                    load_q(i, 1)
                    sp.dma_start(k_in[0:HD, :], g.k_scr[bass.ds(group, 1), :, :]
                                 .rearrange("a p c -> p (a c)")).then_inc(k_arr, 16)
                    load_w(1, nth(i, 4, 1), i * P + GA_COL)
                    sp.wait_ge(av_group, nth(i, GROUPS, GROUPS - 1))
                    sp.dma_start(v_in[0:META, 0, :], g.v_scr[0:META, bass.ds(group * HD, HD)]).then_inc(v_arr, 16)
                    sp.dma_start(v_in[:, 1:TILES, :], g.v_scr[META:PROMPT, bass.ds(group * HD, HD)]
                                 .rearrange("(t p) d -> p t d", p=P)).then_inc(v_arr, 16)
                    load_pages(i, 1)
                    sp.wait_ge(proj_done, nth(i, SLOTS, SLOTS - 1))
                    for n, w in ((0, g.w_rgate), (1, g.w_igate)):
                        for h in range(2):
                            sp.dma_start(gate_w[HD * h:HD * (h + 1), n, HD * h:HD * (h + 1)],
                                         w[0, bass.ds(i * 2 + h, 1), :, :].rearrange("a p c -> p (a c)"))\
                              .then_inc(gw_arr, 16)
                    load_w(0, nth(i, 4, 2), i * P + GR_COL)
                    for j in range(2, 16):
                        load_pages(i, j)
                        if j == 2:
                            load_w(1, nth(i, 4, 3), i * P + GB_COL)
                        if j == 6:
                            load_w(0, nth(i, 4, 4), i * P + (XR_COL + P))
                for k in (1, 0):
                    sp.wait_ge(w_lo_ready, nth(KT - 1, 4, 6 - k))
                    sp.dma_start(w_raw[:, k, :, :].rearrange("p k c -> p (k c)"),
                                 g.w_out[0, P * k:P * (k + 1), :]).then_inc(g.wo_arr[k], 16)

            @block.gpsimd
            def _(pool):
                pool.sem_inc(w_lo_ready, 2)
                for n, (part, value) in enumerate(((z[:, 0:P], 0.0), (gate_w[:, :, :], 0.0), (k_in[HD:HD + 1, :], 1.0),
                                                   (xc[:, LAST:COLS], 0.0), (zd[:, :, :], 0.0),
                                                   (spd[:, :, PAGES:PAGES + 1], 0.0))):
                    if n:
                        pool.wait_ge(inits, n)
                    pool.memset(part, value).then_inc(inits, 1)
                pool.affine_select(out=z[:, 0:P], in_=z[:, 0:P], compare_op=ALU.is_gt, fill=-1e30, base=0,
                                   pattern=[[-1, P]], channel_multiplier=1).then_inc(inits, 1)

                def low_part(slot, index):
                    pool.wait_ge(w_hi_ready, index)
                    pool.tensor_tensor(w_lo[:, slot, :, :], w_raw[:, slot, :, :],
                                       w_hi[:, slot, :, :].bitcast(F32), ALU.subtract).then_inc(w_lo_ready, 1)

                low_part(0, 1)
                with pool.Fori(0, KT, 1) as i:
                    for t in range(4):
                        low_part((t + 1) % 2, nth(i, 4, t + 1))

            @block.scalar
            def _(act):
                own = Chain(act, act_step)
                act.sem_inc(proj_out, 2)

                def high_part(slot, chunks, turns):
                    act.wait_ge(w_in[slot], turns)
                    act.wait_ge(proj_done, chunks)
                    act.activation(w_hi[:, slot, :, :], w_raw[:, slot, :, :], ACT.Copy).then_inc(w_hi_ready, 1)

                act.wait_ge(inits, 7)
                act.activation(never[:, :], z[:, 0:P], ACT.Copy).then_inc(masks, 1)
                act.activation(ident_b[:, :], g.ident[:, :], ACT.Copy).then_inc(masks, 1)
                high_part(0, SLOTS, 16)
                act.preload_act_table_set("natural_log_exp_and_others")

                def slots(i, first):
                    own.turn(0, i, 2 * SLOTS + 2)
                    if not first:
                        act.wait_ge(proj_out, nth(i, SLOTS, -1, 2))
                        branch.act_rate(act, i - 1)
                        branch.act_roots(act, i - 1)
                    for s in range(SLOTS + LAG):
                        if s in (1, 4, 8, 12):
                            t = s // 4
                            high_part((t + 1) % 2, nth(i, SLOTS, SLOTS - 1) if t == 0
                                      else nth(i, SLOTS, 3 * t - 1, SLOTS), 16 * (nth(i, 2, (0, 1, 1, 2)[t])))
                        if s < SLOTS:
                            a, b, q0, nq, nk = unit(s)
                            zs, so = z[0:nq, Z_AT[s]:Z_AT[s] + nk], sums[0:nq, soft_at(s):soft_at(s) + nk]
                            act.wait_ge(z_copied, nth(i, SLOTS, s, 2))
                            act.wait_ge(summed, nth(i, SLOTS, s))
                            own.step(act.activation(so, zs, ACT.Abs))
                            own.step(act.activation(so, so, ACT.Exp, scale=-1.0))
                            act.activation(so, so, ACT.Ln, bias=1.0).then_inc(soft_done, 1)
                        if 1 <= s <= SLOTS:
                            a, b, q0, nq, nk = unit(s - 1)
                            zs = z[0:nq, Z_AT[s - 1]:Z_AT[s - 1] + nk]
                            act.wait_ge(arg_ready, nth(i, SLOTS, s - 1, 1))
                            act.activation(zs, zs, ACT.Exp).then_inc(w_ready, 1)
                        if s == SLOTS + 1:
                            act.wait_ge(proj_out, nth(i, SLOTS, SLOTS - 2, 2))
                            branch.act_gates(act, i)
                        for n in chunks_of(s):
                            what, c = CHUNK_ORDER[n]
                            cols = slice(CW * c, CW * (c + 1))
                            if what == "ga":
                                out = g.mix[:, bass.ds(i + 1, 1), cols].rearrange("p a c -> p (a c)")
                            else:
                                out = {"xr": xr, "gr": gr, "gb": gb, "rg": rg, "ig": ig}[what][:, cols]
                            if n == 0 and not first:
                                act.wait_ge(branch.root_used, nth(i, 1, 0) - 1)
                            if n == 6 and not first:
                                act.wait_ge(branch.tail_done, nth(i, 1, 0) - 1)
                            act.wait_ge(proj_done, nth(i, SLOTS, n, SLOTS))
                            act.activation(out, p_proj[:, n % 2, 0:CW], ACT.Copy).then_inc(proj_out, 1)
                        if not first:
                            branch.act_late(act, i - 1, s)
                        if s == 8:
                            act.wait_ge(zd_read, nth(i, 1, 0))
                            own.step(act.activation(softd[:, :, :], zd[:, :, :], ACT.Abs))
                            own.step(act.activation(softd[:, :, :], softd[:, :, :], ACT.Exp, scale=-1.0))
                            act.activation(softd[:, :, :], softd[:, :, :], ACT.Ln, bias=1.0).then_inc(softd_done, 1)
                        if s == 11:
                            act.wait_ge(argd_ready, nth(i, 1, 0))
                            act.activation(zd[:, :, :], zd[:, :, :], ACT.Exp).then_inc(wd_ready, 1)
                    assert own.n == 2 * SLOTS + 2

                slots(0, True)
                with act.Fori(1, KT, 1) as i:
                    slots(i, False)

            @block.vector
            def _(dve):
                own = Chain(dve, dve_step)
                for s, n in ((z_copied, 2), (summed, 2), (arg_ready, 1), (wt_out, 1), (av_out, 1),
                             (vd_added, 1)):
                    dve.sem_inc(s, n)
                dve.wait_ge(inits, 7)
                dve.wait_ge(masks, 2)

                def turn_out(i, s, n):
                    a, b, q0, nq, nk = unit(s)
                    q = GROUPS_TO[s] + n
                    blocks = key_groups(b)[n]
                    full = [m for m, _, size in blocks if size == P]
                    dve.wait_ge(wt_turned, nth(i, GROUPS, q, GROUPS))
                    dve.wait_ge(av_group, nth(i, GROUPS, q - 2, GROUPS))
                    if full and len(blocks) > len(full):
                        dve.tensor_copy(w_t[:, q % 2, 0:len(full), 0:nq], p_wt[:, 0:len(full), 0:nq])
                    if len(blocks) > len(full):
                        r = len(full)
                        dve.tensor_copy(w_t[0:META, q % 2, r, 0:nq], p_wt[0:META, r, 0:nq]).then_inc(wt_out, 1)
                    else:
                        dve.tensor_copy(w_t[:, q % 2, 0:len(full), 0:nq], p_wt[:, 0:len(full), 0:nq])\
                           .then_inc(wt_out, 1)

                def values_out(i, s):
                    a, b, q0, nq, nk = unit(s)
                    dve.wait_ge(av_group, nth(i, GROUPS, GROUPS_TO[s + 1] - 1, GROUPS))
                    if b == 0:
                        dve.sem_inc(passed[1], 1)
                    rows = slice(HD * a, HD * (a + 1))
                    dve.tensor_copy(g.mix[rows, bass.ds(i, 1), FIRST + q0:FIRST + q0 + nq]
                                    .rearrange("p a c -> p (a c)"),
                                    p_av[rows, P * (s % 2):P * (s % 2) + nq]).then_inc(av_out, 1)

                def conv(i, s):
                    cw = lambda j: pc[:, R_CONVW + j:R_CONVW + j + 1]
                    cb = pc[:, R_CONVB:R_CONVB + 1]
                    if s == 4:
                        own.mark(dve.tensor_copy(pc[:, :], g.par[:, bass.ds(i, 1), :].rearrange("p a r -> p (a r)")))
                        own.mark(dve.tensor_copy(rc[:, :], g.rates[:, :, bass.ds(i, 1)].rearrange("p r a -> p (r a)")))
                        dve.wait_ge(proj_out, nth(i, SLOTS, 2, 2))
                        own.mark(dve.tensor_copy(g.x_out[:, bass.ds(i, 1), 0:DEC].rearrange("p a c -> p (a c)"),
                                                 xr[:, 0:DEC]))
                        own.step(dve.tensor_copy(g.x_out[:, bass.ds(i, 1), DEC:DEC + 3].rearrange("p a c -> p (a c)"),
                                                 xr[:, LAST - 3:LAST]))
                        own.step(dve.tensor_scalar(xc[:, 0:DEC], xr[:, 0:DEC], cw(3), cb, ALU.mult, ALU.add))
                        for j in range(3):
                            own.step(dve.scalar_tensor_tensor(xc[:, 0:DEC], pc[:, R_CONVSTATE + j:R_CONVSTATE + 24:3],
                                                              cw(j), xc[:, 0:DEC], ALU.mult, ALU.add))
                    if s == 5:
                        own.step(dve.memset(xr[:, FIRST - 3:FIRST], 0.0))
                        own.step(dve.tensor_scalar(xc[:, FIRST:LAST], xr[:, FIRST:LAST], cw(3), cb,
                                                   ALU.mult, ALU.add))
                    if s in (7, 8, 10):
                        j = {7: 2, 8: 1, 10: 0}[s]
                        ins = dve.scalar_tensor_tensor(xc[:, FIRST:LAST], xr[:, FIRST - 3 + j:LAST - 3 + j], cw(j),
                                                       xc[:, FIRST:LAST], ALU.mult, ALU.add)
                        if j:
                            own.step(ins)
                        else:
                            ins.then_inc(xc_ready, 1)

                CONV_STEPS = 8 + 2 + 2

                def decode(i, s):
                    if s < 8:
                        dve.wait_ge(page_used, nth(i, 16, s, 2))
                        if s:
                            dve.wait_ge(zd_done, nth(i, 8, s - 1))
                        dve.tensor_copy(k_t[:, :, :].rearrange("p a c -> p (a c)"), p_kt[:, :]).then_inc(kt_out, 1)
                    if s == 8:
                        dve.wait_ge(zd_done, nth(i, 8, 7))
                        dve.tensor_tensor(zd[:, :, :], p_zd,
                                          g.bias_all[:, :].unsqueeze(2).to_broadcast([P, HEADS, PAGES]),
                                          ALU.add).then_inc(zd_read, 1)
                        dve.wait_ge(zd_read, nth(i, 1, 0))
                        dve.tensor_scalar(posd[:, :, :], zd[:, :, :], 0.0, None, ALU.max).then_inc(posd_done, 1)
                        dve.wait_ge(posd_done, nth(i, 2, 0))
                    if s == 9:
                        dve.wait_ge(softd_done, nth(i, 1, 0))
                        dve.tensor_tensor(spd[:, :, 0:PAGES], softd[:, :, :], posd[:, :, :],
                                          ALU.add).then_inc(posd_done, 1)
                        dve.wait_ge(posd_done, nth(i, 2, 1))
                        flat = lambda x: x[:, :, :].rearrange("p h n -> p (h n)")
                        n = HEADS * (PAGES + 1)
                        dve.tensor_tensor_scan(flat(laterd)[:, 0:n - 1][:, ::-1],
                                               flat(g.page_mask)[:, 0:n - 1][:, ::-1],
                                               flat(spd)[:, 1:n][:, ::-1], 0.0,
                                               ALU.mult, ALU.add).then_inc(laterd_done, 1)
                    if s == 10:
                        dve.wait_ge(td_done, nth(i, 1, 0))
                        dve.tensor_tensor(zd[:, :, :], zd[:, :, :], p_td, ALU.subtract).then_inc(argd_ready, 1)
                    if s >= 12:
                        dve.wait_ge(page_used, nth(i, 16, s - 4, 2))
                        if s == 12:
                            dve.tensor_copy(vacc[:, :, :], p_vd).then_inc(vd_added, 1)
                        else:
                            dve.tensor_tensor(vacc[:, :, :], vacc[:, :, :], p_vd, ALU.add).then_inc(vd_added, 1)
                        dve.wait_ge(vd_added, nth(i, 8, s - 12, 1))

                def decode_values_out(i):
                    for pair in range(2):
                        for half in range(2):
                            for odd in range(2):
                                t0 = 4 * pair + 2 * half
                                last = dve.tensor_copy(g.att_dec[HD * odd:HD * (odd + 1), t0:t0 + 2, bass.ds(i, 1)],
                                                vacc[HD * half:HD * (half + 1), pair,
                                                     4 * half + odd:4 * half + odd + 3:2].unsqueeze(2))
                    last.then_inc(att_out, 1)
                    dve.wait_ge(att_out, nth(i, 1, 0))

                def slots(i, first):
                    if first:
                        own.turn(0, 0, 0)
                    else:
                        own.turn(-LATE_STEPS, i, CONV_STEPS + TAIL_STEPS + LATE_STEPS)
                    for s in range(SLOTS + LAG):
                        v = s - LAG
                        groups = len(key_groups(UNITS[v][1])) if v >= 0 else 0
                        if groups:
                            turn_out(i, v, 0)
                        if s < SLOTS:
                            a, b, q0, nq, nk = unit(s)
                            zs = z[0:nq, Z_AT[s]:Z_AT[s] + nk]
                            zp = Z_BANK_AT.get(b, 0)
                            dve.wait_ge(qk_done, nth(i, SLOTS, s, SLOTS))
                            before = GROUPS_TO[s - 2] + GROUPS if s >= 3 else GROUPS_TO[s + 16]
                            dve.wait_ge(wt_turned, nth(i, GROUPS, before - 1))
                            dve.tensor_copy(zs, p_z[0:nq, zp:zp + nk]).then_inc(z_copied, 1)
                        if 1 <= s <= SLOTS:
                            u = s - 1
                            a, b, q0, nq, nk = unit(u)
                            zs = z[0:nq, Z_AT[u]:Z_AT[u] + nk]
                            so = sums[0:nq, soft_at(u):soft_at(u) + nk]
                            pos = sums[0:nq, pos_at(u):pos_at(u) + nk]
                            dve.wait_ge(z_copied, nth(i, SLOTS, u, 2))
                            dve.wait_ge(arg_ready, nth(i, SLOTS, u))
                            dve.tensor_scalar(pos, zs, 0.0, None, ALU.max).then_inc(pos_done, 1)
                            dve.wait_ge(pos_done, nth(i, SLOTS, u))
                            dve.wait_ge(soft_done, nth(i, SLOTS, u))
                            dve.tensor_tensor_scan(pos[:, ::-1], so[:, ::-1], pos[:, ::-1], 0.0, ALU.add, ALU.add)\
                               .then_inc(summed, 1)
                        if groups > 1:
                            turn_out(i, v, 1)
                        if 1 <= s <= SLOTS:
                            dve.wait_ge(summed, nth(i, SLOTS, u, 2))
                            dve.tensor_tensor(zs, zs, pos, ALU.subtract).then_inc(arg_ready, 1)
                        if groups > 2:
                            turn_out(i, v, 2)
                        if groups:
                            values_out(i, v)
                        decode(i, s)
                        if not first:
                            if s == 1:
                                dve.wait_ge(av_out, nth(i, SLOTS, -1, 1))
                            branch.late(dve, own, i - 1, s)
                        conv(i, s)
                    branch.gate(dve, own, i)
                    assert own.n == CONV_STEPS + TAIL_STEPS + (0 if first else LATE_STEPS), own.n
                    decode_values_out(i)

                slots(0, True)
                with dve.Fori(1, KT, 1) as i:
                    slots(i, False)
                own.turn(KT * (CONV_STEPS + TAIL_STEPS + LATE_STEPS) - LATE_STEPS, 0, 0)
                own.step(dve.tensor_tensor(g.gate_dec[:, :, :], g.gate_dec[:, :, :], g.att_dec[:, :, :], ALU.mult))
                dve.wait_ge(branch.tail_done, KT - 1)
                own.step(dve.tensor_tensor(g.mix[:, 0:KT - 1, 0:DEC], g.mix[:, 0:KT - 1, 0:DEC],
                                           g.gate_dec[:, 0:KT - 1, :], ALU.add))

            @block.tensor
            def _(pe):
                for s, n in ((proj_done, SLOTS), (qk_done, SLOTS), (wt_turned, GROUPS), (av_group, GROUPS),
                             (page_used, 2)):
                    pe.sem_inc(s, n)
                pe.wait_ge(masks, 2)

                def scores(i, s):
                    a, b, q0, nq, nk = unit(s)
                    zp = Z_BANK_AT.get(b, 0)
                    if s == 0:
                        pe.wait_ge(k_arr, 16 * nth(i, 1, 0))
                    if s % 9 == 0:
                        pe.wait_ge(q_arr[a], 16 * nth(i, 1, 0))
                    alone = s == 0 or score_banks(s) & score_banks(s - 1)
                    pe.wait_ge(z_copied, nth(i, SLOTS, s + 1 if alone else s))
                    diagonal = zp + nk - nq
                    c = zp
                    while c < zp + nk:
                        e = min(zp + nk, (c // 512 + 1) * 512)
                        m = max(c, diagonal)
                        last = pe.matmul(p_z[0:nq, c:e], q_in[:, a, q0:q0 + nq], k_in[:, c - zp:e - zp],
                                         start=True, stop=m >= e)
                        if m < e:
                            last = pe.matmul(p_z[0:nq, m:e], ident_b[0:nq, 0:nq],
                                             never[0:nq, m - diagonal:e - diagonal], start=False, stop=True)
                        c = e
                    last.then_inc(qk_done, 1)

                def turn(i, s, n):
                    a, b, q0, nq, nk = unit(s)
                    q = GROUPS_TO[s] + n
                    if n == 0:
                        pe.wait_ge(w_ready, nth(i, SLOTS, s))
                    pe.wait_ge(wt_out, nth(i, GROUPS, q))
                    if b == 0:
                        pe.sem_inc(passed[0], 1)
                    for r, (m, k0, size) in enumerate(key_groups(b)[n]):
                        last = pe.transpose(p_wt[0:size, r, 0:nq], z[0:nq, Z_AT[s] + k0:Z_AT[s] + k0 + size],
                                            g.ident[0:nq, 0:nq])
                    last.then_inc(wt_turned, 1)

                def values(i, s, n):
                    a, b, q0, nq, nk = unit(s)
                    q = GROUPS_TO[s] + n
                    groups = key_groups(b)
                    if s == 0 and n == 0:
                        pe.wait_ge(v_arr, 32 * nth(i, 1, 0))
                    if n == 0:
                        pe.wait_ge(av_out, nth(i, SLOTS, s))
                    if n == 0 and s == 9 - LAG:
                        pe.wait_ge(zd_read, nth(i, 1, 0))
                    pe.wait_ge(wt_out, nth(i, GROUPS, q, 1))
                    for r, (m, k0, size) in enumerate(groups[n]):
                        last = pe.matmul(p_av[HD * a:HD * (a + 1), P * (s % 2):P * (s % 2) + nq],
                                         v_in[0:size, m, :], w_t[0:size, q % 2, r, 0:nq],
                                         start=(n == 0 and r == 0), stop=(m == 0))
                    last.then_inc(av_group, 1)

                def decode(i, s):
                    if 1 <= s <= 8:
                        j = s - 1
                        pe.wait_ge(kt_out, nth(i, 8, j))
                        if s > LAG:
                            pe.wait_ge(av_out, nth(i, SLOTS, s - LAG))
                        for n in range(2):
                            for pair in range(2):
                                last = pe.matmul(p_zd[:, 8 * pair:8 * (pair + 1), 2 * j + n], k_t[:, 2 * n + pair, :],
                                                 g.q_block[:, pair, bass.ds(i, 1), :].rearrange("p a h -> p (a h)"),
                                                 start=True, stop=True)
                        last.then_inc(zd_done, 1)
                    if s < 8:
                        pe.wait_ge(page_arr[s % 2], 32 * nth(i, 8, s // 2))
                        if s == 0:
                            pe.wait_ge(vd_added, nth(i, 8, -1, 1))
                        for n in range(2):
                            for pair in range(2):
                                r = 2 * n + pair
                                last = pe.transpose(p_kt[:, P * r:P * (r + 1)],
                                                    page[:, s % 2, n, P * pair:P * (pair + 1)], g.ident[:, :])
                        last.then_inc(page_used, 1)
                    if s == 10:
                        pe.wait_ge(laterd_done, nth(i, 1, 0))
                        pe.matmul(p_td, g.tri[:, :], spd[:, :, 0:PAGES], start=True, stop=False)
                        pe.matmul(p_td, g.ones[:, :], laterd[:, :, 0:PAGES], start=False, stop=True)\
                          .then_inc(td_done, 1)
                    if s >= 12:
                        j = s - 12
                        if j == 0:
                            pe.wait_ge(wd_ready, nth(i, 1, 0))
                        else:
                            pe.wait_ge(vd_added, nth(i, 8, j - 1, 1))
                        pe.wait_ge(page_arr[j % 2], 32 * nth(i, 8, 4 + j // 2))
                        for pair in range(2):
                            for n in range(2):
                                last = pe.matmul(p_vd[:, pair, :], page[:, j % 2, n, P * pair:P * (pair + 1)],
                                                 zd[:, 8 * pair:8 * (pair + 1), 2 * j + n], start=(n == 0),
                                                 stop=(n == 1))
                        last.then_inc(page_used, 1)

                def project_piece(i, n, k0, k1):
                    what, c = CHUNK_ORDER[n]
                    if k0 == 0:
                        pe.wait_ge(proj_out, nth(i, SLOTS, n))
                    if what in ("rg", "ig"):
                        if n == 9:
                            pe.wait_ge(xc_ready, nth(i, 1, 0))
                            pe.wait_ge(gw_arr, 64 * nth(i, 1, 0))
                        last = pe.matmul(p_proj[:, n % 2, 0:CW], gate_w[:, 0 if what == "rg" else 1, :],
                                         xc[:, CW * c:CW * (c + 1)], start=True, stop=True)
                    else:
                        tile = ("xr", "ga", "gr", "gb").index(what)
                        if k0 == 0 and c == 0:
                            pe.wait_ge(w_lo_ready, nth(i, 4, tile, 2))
                        last = project_part(pe, p_proj[:, n % 2, 0:CW], w_hi[:, tile % 2], w_lo[:, tile % 2],
                                            g.n_hi, g.n_lo, CW * c, k0, k1)
                    if k1 == KT:
                        last.then_inc(proj_done, 1)

                with pe.Fori(0, KT, 1) as i:
                    for s in range(SLOTS + LAG):
                        v = s - LAG
                        if s == 0:
                            scores(i, 0)
                        groups = len(key_groups(UNITS[v][1])) if v >= 0 else 0
                        if groups:
                            turn(i, v, 0)
                        for n in range(3):
                            for piece in PLACES[s][n]:
                                project_piece(i, *piece)
                            if n == 0:
                                decode(i, s)
                            if n < groups:
                                values(i, v, n)
                            if n + 1 < groups:
                                turn(i, v, n + 1)
                        if s + 1 < SLOTS:
                            scores(i, s + 1)


def phase_out(nc, g, branch, sem):
    ctx = ExitStack()
    with ctx:
        sb = lambda name, shape, dt=F32: ctx.enter_context(nc.sbuf_tensor(name, shape, dt))
        pb = lambda name, shape: ctx.enter_context(nc.psum_tensor(name, shape, F32))
        wo_raw = g.w_raw[:, :, :, :].rearrange("p s k c -> p s (k c)")
        wo_hi = sb("c_wo_hi", [P, KT, D], F32R)
        wo_lo = sb("c_wo_lo", [P, KT, D], F32R)
        x1 = (branch.xr[:, 0:D], branch.xc[:, 0:D])
        xn = branch.gr[:, 0:D]
        tmp = branch.rg[:, 0:D].rearrange("p (k c) -> p k c", c=P)
        stat = sb("c_stat", [P, 3, TILES])
        p_x1 = pb("c_p_x1", [P, 2, D])
        p_xt = pb("c_p_xt", [P, KT, P])
        p_junk = pb("c_p_junk", [P, D])

        w_arr = g.wo_arr
        x_arr = [sem(f"c_x_arr{s}") for s in range(2)]
        wo_hi_ready, wo_lo_ready = sem("c_wo_hi_ready"), sem("c_wo_lo_ready")
        mix_hi, mix_lo = sem("c_mix_hi"), sem("c_mix_lo")
        multiplied = sem("c_multiplied")
        added = sem("c_added")
        stored = [sem(f"c_stored{s}") for s in range(2)]
        squared, meaned, rooted, inverted = sem("c_squared"), sem("c_meaned"), sem("c_rooted"), sem("c_inverted")
        normed, turned, scaled = sem("c_normed"), sem("c_turned"), sem("c_scaled")
        hi_ready, lo_ready = sem("c_hi_ready"), sem("c_lo_ready")
        dve_step, dec_added = sem("c_dve_step"), sem("c_dec_added")

        def rows_of(t):
            return g.x1_scr[0:HEAD_ROWS, :] if t == 0 else g.x1_scr[HEAD_ROWS + P * (t - 1):HEAD_ROWS + P * t, :]

        with nc.Block() as block:

            @block.sync
            def _(sp):
                def load_x(t):
                    if t >= 2:
                        sp.wait_ge(stored[t % 2], 16 * (t // 2))
                        sp.wait_ge(normed, t - 1)
                    if t < 2:
                        sp.wait_ge(branch.tail_done, KT)
                    if t == 0:
                        sp.dma_start(x1[0][0:DEC, :], g.x_sample.rearrange("s o d -> (s o) d")).then_inc(x_arr[0], 16)
                        sp.dma_start(x1[0][DEC:HEAD_ROWS, :], g.meta_tokens).then_inc(x_arr[0], 16)
                    else:
                        sp.dma_start(x1[t % 2], g.x_prompt[0, P * (t - 1):P * t, :]).then_inc(x_arr[t % 2], 16)

                for k in range(2, KT):
                    sp.wait_ge(wo_lo_ready, k - 1)
                    sp.dma_start(wo_raw[:, k % 2, :], g.w_out[0, P * k:P * (k + 1), :]).then_inc(w_arr[k % 2], 16)
                load_x(0)
                load_x(1)
                for n in range(2):
                    sp.wait_ge(wo_lo_ready, KT - 1 + n)
                    sp.dma_start(g.w_raw[:, n, :, :], g.w_up.rearrange("o (k p) c -> p (o k) c", p=P)
                                 [:, :, DFF * n:DFF * n + P]).then_inc(g.up_arr[n], 16)
                for t in range(TILES):
                    _, nr = token_tile(t)
                    sp.wait_ge(added, t + 1)
                    sp.dma_start(rows_of(t), x1[t % 2][0:nr, :]).then_inc(stored[t % 2], 16)
                    if t + 2 < TILES:
                        load_x(t + 2)
                for n in range(2):
                    sp.wait_ge(stored[n], 16 * (5 - n))

            @block.gpsimd
            def _(pool):
                for k in range(KT):
                    pool.wait_ge(wo_hi_ready, k + 1)
                    pool.tensor_tensor(wo_lo[:, k, :], wo_raw[:, k % 2, :], wo_hi[:, k, :].bitcast(F32),
                                       ALU.subtract).then_inc(wo_lo_ready, 1)

            @block.scalar
            def _(act):
                def mix_high(k):
                    if k == KT - 1:
                        act.wait_ge(branch.tail_done, KT)
                        act.wait_ge(dec_added, 1)
                    act.activation(g.n_hi[:, k, 0:LAST], g.mix[:, k, 0:LAST], ACT.Copy, scale=0.5).then_inc(mix_hi, 1)

                for k in range(KT):
                    if k == 1:
                        mix_high(0)
                        mix_high(1)
                    act.wait_ge(w_arr[k % 2], 16 * (k // 2 + 1))
                    act.activation(wo_hi[:, k, :], wo_raw[:, k % 2, :], ACT.Copy).then_inc(wo_hi_ready, 1)
                    if k == 1:
                        branch.act_rate(act, KT - 1)
                    if k == 2:
                        branch.act_roots(act, KT - 1)
                    if k == 3:
                        for s in range(2):
                            branch.act_late(act, KT - 1, s)
                    if 1 <= k < KT - 1:
                        mix_high(k + 1)
                for t in range(TILES):
                    c0, nr = token_tile(t)
                    act.wait_ge(added, t + 1)
                    if t:
                        act.wait_ge(squared, t)
                    act.activation(p_junk[0:nr, :], x1[t % 2][0:nr, :], ACT.Square,
                                   accum_out=stat[0:nr, 0, t:t + 1]).then_inc(squared, 1)
                    act.wait_ge(meaned, t + 1)
                    act.activation(stat[0:nr, 2, t:t + 1], stat[0:nr, 1, t:t + 1], ACT.Sqrt).then_inc(rooted, 1)
                    act.wait_ge(scaled, t + 1)
                    act.activation(g.n_hi[:, :, c0:c0 + nr], tmp[:, :, 0:nr], ACT.Copy).then_inc(hi_ready, 1)

            @block.vector
            def _(dve):
                own = Chain(dve, dve_step)
                for k in range(KT):
                    if k in (1, 2, 3, 4, 5):
                        branch.late(dve, own, KT - 1, (0, 1, 3, 4, 5)[k - 1])
                    if k == 5:
                        dve.tensor_tensor(g.mix[:, KT - 1, 0:DEC], g.mix[:, KT - 1, 0:DEC],
                                          g.gate_dec[:, KT - 1, :], ALU.add).then_inc(dec_added, 1)
                    dve.wait_ge(mix_hi, k + 1)
                    dve.scalar_tensor_tensor(g.n_lo[:, k, 0:LAST], g.mix[:, k, 0:LAST], 0.5,
                                             g.n_hi[:, k, 0:LAST].bitcast(F32), ALU.mult,
                                             ALU.subtract).then_inc(mix_lo, 1)
                dve.wait_ge(branch.tail_done, KT)
                for t in range(TILES):
                    c0, nr = token_tile(t)
                    dve.wait_ge(multiplied, 2 * t + 2)
                    dve.wait_ge(x_arr[t % 2], 16 * (t // 2 + 1 + (t % 2 == 0)))
                    dve.tensor_tensor(x1[t % 2][0:nr, :], p_x1[0:nr, t % 2, :], x1[t % 2][0:nr, :],
                                      ALU.add).then_inc(added, 1)
                    dve.wait_ge(squared, t + 1)
                    dve.tensor_scalar(stat[0:nr, 1, t:t + 1], stat[0:nr, 0, t:t + 1], 1.0 / D, EPS,
                                      ALU.mult, ALU.add).then_inc(meaned, 1)
                    dve.wait_ge(rooted, t + 1)
                    dve.reciprocal(stat[0:nr, 2, t:t + 1], stat[0:nr, 2, t:t + 1]).then_inc(inverted, 1)
                    dve.wait_ge(inverted, t + 1)
                    if t:
                        dve.wait_ge(turned, t)
                    dve.tensor_scalar(xn[0:nr, :], x1[t % 2][0:nr, :], stat[0:nr, 2, t:t + 1], None,
                                      ALU.mult).then_inc(normed, 1)
                    dve.wait_ge(turned, t + 1)
                    if t:
                        dve.wait_ge(lo_ready, t)
                    dve.tensor_tensor(tmp[:, :, 0:nr], p_xt[:, :, 0:nr],
                                      g.par[:, :, R_GFFN:R_GFFN + 1].to_broadcast([P, KT, nr]),
                                      ALU.mult).then_inc(scaled, 1)
                    dve.wait_ge(hi_ready, t + 1)
                    dve.tensor_tensor(g.n_lo[:, :, c0:c0 + nr], tmp[:, :, 0:nr],
                                      g.n_hi[:, :, c0:c0 + nr].bitcast(F32), ALU.subtract).then_inc(lo_ready, 1)

            @block.tensor
            def _(pe):
                def product(t, half, k):
                    c0, nr = token_tile(t)
                    cols = slice(512 * half, 512 * (half + 1))
                    for x, w in ((g.n_hi, wo_hi), (g.n_hi, wo_lo), (g.n_lo, wo_hi)):
                        last = pe.matmul(p_x1[0:nr, t % 2, cols], x[:, k, c0:c0 + nr], w[:, k, cols],
                                         start=(k == 0 and x is g.n_hi and w is wo_hi),
                                         stop=(k == KT - 1 and x is g.n_lo))
                    if k == KT - 1:
                        last.then_inc(multiplied, 1)

                for k in range(KT):
                    pe.wait_ge(mix_lo, k + 1)
                    pe.wait_ge(wo_lo_ready, k + 1)
                    for t in range(2):
                        for half in range(2):
                            product(t, half, k)
                for t in range(1, TILES + 1):
                    if 2 <= t < TILES:
                        pe.wait_ge(added, t - 1)
                        for half in range(2):
                            for k in range(KT):
                                product(t, half, k)
                    if t:
                        _, nr = token_tile(t - 1)
                        pe.wait_ge(normed, t)
                        if t >= 2:
                            pe.wait_ge(scaled, t - 1)
                        for k in range(KT):
                            last = pe.transpose(p_xt[:, k, 0:nr], xn[0:nr, P * k:P * (k + 1)], g.ident[0:nr, 0:nr])
                        last.then_inc(turned, 1)


FPAIR = 2
TURNS = FT // FPAIR
UPC = 2 * FPAIR * CHUNKS
DOWNC = KT * CHUNKS


def phase_ffn(nc, g, sem):
    ctx = ExitStack()
    with ctx:
        sb = lambda name, shape, dt=F32: ctx.enter_context(nc.sbuf_tensor(name, shape, dt))
        pb = lambda name, shape: ctx.enter_context(nc.psum_tensor(name, shape, F32))
        y = g.mix
        w_raw = g.w_raw
        w_hi = sb("d_w_hi", [P, 2, KT, P], F32R)
        w_lo = sb("d_w_lo", [P, 2, KT, P], F32R)
        wd_hi = sb("d_wd_hi", [P, FPAIR, D], F32R)
        wd_lo = sb("d_wd_lo", [P, FPAIR, D], F32R)
        up = sb("d_up", [P, 2, COLS])
        cv = sb("d_cv", [P, 2, COLS])
        a_par = sb("d_a_par", [F_ROWS, 2, COLS])
        prod = sb("d_prod", [P, FPAIR, COLS])
        a_hi = sb("d_a_hi", [P, FPAIR, COLS], F32R)
        a_lo = sb("d_a_lo", [P, FPAIR, COLS], F32R)
        fp = sb("d_fp", [P, F_ROWS])
        fpar = sb("d_fpar", [P, 2 * FT, F_ROWS])
        p_up = pb("d_p_up", [P, 2, 512])
        p_down = pb("d_p_down", [P, 4, 512])
        p_par = pb("d_p_par", [P, 2, 512])

        w_arr = g.up_arr
        par_arr = sem("d_par_arr")
        par_turned, par_out = sem("d_par_turned"), sem("d_par_out")
        inits = sem("d_inits")
        hi_up, hi_down = sem("d_hi_up"), sem("d_hi_down")
        lo_ready = sem("d_lo_ready")
        up_done = sem("d_up_done")
        up_out = sem("d_up_out")
        conv_done = sem("d_conv_done")
        gelu_done = sem("d_gelu_done")
        prod_done = sem("d_prod_done")
        a_hi_ready, a_lo_ready = sem("d_a_hi_ready"), sem("d_a_lo_ready")
        down_done = sem("d_down_done")
        down_out = sem("d_down_out")
        dve_step = sem("d_dve_step")

        up_view = g.w_up.rearrange("o (k p) c -> p (o k) c", p=P)
        pieces = [buf[0:F_ROWS, n, :] for buf in (a_par, cv, prod) for n in range(2)]

        def down_part(u):
            return range(DOWNC // 4 * u, DOWNC // 4 * (u + 1))

        def up_col(i, u):
            return i * (FPAIR * P) + (P * (u // 2) + (DFF if u % 2 else 0))

        with nc.Block() as block:

            @block.sync
            def _(sp):
                def load_up(slot, index, i, u):
                    sp.wait_ge(lo_ready, index)
                    sp.dma_start(w_raw[:, slot, :, :], up_view[:, :, bass.ds(up_col(i, u), P)]).then_inc(w_arr[slot], 16)

                def load_down(slot, index, i, n):
                    sp.wait_ge(lo_ready, index)
                    sp.dma_start(w_raw[:, slot, :, :].rearrange("p k c -> p (k c)"),
                                 g.w_down[0, bass.ds(i * (FPAIR * P) + P * n, P), :]).then_inc(w_arr[slot], 16)

                for n, piece in enumerate(pieces):
                    c0, c1 = D * n, min(D * (n + 1), 2 * DFF)
                    for r, rows in ((F_STATE, g.state_ffn_conv.rearrange("o s j c -> (o s j) c")),
                                    (F_W, g.w_ffn_conv[0]), (F_B, g.b_ffn_conv)):
                        nrow = rows.shape[0]
                        sp.dma_start(piece[r:r + nrow, 0:c1 - c0], rows[:, c0:c1]).then_inc(par_arr, 16)
                for n in (2, 3):
                    load_up(n % 2, n + 1, 0, n)
                load_up(0, 5, 1, 0)
                with sp.Fori(0, TURNS - 1, 1) as m:
                    load_down(1, nth(m, 6, 5), m, 0)
                    load_down(0, nth(m, 6, 6), m, 1)
                    for n in (1, 2, 3):
                        load_up(n % 2, nth(m, 6, n + 6), m + 1, n)
                    load_up(0, nth(m, 6, 10), m + 2, 0)
                load_down(1, 6 * (TURNS - 1) + 6, TURNS - 1, 0)
                load_down(0, 6 * (TURNS - 1) + 7, TURNS - 1, 1)

            @block.gpsimd
            def _(pool):
                pool.sem_inc(lo_ready, 2)

                def low_up(slot, index, raw):
                    pool.wait_ge(hi_up, index)
                    pool.tensor_tensor(w_lo[:, slot, :, :], w_raw[:, raw, :, :],
                                       w_hi[:, slot, :, :].bitcast(F32), ALU.subtract).then_inc(lo_ready, 1)

                def low_down(n, index, raw):
                    pool.wait_ge(hi_down, index)
                    pool.tensor_tensor(wd_lo[:, n, :], w_raw[:, raw, :, :].rearrange("p k c -> p (k c)"),
                                       wd_hi[:, n, :].bitcast(F32), ALU.subtract).then_inc(lo_ready, 1)

                for n in range(5):
                    low_up(n % 2, n + 1, n % 2)
                    if n == 2:
                        pool.memset(y[:, 0:KT, :], 0.0).then_inc(inits, 1)
                with pool.Fori(0, TURNS - 1, 1) as m:
                    low_down(0, nth(m, 2, 0), 1)
                    low_down(1, nth(m, 2, 1), 0)
                    for n in (1, 2, 3):
                        low_up(n % 2, nth(m, 4, n + 4), n % 2)
                    low_up(0, nth(m, 4, 8), 0)
                for n in range(2):
                    pool.wait_ge(hi_down, 2 * TURNS - 1 + n)
                    pool.tensor_tensor(w_lo[:, n, :, :], w_raw[:, 1 - n, :, :], w_hi[:, n, :, :].bitcast(F32),
                                       ALU.subtract).then_inc(lo_ready, 1)

            @block.scalar
            def _(act):
                act.sem_inc(up_out, 2)

                def high_up(slot, chunks, raw, turns):
                    act.wait_ge(w_arr[raw], turns)
                    act.wait_ge(up_done, chunks)
                    act.activation(w_hi[:, slot, :, :], w_raw[:, raw, :, :], ACT.Copy).then_inc(hi_up, 1)

                def high_down(n, chunks, raw, turns):
                    act.wait_ge(w_arr[raw], turns)
                    act.wait_ge(down_done, chunks)
                    act.activation(wd_hi[:, n, :], w_raw[:, raw, :, :].rearrange("p k c -> p (k c)"),
                                   ACT.Copy).then_inc(hi_down, 1)

                def up_tile(i, u, chunks=range(CHUNKS)):
                    if 0 in chunks:
                        act.wait_ge(conv_done, nth(i, 4, u))
                    for c in chunks:
                        n = CHUNKS * u + c
                        act.wait_ge(up_done, nth(i, UPC, n, 6))
                        act.activation(up[:, u % 2, CW * c:CW * (c + 1)], p_up[:, n % 2, 0:CW],
                                       ACT.Copy).then_inc(up_out, 1)

                def gelu(i, n):
                    act.wait_ge(conv_done, nth(i, 4, 2 * n, 2))
                    act.activation(cv[:, 0, 0:LAST], cv[:, 0, 0:LAST], ACT.Gelu_apprx_tanh).then_inc(gelu_done, 1)

                def high_a(m, n):
                    act.wait_ge(prod_done, nth(m, FPAIR, n, 2))
                    act.activation(a_hi[:, n, 0:LAST], prod[:, n, 0:LAST], ACT.Copy).then_inc(a_hi_ready, 1)

                high_up(0, 3, 0, 16)
                high_up(1, 6, 1, 16)
                for u in range(4):
                    up_tile(0, u)
                    slot = u % 2
                    high_up(slot, 3 * (u + 1) + 6, slot, 16 * (u // 2 + 2)) if u < 3 else None
                    if u % 2 == 0:
                        gelu(0, u // 2)
                with act.Fori(0, TURNS - 1, 1) as m:
                    i = m + 1
                    high_down(0, nth(m, DOWNC, DOWNC - 1), 1, 16 * nth(m, 3, 2))
                    high_down(1, nth(m, DOWNC, DOWNC - 1), 0, 16 * nth(m, 3, 3))
                    high_a(m, 0)
                    up_tile(i, 0, (0, 1))
                    high_a(m, 1)
                    high_up(1, nth(i, UPC, -1, 6), 1, 16 * nth(m, 3, 3))
                    up_tile(i, 0, (2,))
                    high_up(0, nth(i, UPC, 2, 6), 0, 16 * nth(m, 3, 4))
                    up_tile(i, 1, (0,))
                    gelu(i, 0)
                    up_tile(i, 1, (1, 2))
                    high_up(1, nth(i, UPC, 5, 6), 1, 16 * nth(m, 3, 4))
                    up_tile(i, 2)
                    high_up(0, nth(i, UPC, 8, 6), 0, 16 * nth(m, 3, 5))
                    up_tile(i, 3, (0,))
                    gelu(i, 1)
                    up_tile(i, 3, (1, 2))
                act.wait_ge(up_done, UPC * TURNS + 6 - CHUNKS)
                act.wait_ge(lo_ready, 2 + 6 * TURNS + 5 - 6)
                for n in range(2):
                    act.wait_ge(w_arr[1 - n], 16 * (3 * TURNS + n))
                    if n:
                        act.wait_ge(up_done, UPC * TURNS + 6)
                    act.activation(w_hi[:, n, :, :], w_raw[:, 1 - n, :, :], ACT.Copy).then_inc(hi_down, 1)
                for n in range(FPAIR):
                    if n == 0:
                        act.wait_ge(down_done, DOWNC * TURNS)
                    high_a(TURNS - 1, n)

            @block.vector
            def _(dve):
                own = Chain(dve, dve_step)
                for s, n in ((conv_done, 2), (down_out, 4), (prod_done, 2)):
                    dve.sem_inc(s, n)
                CONV = 7

                def conv(i, u):
                    x, c = up[:, u % 2, :], cv[:, u % 2, :]
                    tile = i * FPAIR + (u // 2 + (FT if u % 2 else 0))
                    dve.wait_ge(up_out, nth(i, UPC, CHUNKS * u + 2, 2))
                    par = fpar[:, bass.ds(tile, 1), :].rearrange("p a r -> p (a r)")
                    own.step(dve.tensor_copy(fp[:, :], par))
                    cw = lambda j: fp[:, F_W + j:F_W + j + 1]
                    cb = fp[:, F_B:F_B + 1]
                    here = g.u_out[:, bass.ds(tile, 1), :].rearrange("p a r -> p (a r)")
                    dve.tensor_copy(here[:, 0:DEC], x[:, 0:DEC])
                    dve.tensor_copy(here[:, DEC:DEC + 2], x[:, LAST - 2:LAST])
                    own.step(dve.tensor_scalar(c[:, 0:DEC], x[:, 0:DEC], cw(2), cb, ALU.mult, ALU.add))
                    for j in range(2):
                        own.step(dve.scalar_tensor_tensor(c[:, 0:DEC], fp[:, F_STATE + j:F_STATE + 16:2], cw(j),
                                                          c[:, 0:DEC], ALU.mult, ALU.add))
                    own.step(dve.memset(x[:, FIRST - 2:FIRST], 0.0))
                    own.step(dve.tensor_scalar(c[:, FIRST:LAST], x[:, FIRST:LAST], cw(2), cb, ALU.mult, ALU.add))
                    own.step(dve.scalar_tensor_tensor(c[:, FIRST:LAST], x[:, FIRST - 1:LAST - 1], cw(1),
                                                      c[:, FIRST:LAST], ALU.mult, ALU.add))
                    dve.scalar_tensor_tensor(c[:, FIRST:LAST], x[:, FIRST - 2:LAST - 2], cw(0),
                                             c[:, FIRST:LAST], ALU.mult, ALU.add).then_inc(conv_done, 1)

                def gated(i, n):
                    dve.wait_ge(gelu_done, nth(i, FPAIR, n))
                    dve.wait_ge(conv_done, nth(i, 4, 2 * n + 1, 2))
                    dve.tensor_tensor(prod[:, n, 0:LAST], cv[:, 0, 0:LAST], cv[:, 1, 0:LAST],
                                      ALU.mult).then_inc(prod_done, 1)
                    dve.wait_ge(prod_done, nth(i, FPAIR, n, 2))

                def low_a(m):
                    for n in range(FPAIR):
                        dve.wait_ge(a_hi_ready, nth(m, FPAIR, n))
                        dve.tensor_tensor(a_lo[:, n, 0:LAST], prod[:, n, 0:LAST], a_hi[:, n, 0:LAST].bitcast(F32),
                                          ALU.subtract).then_inc(a_lo_ready, 1)
                    dve.wait_ge(a_lo_ready, nth(m, FPAIR, 1, 1))

                def add_down(m, chunks):
                    for n in chunks:
                        tile, c = n // CHUNKS, n % CHUNKS
                        to = y[:, tile, CW * c:CW * (c + 1)]
                        dve.wait_ge(down_done, nth(m, DOWNC, n, DOWNC))
                        dve.tensor_tensor(to, to, p_down[:, n % 4, 0:CW], ALU.add).then_inc(down_out, 1)

                for half in range(2):
                    dve.wait_ge(par_turned, half + 1)
                    dve.tensor_copy(fpar[:, FT * half:FT * (half + 1), :].rearrange("p t r -> p (t r)"),
                                    p_par[:, half, 0:FT * F_ROWS]).then_inc(par_out, 1)
                dve.wait_ge(par_out, 2)
                dve.memset(a_hi[:, :, LAST:COLS].bitcast(F32), 0.0).then_inc(a_lo_ready, 1)
                dve.memset(a_lo[:, :, LAST:COLS].bitcast(F32), 0.0)
                for u in range(4):
                    conv(0, u)
                    if u % 2:
                        gated(0, u // 2)
                dve.wait_ge(inits, 1)
                with dve.Fori(0, TURNS - 1, 1) as m:
                    own.turn(4 * CONV, m, 4 * CONV)
                    low_a(m)
                    for u in range(4):
                        add_down(m, down_part(u))
                        conv(m + 1, u)
                        if u % 2:
                            gated(m + 1, u // 2)
                    assert own.n == 4 * CONV, own.n
                low_a(TURNS - 1)
                add_down(TURNS - 1, range(DOWNC))

            @block.tensor
            def _(pe):
                for s, n in ((up_done, 6), (down_done, DOWNC)):
                    pe.sem_inc(s, n)
                def up_tile(i, u, split):
                    pe.wait_ge(lo_ready, split)
                    for c in range(CHUNKS):
                        n = CHUNKS * u + c
                        pe.wait_ge(up_out, nth(i, UPC, n))
                        project(pe, p_up[:, n % 2, 0:CW], w_hi[:, u % 2], w_lo[:, u % 2],
                                g.n_hi, g.n_lo, CW * c).then_inc(up_done, 1)

                def down(m, split, chunks, wd_hi=wd_hi, wd_lo=wd_lo):
                    if 0 in chunks:
                        pe.wait_ge(lo_ready, split)
                        pe.wait_ge(a_lo_ready, nth(m, FPAIR, 1, 1))
                    for n in chunks:
                        tile, c = n // CHUNKS, n % CHUNKS
                        pe.wait_ge(down_out, nth(m, DOWNC, n))
                        for k in range(FPAIR):
                            for w, a in ((wd_hi, a_hi), (wd_hi, a_lo), (wd_lo, a_hi)):
                                last = pe.matmul(p_down[:, n % 4, 0:CW], w[:, k, P * tile:P * (tile + 1)],
                                                 a[:, k, CW * c:CW * (c + 1)],
                                                 start=(k == 0 and w is wd_hi and a is a_hi),
                                                 stop=(k == FPAIR - 1 and w is wd_lo))
                        last.then_inc(down_done, 1)

                def params():
                    pe.wait_ge(par_arr, 16 * 18)
                    for half in range(2):
                        for n in range(FT):
                            t = FT * half + n
                            last = pe.transpose(p_par[:, half, F_ROWS * n:F_ROWS * (n + 1)],
                                                pieces[t // KT][:, P * (t % KT):P * (t % KT + 1)],
                                                g.ident[0:F_ROWS, 0:F_ROWS])
                        last.then_inc(par_turned, 1)

                for u in range(4):
                    up_tile(0, u, 2 + u + 1)
                    if u == 0:
                        params()
                with pe.Fori(0, TURNS - 1, 1) as m:
                    for u in range(4):
                        up_tile(m + 1, u, nth(m, 6, 6 + u if u else 4, 2))
                        down(m, nth(m, 6, 6, 2), down_part(u))
                down(TURNS - 1, 2 + 5 + 6 * (TURNS - 1) + 2, range(DOWNC),
                     w_hi[:, :, :, :].rearrange("p s k c -> p s (k c)"), w_lo[:, :, :, :].rearrange("p s k c -> p s (k c)"))


def phase_last(nc, g, sem):
    ctx = ExitStack()
    with ctx:
        sb = lambda name, shape, dt=F32: ctx.enter_context(nc.sbuf_tensor(name, shape, dt))
        pb = lambda name, shape: ctx.enter_context(nc.psum_tensor(name, shape, F32))
        x1 = sb("e_x1", [P, TILES, D])
        g_last = sb("e_g_last", [P, D])
        out = sb("e_out", [P, 2, D])
        stat = sb("e_stat", [P, 3, TILES])
        junk = sb("e_junk", [P, 2, D])
        u_rows = sb("e_u_rows", [DEC + 2, 2 * DFF])
        x_rows = sb("e_x_rows", [DEC + 3, D])
        h_rows = sb("e_h_rows", [DEC + 1, D])
        p_y = pb("e_p_y", [P, 2, D])
        p_rows = pb("e_p_rows", [P, 4, 512])

        x_arr = [sem(f"e_x_arr{t}") for t in range(TILES)]
        g_arr = sem("e_g_arr")
        turned, added, squared, meaned = sem("e_turned"), sem("e_added"), sem("e_squared"), sem("e_meaned")
        rooted, inverted, made = sem("e_rooted"), sem("e_inverted"), sem("e_made")
        stored = [sem(f"e_stored{s}") for s in range(2)]
        rows_turned, rows_out, rows_stored = sem("e_rows_turned"), sem("e_rows_out"), sem("e_rows_stored")

        kept = [(g.u_out, t, u_rows) for t in range(0, 2 * FT, 4)] + \
               [(g.x_out, t, x_rows) for t in (0, 4)] + [(g.h_out, t, h_rows) for t in (0, 4)]

        def kept_after(t):
            return range(2 * t, min(2 * t + 2, len(kept)))

        with nc.Block() as block:

            @block.sync
            def _(sp):
                for t in range(TILES):
                    c0, nr = token_tile(t)
                    sp.dma_start(x1[0:nr, t, :], g.x1_scr[c0:c0 + nr, :]).then_inc(x_arr[t], 16)
                    if t == 0:
                        sp.dma_start(g_last[:, :], g.g_final.partition_broadcast(P)).then_inc(g_arr, 16)
                for t in range(TILES):
                    sp.wait_ge(made, t + 1)
                    if t == 0:
                        sp.dma_start(g.y_sample.rearrange("s o d -> (s o) d"), out[0:DEC, 0, :]).then_inc(stored[0], 16)
                    else:
                        sp.dma_start(g.y_prompt[0, P * (t - 1):P * t, :], out[:, t % 2, :]).then_inc(stored[t % 2], 16)
                sp.wait_ge(rows_out, len(kept))
                for to, rows in ((g.prompt_ffn_conv[0, 0], u_rows[DEC:DEC + 2, :]),
                                 (g.sample_ffn_conv[0, :, 1, :], u_rows[0:DEC, :]),
                                 (g.prompt_rnn_conv[0, 0], x_rows[DEC:DEC + 3, :]),
                                 (g.sample_rnn_conv[0, :, 2, :], x_rows[0:DEC, :]),
                                 (g.prompt_rnn_h[0], h_rows[DEC:DEC + 1, :]),
                                 (g.sample_rnn_h[0], h_rows[0:DEC, :])):
                    sp.dma_start(to, rows).then_inc(rows_stored, 16)
                sp.wait_ge(rows_stored, 16 * 6)
                for n in range(2):
                    sp.wait_ge(stored[n], 16 * (5 - n))

            @block.scalar
            def _(act):
                def rows(n):
                    src, t, to = kept[n]
                    act.wait_ge(rows_turned, n + 1)
                    act.activation(to[:, P * t:P * (t + 4)], p_rows[0:to.shape[0], n % 4, :],
                                   ACT.Copy).then_inc(rows_out, 1)

                for t in range(TILES):
                    _, nr = token_tile(t)
                    act.wait_ge(added, t + 1)
                    if t >= 2:
                        act.wait_ge(squared, t - 1)
                    act.activation(junk[0:nr, t % 2, :], x1[0:nr, t, :], ACT.Square,
                                   accum_out=stat[0:nr, 0, t:t + 1]).then_inc(squared, 1)
                    act.wait_ge(meaned, t + 1)
                    act.activation(stat[0:nr, 2, t:t + 1], stat[0:nr, 1, t:t + 1], ACT.Sqrt).then_inc(rooted, 1)
                    for n in kept_after(t):
                        rows(n)

            @block.vector
            def _(dve):
                for t in range(TILES + 2):
                    if t < TILES:
                        _, nr = token_tile(t)
                        dve.wait_ge(turned, t + 1)
                        dve.wait_ge(x_arr[t], 16)
                        dve.tensor_tensor(x1[0:nr, t, :], p_y[0:nr, t % 2, :], x1[0:nr, t, :],
                                          ALU.add).then_inc(added, 1)
                    if t >= 2:
                        u = t - 2
                        _, nr = token_tile(u)
                        dve.wait_ge(rooted, u + 1)
                        dve.reciprocal(stat[0:nr, 2, u:u + 1], stat[0:nr, 2, u:u + 1]).then_inc(inverted, 1)
                    if 1 <= t <= TILES:
                        u = t - 1
                        _, nr = token_tile(u)
                        dve.wait_ge(squared, u + 1)
                        dve.tensor_scalar(stat[0:nr, 1, u:u + 1], stat[0:nr, 0, u:u + 1], 1.0 / D, EPS,
                                          ALU.mult, ALU.add).then_inc(meaned, 1)
                    if t >= 2:
                        u = t - 2
                        _, nr = token_tile(u)
                        dve.wait_ge(inverted, u + 1)
                        if u == 0:
                            dve.wait_ge(g_arr, 16)
                        if u >= 2:
                            dve.wait_ge(stored[u % 2], 16 * (u // 2))
                        dve.scalar_tensor_tensor(out[0:nr, u % 2, :], x1[0:nr, u, :], stat[0:nr, 2, u:u + 1],
                                                 g_last[0:nr, :], ALU.mult, ALU.mult).then_inc(made, 1)

            @block.tensor
            def _(pe):
                for t in range(TILES):
                    c0, nr = token_tile(t)
                    if t >= 2:
                        pe.wait_ge(added, t - 1)
                    for k in range(KT):
                        last = pe.transpose(p_y[0:nr, t % 2, P * k:P * (k + 1)], g.mix[:, k, c0:c0 + nr],
                                            g.ident[:, :])
                    last.then_inc(turned, 1)
                    for n in kept_after(t):
                        src, first, to = kept[n]
                        if n >= 4:
                            pe.wait_ge(rows_out, n - 3)
                        for r in range(4):
                            last = pe.transpose(p_rows[0:to.shape[0], n % 4, P * r:P * (r + 1)], src[:, first + r, :],
                                                g.ident[:, :])
                        last.then_inc(rows_turned, 1)


class Shared:

    def __init__(self, ins, outs):
        (self.x_prompt, self.x_sample, self.cache_k, self.cache_v, self.page_table, self.state_rnn_h,
         self.state_rnn_conv, self.state_ffn_conv, self.meta_tokens, self.g_mix, self.w_in, self.sb_bias,
         self.w_rnn_conv, self.b_rnn_conv, self.w_rgate, self.b_rgate, self.w_igate, self.b_igate,
         self.rglru_lambda, self.w_out, self.g_ffn, self.w_up, self.w_ffn_conv, self.b_ffn_conv,
         self.w_down, self.g_final) = (ins[name] for name in _INS)
        (self.y_prompt, self.y_sample, self.prompt_k, self.prompt_v, self.prompt_rnn_h, self.prompt_rnn_conv,
         self.prompt_ffn_conv, self.sample_k, self.sample_v, self.sample_rnn_h, self.sample_rnn_conv,
         self.sample_ffn_conv) = (outs[name] for name, _ in _OUTS)


def hybrid_step(nc, a, o):
    ctx = ExitStack()
    with ctx:
        sb = lambda name, shape, dt=F32: ctx.enter_context(nc.sbuf_tensor(name, shape, dt))
        sem = lambda name: ctx.enter_context(nc.semaphore(name))
        g = Shared(a, o)
        g.n_hi = sb("n_hi", [P, KT, COLS], F32R)
        g.n_lo = sb("n_lo", [P, KT, COLS], F32R)
        g.mix = sb("mix", [P, KT + 1, COLS])
        g.w_raw = sb("w_raw", [P, 2, KT, P])
        g.ident = sb("ident", [P, P])
        g.tri = sb("tri", [P, P])
        g.ones = sb("ones", [P, P])
        g.par = sb("par", [P, KT, N_ROWS])
        g.rates = sb("rates", [P, 4, KT])
        g.bias_all = sb("bias_all", [P, HEADS])
        g.q_dec = sb("q_dec", [P, KT, DEC])
        g.q_block = sb("q_block", [P, 2, DEC, 8])
        g.table = sb("table", [1, DEC * PAGES], I32)
        g.page_mask = sb("page_mask", [P, HEADS, PAGES + 1])
        g.x_out = sb("x_out", [P, KT, DEC + 3])
        g.h_out = sb("h_out", [P, KT, DEC + 1])
        g.att_dec = sb("att_dec", [P, KT, DEC])
        g.gate_dec = sb("gate_dec", [P, KT, DEC])
        g.q_scr = nc.dram_tensor("q_scr", (HEADS, HD + 1, PROMPT), F32).ap()
        g.k_scr = nc.dram_tensor("k_scr", (KVH, HD, PROMPT), F32).ap()
        g.x1_scr = nc.dram_tensor("x1_scr", (HEAD_ROWS + SEQ, D), F32).ap()
        g.v_scr = nc.dram_tensor("v_scr", (PROMPT, KVH * HD), F32).ap()
        phase_qkv(nc, g, sem)
        g.wo_arr = [sem(f"wo_arr{s}") for s in range(2)]
        g.up_arr = [sem(f"up_arr{s}") for s in range(2)]
        with ExitStack() as branch_ctx:
            branch = Branch(nc, branch_ctx, g, sem)
            phase_mix(nc, g, branch, sem)
            phase_out(nc, g, branch, sem)
        g.u_out = sb("u_out", [P, 2 * FT, DEC + 2])
        phase_ffn(nc, g, sem)
        phase_last(nc, g, sem)


_INS = ['x_prompt', 'x_sample', 'cache_k', 'cache_v', 'page_table', 'state_rnn_h', 'state_rnn_conv',
        'state_ffn_conv', 'meta_tokens', 'g_mix', 'w_in', 'sb_bias', 'w_rnn_conv', 'b_rnn_conv', 'w_rgate',
        'b_rgate', 'w_igate', 'b_igate', 'rglru_lambda', 'w_out', 'g_ffn', 'w_up', 'w_ffn_conv', 'b_ffn_conv',
        'w_down', 'g_final']
_OUTS = [('y_prompt', (1, SEQ, D)), ('y_sample', (DEC, 1, D)),
         ('prompt_k', (1, 1, PROMPT, KVH, HD)), ('prompt_v', (1, 1, PROMPT, KVH, HD)),
         ('prompt_rnn_h', (1, 1, D)), ('prompt_rnn_conv', (1, 1, 3, D)), ('prompt_ffn_conv', (1, 1, 2, 2 * DFF)),
         ('sample_k', (1, DEC, 1, KVH, HD)), ('sample_v', (1, DEC, 1, KVH, HD)),
         ('sample_rnn_h', (1, DEC, D)), ('sample_rnn_conv', (1, DEC, 3, D)),
         ('sample_ffn_conv', (1, DEC, 2, 2 * DFF))]


def kernel(**inputs):
    import numpy as np
    import concourse.bacc as bacc
    from concourse.bass_utils import run_bass_kernel_spmd

    nc = bacc.Bacc("TRN2", target_bir_lowering=False, num_devices=1)
    arrays, ins, outs = {}, {}, {}
    for name in _INS:
        x = np.ascontiguousarray(inputs[name])
        arrays[f"in_{name}"] = x
        ins[name] = nc.dram_tensor(f"in_{name}", x.shape, mybir.dt.from_np(x.dtype), kind="ExternalInput").ap()
    for name, shape in _OUTS:
        outs[name] = nc.dram_tensor(f"out_{name}", shape, F32, kind="ExternalOutput").ap()
    hybrid_step(nc, ins, outs)
    r = run_bass_kernel_spmd(nc, [arrays], core_ids=[0])
    return tuple(r.results[0][f"out_{name}"] for name, _ in _OUTS)
```
